# Optimizing a Trainium2 kernel written in Bass

```python
import jax
import jax.numpy as jnp
from jax import lax
import numpy as np

D_MODEL = 1024
BATCH = 1
SEQ = 256
DEPTH = 2

GRID_W = 64
CTX_LEN = 256
EPS = 1e-6
N_MOD = 6

MLA_HEADS = 8
MLA_Q_RANK = 256
MLA_KV_RANK = 128
MLA_NOPE = 64
MLA_ROPE = 32
MLA_V = 64
MLA_WIDTH = MLA_HEADS * MLA_V
MLA_SCALE = (MLA_NOPE + MLA_ROPE) ** -0.5
ROPE_BASE = 10000.0
Q_BLOCK = 128

FOURIER_GROUPS = 4
FOURIER_CH = 64
FOURIER_WIDTH = FOURIER_GROUPS * FOURIER_CH

HGRN_HEADS = 4
HGRN_EXPAND = 128
HGRN_HEAD_V = 64
HGRN_KEY_WIDTH = HGRN_HEADS * HGRN_EXPAND
HGRN_WIDTH = HGRN_HEADS * HGRN_HEAD_V
CHUNK = 64

MIX_WIDTH = MLA_WIDTH + FOURIER_WIDTH + HGRN_WIDTH
IN_SIZES = (MLA_Q_RANK, MLA_KV_RANK, MLA_ROPE, FOURIER_WIDTH, HGRN_KEY_WIDTH, HGRN_KEY_WIDTH, HGRN_KEY_WIDTH, HGRN_WIDTH, HGRN_WIDTH)
IN_WIDTH = sum(IN_SIZES)

D_FF = 2816
N_EXPERTS = 8
TOP_K = 2
N_DENSE = (DEPTH + 1) // 2
N_MOE = DEPTH // 2

kernel_name = 'hybrid_mla_fourier_hgrn2_moe_dit'

F32 = jnp.float32

def normalize_f32(x):
    xf = x.astype(F32)
    return xf * lax.rsqrt(jnp.mean(xf * xf, axis=-1, keepdims=True) + EPS)

def rms_norm(x, gain):
    return (normalize_f32(x) * gain.astype(F32)).astype(x.dtype)

def modulate(x, shift, scale):
    return (normalize_f32(x) * (1.0 + scale.astype(F32)) + shift.astype(F32)).astype(x.dtype)

def split_columns(p):
    out, start = [], 0
    for size in IN_SIZES:
        out.append(p[..., start:start + size])
        start += size
    return out

def axial_rope_tables(n_tokens):
    rows = n_tokens // GRID_W
    row_ids = jnp.repeat(jnp.arange(rows, dtype=F32), GRID_W)
    col_ids = jnp.tile(jnp.arange(GRID_W, dtype=F32), rows)
    per_axis = MLA_ROPE // 2
    inv_freq = ROPE_BASE ** (-jnp.arange(0, per_axis, 2, dtype=F32) / per_axis)
    ang = jnp.concatenate([row_ids[:, None] * inv_freq, col_ids[:, None] * inv_freq], axis=-1)
    return jnp.cos(ang), jnp.sin(ang)

def apply_axial_rope(x, cos, sin):
    quarter = MLA_ROPE // 4
    bshape = (1, x.shape[1]) + (1,) * (x.ndim - 3) + (2, quarter)
    xf = x.astype(F32).reshape(x.shape[:-1] + (2, 2, quarter))
    x1, x2 = xf[..., 0, :], xf[..., 1, :]
    c, s = cos.reshape(bshape), sin.reshape(bshape)
    out = jnp.stack([x1 * c - x2 * s, x1 * s + x2 * c], axis=-2)
    return out.reshape(x.shape).astype(x.dtype)

def mla_queries(dq, q_norm_g, w_uq, rope):
    cq = rms_norm(dq, q_norm_g)
    q = (cq @ w_uq).reshape(dq.shape[:2] + (MLA_HEADS, MLA_NOPE + MLA_ROPE))
    qn, qr = q[..., :MLA_NOPE], q[..., MLA_NOPE:]
    if rope is not None:
        qr = apply_axial_rope(qr, *rope)
    return qn, qr

def mla_keys_values(dkv, kr, kv_norm_g, w_ukv, rope):
    ckv = rms_norm(dkv, kv_norm_g)
    kv = (ckv @ w_ukv).reshape(dkv.shape[:2] + (MLA_HEADS, MLA_NOPE + MLA_V))
    kn, v = kv[..., :MLA_NOPE], kv[..., MLA_NOPE:]
    if rope is not None:
        kr = apply_axial_rope(kr, *rope)
    return kn, kr, v

def block_attention(qn, qr, kn, kr, v):
    B, T = qn.shape[:2]
    nb = T // Q_BLOCK

    def to_blocks(a):
        return a.reshape((B, nb, Q_BLOCK) + a.shape[2:]).swapaxes(0, 1)

    def one_block(blk):
        qn_b, qr_b = blk
        s = jnp.einsum('bqhd,bkhd->bhqk', qn_b, kn) + jnp.einsum('bqhr,bkr->bhqk', qr_b, kr)
        p = jax.nn.softmax(s.astype(F32) * MLA_SCALE, axis=-1)
        return jnp.einsum('bhqk,bkhd->bqhd', p.astype(v.dtype), v)

    o = lax.map(one_block, (to_blocks(qn), to_blocks(qr)))
    return o.swapaxes(0, 1).reshape(B, T, MLA_HEADS * MLA_V)

def fourier_mix(u):
    B, T, _ = u.shape
    uf = u.astype(F32).reshape(B, T, FOURIER_GROUPS, FOURIER_CH)
    y = jnp.fft.fft2(uf, axes=(1, 3), norm='ortho').real
    return y.reshape(B, T, FOURIER_WIDTH).astype(u.dtype)

def hgrn_heads(a, d):
    return a.reshape(a.shape[:2] + (HGRN_HEADS, d))

def hgrn_lower_bounds(lb_logits):
    p = jax.nn.softmax(lb_logits.astype(F32), axis=1)
    return jnp.cumsum(p, axis=1) - p[:, :1]

def hgrn_forget(f_raw, lb):
    f = lb + (1.0 - lb) * jax.nn.sigmoid(f_raw.astype(F32))
    return hgrn_heads(1.0 - f, HGRN_EXPAND), hgrn_heads(jnp.log(f), HGRN_EXPAND)

def chunk_scan(k, log_f, v, s0, q):
    B, T, H, _ = k.shape
    n = T // CHUNK

    def blocks(a):
        return a.reshape(B, n, CHUNK, H, a.shape[-1]).transpose(1, 0, 3, 2, 4)

    def state_update(S, kb, G, vb):
        G_end = G[:, :, -1:, :]
        return jnp.exp(G_end[:, :, 0, :])[..., None] * S + jnp.einsum('bhsd,bhsv->bhdv', kb * jnp.exp(G_end - G), vb)

    if q is None:
        def state_step(S, xs):
            kb, gb, vb = xs
            return state_update(S, kb, jnp.cumsum(gb, axis=2), vb), None
        S_fin, _ = lax.scan(state_step, s0, (blocks(k), blocks(log_f), blocks(v)))
        return None, S_fin

    lower = jnp.tril(jnp.ones((CHUNK, CHUNK), dtype=bool))[:, :, None]

    def step(S, xs):
        qb, kb, gb, vb = xs
        G = jnp.cumsum(gb, axis=2)
        diff = G[:, :, :, None, :] - G[:, :, None, :, :]
        decay = jnp.exp(jnp.where(lower, diff, -jnp.inf))
        scores = jnp.einsum('bhtd,bhsd,bhtsd->bhts', qb, kb, decay)
        o = jnp.einsum('bhts,bhsv->bhtv', scores, vb) + jnp.einsum('bhtd,bhdv->bhtv', qb * jnp.exp(G), S)
        return state_update(S, kb, G, vb), o

    S_fin, o = lax.scan(step, s0, (blocks(q), blocks(k), blocks(log_f), blocks(v)))
    o = o.transpose(1, 0, 3, 2, 4).reshape(B, T, H, v.shape[-1])
    return o, S_fin

def hgrn_direction(q, k, log_f, v, s0, reverse):
    if reverse:
        k, log_f, v = jnp.flip(k, 1), jnp.flip(log_f, 1), jnp.flip(v, 1)
        q = None if q is None else jnp.flip(q, 1)
    o, s = chunk_scan(k, log_f, v, s0, q)
    if reverse and o is not None:
        o = jnp.flip(o, 1)
    return o, s

def hgrn_readout(o, g_raw, gain):
    o = normalize_f32(o) * gain.astype(F32)
    o = o * jax.nn.silu(hgrn_heads(g_raw.astype(F32), HGRN_HEAD_V))
    return o.reshape(o.shape[:2] + (HGRN_WIDTH,)).astype(g_raw.dtype)

def token_mix(h_lat, h_ctx, w_in, q_norm_g, kv_norm_g, w_uq, w_ukv, hgrn_g, lb_fwd, lb_bwd, rope, need_ctx):
    B = h_lat.shape[0]
    dq_l, dkv_l, kr_l, fo_l, hq_l, hff_l, hfb_l, hi_l, hg_l = split_columns(h_lat @ w_in)
    dq_c, dkv_c, kr_c, fo_c, hq_c, hff_c, hfb_c, hi_c, hg_c = split_columns(h_ctx @ w_in)

    kn_c, krr_c, v_c = mla_keys_values(dkv_c, kr_c, kv_norm_g, w_ukv, None)
    kn_l, krr_l, v_l = mla_keys_values(dkv_l, kr_l, kv_norm_g, w_ukv, rope)
    qn_l, qr_l = mla_queries(dq_l, q_norm_g, w_uq, rope)
    att_l = block_attention(qn_l, qr_l, jnp.concatenate([kn_c, kn_l], axis=1),
                            jnp.concatenate([krr_c, krr_l], axis=1), jnp.concatenate([v_c, v_l], axis=1))

    four_l = fourier_mix(fo_l)

    kf_c, gf_c = hgrn_forget(hff_c, lb_fwd)
    kb_c, gb_c = hgrn_forget(hfb_c, lb_bwd)
    v_hc = hgrn_heads(hi_c.astype(F32), HGRN_HEAD_V)
    q_hc = hgrn_heads(jax.nn.silu(hq_c.astype(F32)), HGRN_EXPAND) if need_ctx else None
    zero = jnp.zeros((B, HGRN_HEADS, HGRN_EXPAND, HGRN_HEAD_V), F32)
    oc_f, sc_f = hgrn_direction(q_hc, kf_c, gf_c, v_hc, zero, False)
    oc_b, sc_b = hgrn_direction(q_hc, kb_c, gb_c, v_hc, zero, True)

    kf_l, gf_l = hgrn_forget(hff_l, lb_fwd)
    kb_l, gb_l = hgrn_forget(hfb_l, lb_bwd)
    v_hl = hgrn_heads(hi_l.astype(F32), HGRN_HEAD_V)
    q_hl = hgrn_heads(jax.nn.silu(hq_l.astype(F32)), HGRN_EXPAND)
    ol_f, _ = hgrn_direction(q_hl, kf_l, gf_l, v_hl, sc_f, False)
    ol_b, _ = hgrn_direction(q_hl, kb_l, gb_l, v_hl, sc_b, True)
    rec_l = hgrn_readout(ol_f + ol_b, hg_l, hgrn_g)

    mix_lat = jnp.concatenate([att_l, four_l, rec_l.astype(att_l.dtype)], axis=-1)
    if not need_ctx:
        return mix_lat, None

    qn_c, qr_c = mla_queries(dq_c, q_norm_g, w_uq, None)
    att_c = block_attention(qn_c, qr_c, kn_c, krr_c, v_c)
    four_c = fourier_mix(fo_c)
    rec_c = hgrn_readout(oc_f + oc_b, hg_c, hgrn_g)
    mix_ctx = jnp.concatenate([att_c, four_c, rec_c.astype(att_c.dtype)], axis=-1)
    return mix_lat, mix_ctx

def swiglu(h, w_gate, w_up, w_down):
    return (jax.nn.silu(h @ w_gate) * (h @ w_up)) @ w_down

def moe_swiglu(h, w_router, w_gate, w_up, w_down):
    logits = jnp.einsum('btd,de->bte', h, w_router).astype(F32)
    top_v, top_i = lax.top_k(logits, TOP_K)
    top_w = jax.nn.softmax(top_v, axis=-1)
    gates = jnp.sum(jax.nn.one_hot(top_i, N_EXPERTS, dtype=F32) * top_w[..., None], axis=-2)
    y = jnp.zeros(h.shape, F32)
    for e in range(N_EXPERTS):
        y = y + gates[..., e:e + 1] * swiglu(h, w_gate[e], w_up[e], w_down[e]).astype(F32)
    return y.astype(h.dtype)

def setup_inputs(seed: int = 0) -> dict:
    key = jax.random.key(seed)
    ks = jax.random.split(key, 26)

    def nrm(k, shape, scale):
        return scale * jax.random.normal(k, shape, F32)

    return {
        'x': nrm(ks[0], (BATCH, SEQ, D_MODEL), 1.0),
        'c': nrm(ks[1], (BATCH, D_MODEL), 1.0),
        'ctx': nrm(ks[2], (BATCH, CTX_LEN, D_MODEL), 1.0),
        'c_ctx': nrm(ks[3], (D_MODEL,), 1.0),
        'w_ada': nrm(ks[4], (DEPTH, D_MODEL, N_MOD * D_MODEL), 0.5 * D_MODEL ** -0.5),
        'b_ada': nrm(ks[5], (DEPTH, N_MOD * D_MODEL), 0.02),
        'w_in': nrm(ks[6], (DEPTH, D_MODEL, IN_WIDTH), D_MODEL ** -0.5),
        'q_norm_g': 1.0 + nrm(ks[7], (DEPTH, MLA_Q_RANK), 0.02),
        'kv_norm_g': 1.0 + nrm(ks[8], (DEPTH, MLA_KV_RANK), 0.02),
        'w_uq': nrm(ks[9], (DEPTH, MLA_Q_RANK, MLA_HEADS * (MLA_NOPE + MLA_ROPE)), MLA_Q_RANK ** -0.5),
        'w_ukv': nrm(ks[10], (DEPTH, MLA_KV_RANK, MLA_HEADS * (MLA_NOPE + MLA_V)), MLA_KV_RANK ** -0.5),
        'hgrn_norm_g': 1.0 + nrm(ks[11], (DEPTH, HGRN_HEAD_V), 0.02),
        'lb_logits': nrm(ks[12], (2, DEPTH, HGRN_KEY_WIDTH), 0.5),
        'w_out': nrm(ks[13], (DEPTH, MIX_WIDTH, D_MODEL), MIX_WIDTH ** -0.5),
        'ffn_w_gate': nrm(ks[14], (N_DENSE, D_MODEL, D_FF), D_MODEL ** -0.5),
        'ffn_w_up': nrm(ks[15], (N_DENSE, D_MODEL, D_FF), D_MODEL ** -0.5),
        'ffn_w_down': nrm(ks[16], (N_DENSE, D_FF, D_MODEL), D_FF ** -0.5),
        'moe_router': nrm(ks[17], (N_MOE, D_MODEL, N_EXPERTS), D_MODEL ** -0.5),
        'moe_w_gate': nrm(ks[18], (N_MOE, N_EXPERTS, D_MODEL, D_FF), D_MODEL ** -0.5),
        'moe_w_up': nrm(ks[19], (N_MOE, N_EXPERTS, D_MODEL, D_FF), D_MODEL ** -0.5),
        'moe_w_down': nrm(ks[20], (N_MOE, N_EXPERTS, D_FF, D_MODEL), D_FF ** -0.5),
        'final_g': 1.0 + nrm(ks[21], (D_MODEL,), 0.02),
    }

def reference(x, c, ctx, c_ctx, w_ada, b_ada, w_in, q_norm_g, kv_norm_g, w_uq, w_ukv, hgrn_norm_g, lb_logits,
              w_out, ffn_w_gate, ffn_w_up, ffn_w_down, moe_router, moe_w_gate, moe_w_up, moe_w_down, final_g):
    dt = x.dtype
    n_lat = x.shape[1]
    n_ctx = ctx.shape[1]
    rope = axial_rope_tables(n_lat)
    lower_bounds = hgrn_lower_bounds(lb_logits)
    cond_lat = jax.nn.silu(c.astype(F32))
    cond_ctx = jax.nn.silu(c_ctx.astype(F32))

    for layer in range(DEPTH):
        need_ctx = layer < DEPTH - 1
        wa = w_ada[layer].astype(F32)
        ba = b_ada[layer].astype(F32)
        m_lat = jnp.split((cond_lat @ wa + ba)[:, None, :], N_MOD, axis=-1)
        m_ctx = jnp.split(cond_ctx @ wa + ba, N_MOD, axis=-1)

        h_lat = modulate(x, m_lat[0], m_lat[1])
        h_ctx = modulate(ctx, m_ctx[0], m_ctx[1])
        mix_lat, mix_ctx = token_mix(h_lat, h_ctx, w_in[layer], q_norm_g[layer], kv_norm_g[layer], w_uq[layer],
                                     w_ukv[layer], hgrn_norm_g[layer], lower_bounds[0, layer],
                                     lower_bounds[1, layer], rope, need_ctx)
        x = (x + m_lat[2] * (mix_lat @ w_out[layer])).astype(dt)
        if need_ctx:
            ctx = (ctx + m_ctx[2] * (mix_ctx @ w_out[layer])).astype(ctx.dtype)

        h = modulate(x, m_lat[3], m_lat[4])
        if need_ctx:
            h = jnp.concatenate([modulate(ctx, m_ctx[3], m_ctx[4]), h], axis=1)
        if layer % 2 == 0:
            j = layer // 2
            y = swiglu(h, ffn_w_gate[j], ffn_w_up[j], ffn_w_down[j])
        else:
            j = layer // 2
            y = moe_swiglu(h, moe_router[j], moe_w_gate[j], moe_w_up[j], moe_w_down[j])
        if need_ctx:
            ctx = (ctx + m_ctx[5] * y[:, :n_ctx]).astype(ctx.dtype)
            x = (x + m_lat[5] * y[:, n_ctx:]).astype(dt)
        else:
            x = (x + m_lat[5] * y).astype(dt)

    return rms_norm(x, final_g)


_drawn_inputs = setup_inputs


def setup_inputs(seed=0):
    import zlib

    import numpy as np

    out = dict(_drawn_inputs(seed))
    spreads = {}
    factors = {'ctx': 2.851,
     'q_norm_g': 8.0,
     'kv_norm_g': 8.0,
     'hgrn_norm_g': 7.203,
     'lb_logits': 6.028,
     'final_g': 2.747}
    for name, (base, spread) in spreads.items():
        noise = np.random.default_rng([zlib.crc32(name.encode()), seed]).standard_normal(out[name].shape)
        drawn = base * np.exp(spread * noise) if base else spread * noise
        out[name] = jnp.asarray(drawn.astype(out[name].dtype))
    for name, factor in factors.items():
        out[name] = (out[name] * factor).astype(out[name].dtype)
    return out
```

```python
from contextlib import ExitStack

import numpy as np

import concourse.bass as bass
from concourse import mybir

F32 = mybir.dt.float32
I32 = mybir.dt.int32
U8 = mybir.dt.uint8
U32 = mybir.dt.uint32
ALU = mybir.AluOpType
ACT = mybir.ActivationFunctionType
AX = mybir.AxisListType

P = 128
D = 1024
KD = D // P
SEG = 256
T = 2 * SEG
NBLK = T // P
DEPTH = 2
EPS = 1e-6
GRID_W = 64

HEADS = 8
NOPE, ROPE, DV = 64, 32, 64
QK = NOPE + ROPE
Q_RANK, KV_RANK = 256, 128
ATT_SCALE = float(QK) ** -0.5

FOUR_CH = 64
RH = 4
RV = 64
LEVELS = [64, 32, 16, 8, 4, 2, 1]
NL = len(LEVELS)

D_FF = 2816
KF = D_FF // P
NE = 8
REGION = 16960

SLOTS = 11
SLAB = 1024
N_FFN_SLABS = 2 * KF + 3 * KD
BANKS = 8
FWD, BWD = 0, 1
CTX, LAT = 0, 1
N_ADA = 6 * D // P

WIN = ([("ff", i) for i in range(8)] + [("hi", 0), ("hi", 1)] + [("hq", i) for i in range(4)]
       + [("hg", i) for i in range(2)] + [("dq", i) for i in range(2)] + [("dkv", 0), ("kr", 0)]
       + [("fo", i) for i in range(2)] + [("uq", 0), ("uq", 1), ("ukv", 0)])


def query_blocks(layer):
    return [0, 1, 2, 3] if layer == 0 else [2, 3]


def query_segments(layer):
    return [CTX, LAT] if layer == 0 else [LAT]


def state_steps(layer):
    fwd = [(FWD, b) for b in (0, 1, 2)]
    bwd = [(BWD, b) for b in (1, 0, 3)]
    return [s for pair in zip(fwd, bwd) for s in pair]


def incoming(direction, block):
    if direction == FWD:
        return block - 1 if block > 0 else None
    return {1: None, 0: 1, 3: 0, 2: 3}[block]


def attention_units(layer):
    return [(h, s) for s in query_segments(layer) for h in range(HEADS)]


def key_blocks(seg):
    return [0, 1] if seg == CTX else [0, 1, 2, 3]


class Tiles:

    def __init__(self):
        self.number, self.consumer, self.rank = {}, [], []
        self.count = {"act": 0, "dve": 0}

    def add(self, name, consumer):
        self.number[name] = len(self.consumer)
        self.consumer.append(consumer)
        self.count[consumer] += 1
        self.rank.append(self.count[consumer])


def plan_tiles():
    t = Tiles()
    for L in range(DEPTH):
        for b in range(3):
            t.add(("ada", L, b), "act")
        for b in range(3):
            t.add(("adaT", L, b), "dve")
        t.add(("ss1", L), "dve")
        for i in range(8):
            t.add(("ff", L, i), "act")
        for b in range(NBLK):
            t.add(("hi", L, b), "dve")
        for i in range(4):
            t.add(("hq", L, i), "act")
        for i in range(2):
            t.add(("hg", L, i), "act")
        for d, b in state_steps(L):
            t.add(("kT", L, d, b), "act")
            t.add(("st", L, d, b), "dve")
        for b in query_blocks(L):
            t.add(("diag", L, b), "dve")
            for d in (FWD, BWD):
                for l in range(NL):
                    t.add(("lv", L, b, d, l), "dve")
                if incoming(d, b) is not None:
                    t.add(("in", L, b, d), "dve")
            t.add(("o", L, b), "dve")
        for i in range(2):
            t.add(("rms", L, i), "dve")
        for i in range(2):
            t.add(("dq", L, i), "dve")
        t.add(("dkv", L), "dve")
        t.add(("kr", L), "dve")
        for i in range(2):
            t.add(("fo", L, i), "act")
        for b in query_blocks(L):
            t.add(("f1", L, b), "act")
        for s in query_segments(L):
            for c in range(2):
                t.add(("f2", L, s, c), "dve")
        t.add(("ssq", L), "dve")
        t.add(("sskv", L), "dve")
        for h in range(HEADS):
            t.add(("q", L, h), "dve")
        for j in range(HEADS // 2):
            t.add(("kn", L, j), "act")
        for b in range(NBLK):
            t.add(("v", L, b), "act")
        units = attention_units(L)
        for i in range(len(units) + 2):
            if i < len(units):
                for qb in range(2):
                    t.add(("s", L, i, qb), "act")
            if 1 <= i <= len(units):
                for kb2 in range(len(key_blocks(units[i - 1][1])) // 2):
                    t.add(("pT", L, i - 1, kb2), "dve")
            if i >= 2:
                t.add(("pv", L, i - 2), "dve")
        for m in range(KD):
            t.add(("wo", L, m), "dve")
        t.add(("ss2", L), "dve")
        if L == 0:
            for k in range(KF):
                t.add(("g", k), "act")
                t.add(("u", k), "dve")
            for m in range(KD):
                t.add(("dn", m), "dve")
        else:
            t.add(("rt",), "dve")
            for j in range(4):
                t.add(("ht", j), "act")
            t.add(("rank",), "dve")
            for j in range(2):
                t.add(("ga0", j), "act")
    return t


TL = plan_tiles()
NR = 6


def range_width(r):
    return 512 if r < NR - 1 else D_FF - 512 * (NR - 1)


EXPERT_TILES = [(("selT",), "dve")]
for _r in range(NR + 1):
    if _r < NR:
        EXPERT_TILES += [(("g", _r), "act"), (("u", _r), "dve")]
    if _r:
        EXPERT_TILES += [(("hT", _r - 1), "act")]
EXPERT_TILES += [(("dn", 0), "act"), (("dn", 1), "dve"), (("ga", 0), "act"), (("ga", 1), "dve")]
EXPERT_TILES += [(("y", j), "dve") for j in range(4)]
N_EX = len(EXPERT_TILES)
EX_AT = {name: i for i, (name, _) in enumerate(EXPERT_TILES)}
EX = {c: sum(q == c for _, q in EXPERT_TILES) for c in ("act", "dve")}
N_BEFORE = len(TL.consumer)
BEFORE = TL.count


def rank_in(consumer, upto):
    return sum(c == consumer for _, c in EXPERT_TILES[:upto + 1])


def plan_pass_slabs():
    out = []
    for r in range(NR):
        for m in "gu":
            out += [(m, r, i) for i in range(KD * range_width(r) // SLAB)]
    return out + [("dn", k) for k in range(KF)]


PASS_SLABS = plan_pass_slabs()
N_PS = len(PASS_SLABS)
assert N_PS % SLOTS == 0


def closes(slab):
    if slab[0] == "dn":
        return ("dn", 1) if slab[1] == KF - 1 else None
    m, r, i = slab
    return (m, r) if i == KD * range_width(r) // SLAB - 1 else None


OWN_PER_PASS = sum(closes(q) is None for q in PASS_SLABS)
MAX_EXTRA = 3
N_PASSES = NE + MAX_EXTRA


def plan_slabs():
    order = []
    for L in range(DEPTH):
        order += [("ada", L, k, n) for k in range(KD) for n in range(6)]
        order += [("win", L, j) for j in range(len(WIN))]
        order += [("wo", L, m) for m in range(KD)]
        if L == 0:
            order += [("ffn", j) for j in range(N_FFN_SLABS)]
    return {name: i for i, name in enumerate(order)}


SL = plan_slabs()
MOE_SLAB0 = len(SL)
OWN_BEFORE = DEPTH * (6 * KD - 3)


def slab_tile(name):
    if name[0] == "ada":
        _, L, k, n = name
        return ("ada", L, n // 2) if k == KD - 1 and n % 2 else None
    if name[0] == "win":
        _, L, j = name
        kind, i = WIN[j]
        if kind == "hi":
            return ("hi", L, NBLK - 1)
        if kind == "uq":
            return ("q", L, HEADS - 1)
        if kind == "ukv":
            return ("v", L, NBLK - 1)
        return (kind, L) if kind in ("dkv", "kr") else (kind, L, i)
    if name[0] == "wo":
        return name
    return ffn_tile(name[1])


def ffn_tile(j):
    if j < 2 * KF:
        return ("gu"[j % 2], j // 2)
    return ("dn", (j - 2 * KF) // 3)


def build(nc, a):
    ctx = ExitStack()
    with ctx:
        def sb(name, shape, dt=F32):
            return ctx.enter_context(nc.sbuf_tensor(name, shape, dt))

        def sem(name):
            return ctx.enter_context(nc.semaphore(name))

        x = sb("x", [P, KD, T])
        h = sb("h", [P, KD, T])
        mix = sb("mix", [P, KD, T])
        ring = sb("ring", [P, SLOTS, SLAB])
        ident = sb("ident", [P, P])
        ones = sb("ones", [P, P])
        ones_blk = sb("ones_blk", [P, P])
        mask = sb("mask", [P, 2, NL, P], I32)
        dftc = sb("dftc", [P, 2 * P])
        dftt = sb("dftt", [P, 2, 2, SEG])
        rope_t = sb("rope_t", [P, T])
        reset = sb("reset", [P, T])
        cond = sb("cond", [P, KD, 32])
        craw = sb("craw", [P, KD, 2])
        bada = sb("bada", [P, DEPTH, N_ADA])
        gains = sb("gains", [P, DEPTH, 4])
        fing = sb("fing", [P, KD])
        iota8 = sb("iota8", [P, NE])
        iota = sb("iota", [P, P])
        before = sb("before", [P, P])
        extra = sb("extra", [1, 1 + MAX_EXTRA], I32)
        lbl = sb("lbl", [P, DEPTH, 8])
        lb = sb("lb", [P, 2, DEPTH, 8])
        lbt = sb("lbt", [P, 4, DEPTH, 8])
        mods = sb("mods", [P, 2, N_ADA])
        router = sb("router", [P, KD, NE])
        rstd = sb("rstd", [P, T])
        msq = sb("msq", [P, T])
        smax = sb("smax", [P, 4, 2 * HEADS * 2])
        region = sb("region", [P, REGION])

        def carve(shapes):
            out, at = [], 0
            for s in shapes:
                n = int(np.prod(s))
                v = region[:, at:at + n]
                at += n
                if len(s) == 2:
                    v = v.rearrange("p (a b) -> p a b", a=s[0])
                elif len(s) == 3:
                    v = v.rearrange("p (a b c) -> p a b c", a=s[0], b=s[1])
                out.append(v)
            assert at <= REGION, at
            return out

        hi, hg, kf, kb, gf, gb, lev, st, kd, sc, tot = carve([
            [NBLK, RH * RV], [2, T], [RH, T], [RH, T], [RH, T], [RH, T],
            [NL + 1, RH * P], [6, RH * RV], [RH * P], [RH * P], [4, RH, NBLK]])
        rq = mix[:, 0:4, :]
        kkf, kkb = lev[:, 0:4, :], lev[:, 4:8, :]
        kt = [msq, rstd]
        osq = kf[:, 0:2, :]
        k_of, g_of = (kf, kb), (gf, gb)
        (ada_sb,) = carve([[3, 512]])
        dq, dkv, kall, qall, vtok, pt, prob = carve([
            [2, T], [T], [HEADS, T], [HEADS, T], [NBLK, HEADS * DV], [2, 4 * SEG], [4, T]])
        fo = region[:, 11776:11776 + 2 * T].rearrange("p (a b) -> p a b", a=2)
        f1 = prob
        lsq = vtok[:, 0:3, :]
        rt1, rt2 = prob[:, 0, :], prob[:, 1, :]
        (hid0,) = carve([[KF, T]])
        (ht, sel, selg, selt, xe, sg, hs, hT, ye, yacc, gates, lg, mx8, ix8, ixf, gt, one_hot,
         rank, cnt, over, at_pass, gate_pass, xsel) = carve([
            [2, D], [2, P], [2, P], [2 * P], [KD, P], [2, 512], [2, 512], [KF, P], [D], [KD, SEG],
            [2, NE], [2, NE], [2, 8], [2, 8], [2, 8], [4, 2, NE], [2, NE],
            [2, NE], [NE], [4, NE], [2, N_PASSES + 1], [2, N_PASSES + 1], [2, 3, NE]])
        ix8 = ix8.bitcast(U32)

        banks = [ctx.enter_context(nc.psum_tensor(f"bank{i}", [P, 512], F32)) for i in range(BANKS)]

        slab_full = [sem(f"slab_full{i}") for i in range(SLOTS)]
        slab_used = sem("slab_used")
        tile_full = sem("tile_full")
        free = {"act": sem("tile_emptied_act"), "dve": sem("tile_emptied_dve")}
        const_in = sem("const_in")
        dve_own = sem("dve_own")
        act_own = sem("act_own")
        cond_zero = sem("cond_zero")
        cond_ready = sem("cond_ready")
        lb_in = sem("lb_in")
        lb_exp = sem("lb_exp")
        sq_ready = sem("sq_ready")
        xn_ready = sem("xn_ready")
        h_ready = sem("h_ready")
        mods_ready = sem("mods_ready")
        var_ready = sem("var_ready")
        sel_own = sem("sel_own")
        sd_ready = sem("sd_ready")
        f_ready = sem("f_ready")
        g_ready = sem("g_ready")
        kk_in = sem("kk_in")
        kk_exp = sem("kk_exp")
        kk_ready = sem("kk_ready")
        lev_in = sem("lev_in")
        lev_exp = sem("lev_exp")
        lev_ready = sem("lev_ready")
        kd_ready = sem("kd_ready")
        rec_ready = sem("rec_ready")
        neg_max = sem("neg_max")
        exp_ready = sem("exp_ready")
        prob_ready = sem("prob_ready")
        k_ready = sem("k_ready")
        sel_ready = sem("sel_ready")
        gather_done = sem("gather_done")
        extra_ready = sem("extra_ready")
        final_full = sem("final_full")
        top_in = sem("top_in")
        top_exp = sem("top_exp")
        gates_ready = sem("gates_ready")
        out_ready = sem("out_ready")
        out_done = sem("out_done")
        block = ctx.enter_context(nc.Block())

        class Own:

            def __init__(self, eng, own):
                self.eng, self.own, self.counts, self.last, self.base = eng, own, {}, None, None

            def sig(self, ins, s=None):
                s = self.own if s is None else s
                ins.then_inc(s, 1)
                key = str(s)
                self.counts[key] = self.counts.get(key, 0) + 1
                self.last = (s, key)

            def settle(self):
                s, key = self.last
                n = self.counts[key]
                if self.base is not None:
                    e, per = self.base
                    n = e * per[key] + n
                self.eng.wait_ge(s, n)

        def full(eng, name):
            n = TL.number[name]
            eng.wait_ge(tile_full, n + 1)
            return banks[n % BANKS]

        def emptied(eng, name):
            n = TL.number[name]
            eng.wait_ge(free[TL.consumer[n]], TL.rank[n])

        def pass_full(eng, name, i):
            eng.wait_ge(tile_full, i * N_EX + (N_BEFORE + EX_AT[name] + 1))
            return banks[EX_AT[name] % BANKS]

        def pass_emptied(eng, name, i):
            c = EXPERT_TILES[EX_AT[name]][1]
            eng.wait_ge(free[c], i * EX[c] + (BEFORE[c] + rank_in(c, EX_AT[name])))

        def passes(eng, body):
            with eng.Fori(0, NE) as i:
                body(i)
            extra_passes(eng, body)

        def extra_passes(eng, body):
            eng.wait_ge(extra_ready, 1)
            n_extra = eng.value_load(extra[0:1, 0:1], min_val=0, max_val=MAX_EXTRA)
            with eng.Fori(0, MAX_EXTRA) as j:
                with eng.If(n_extra > j):
                    body(j + NE)

        def n_passes(eng):
            return eng.value_load(extra[0:1, 0:1], min_val=0, max_val=MAX_EXTRA) + NE

        def seg(s):
            return slice(s * SEG, (s + 1) * SEG)

        def lowc(v):
            return v.rearrange("p (a b) -> p a b", a=RH)

        N_CONST = 19

        @block.sync
        def _(sp):
            consts = [(craw, a["cond"]), (gains, a["gains"]), (bada, a["bada"]), (lbl, a["lbl"]),
                      (ident, a["ident"]), (ones, a["ones"]), (ones_blk, a["ones_blk"]),
                      (mask, a["mask"]), (dftc, a["dftc"]), (dftt, a["dftt"]), (rope_t, a["rope"]),
                      (reset, a["reset"]), (router, a["router"]), (fing, a["fing"]), (iota8, a["iota8"]),
                      (iota, a["iota"]), (before, a["before"])]
            assert len(consts) + 2 == N_CONST
            for dst, src in consts:
                sp.dma_start(dst[:], src).then_inc(const_in, 16)
            for s in range(2):
                sp.dma_start(x[:, :, seg(s)], a["x"][s]).then_inc(const_in, 16)

            names = list(SL)
            own_used = 0
            used_at = []
            for name in names:
                if slab_tile(name) is None:
                    own_used += 1
                    used_at.append((slab_used, own_used))
                else:
                    used_at.append((tile_full, TL.number[slab_tile(name)] + 1))

            def load(n, src):
                sp.dma_start(ring[:, n % SLOTS, 0:src.shape[-1]], src).then_inc(slab_full[n % SLOTS], 16)

            for n, name in enumerate(names):
                if n >= SLOTS:
                    sp.wait_ge(*used_at[n - SLOTS])
                if name[0] == "ada":
                    _, L, k, j = name
                    load(n, a["ada"][L, k * P:(k + 1) * P, j * SLAB:(j + 1) * SLAB])
                elif name[0] == "win":
                    load(n, a["win"][name[1], name[2]])
                elif name[0] == "wo":
                    load(n, a["wo"][name[1], name[2]])
                else:
                    load(n, a["ffn"][name[1]])
            def pass_load(j, expert):
                load(MOE_SLAB0 + j, a["moe"][bass.ds(expert, 1), j].rearrange("e p n -> (e p) n")
                     if not isinstance(expert, int) else a["moe"][expert, j])

            def pass_used(j, i):
                tile = closes(PASS_SLABS[j])
                if tile is None:
                    own = sum(closes(q) is None for q in PASS_SLABS[:j + 1])
                    sp.wait_ge(slab_used, i * OWN_PER_PASS + (OWN_BEFORE + own))
                else:
                    sp.wait_ge(tile_full, i * N_EX + (N_BEFORE + EX_AT[tile] + 1))

            def head(i, expert, before_loop=False):
                for j in range(SLOTS):
                    if before_loop:
                        sp.wait_ge(*used_at[MOE_SLAB0 + j - SLOTS])
                    else:
                        pass_used(N_PS + j - SLOTS, i - 1)
                    pass_load(j, expert)

            def rest(i, expert):
                for j in range(SLOTS, N_PS):
                    pass_used(j - SLOTS, i)
                    pass_load(j, expert)

            head(0, 0, before_loop=True)
            with sp.Fori(0, NE - 1) as i:
                rest(i, i)
                head(i + 1, i + 1)
            rest(NE - 1, NE - 1)

            def again(i):
                expert = sp.value_load(extra[0:1, bass.ds(i - (NE - 1), 1)], min_val=0, max_val=NE - 1)
                head(i, expert)
                rest(i, expert)

            extra_passes(sp, again)
            for i in range(2):
                sp.wait_ge(out_ready, 4 * (i + 1))
                sp.dma_start(a["out"][:, i * 4:(i + 1) * 4, :], h[:, i * 4:(i + 1) * 4, seg(LAT)]).then_inc(out_done, 16)
            sp.wait_ge(out_done, 32)

        @block.gpsimd
        def _(pool):
            pool.memset(cond[:, :, :], 0.0).then_inc(cond_zero, 1)

        @block.tensor
        def _(pe):
            def open_tile(name):
                n = TL.number[name]
                if n >= BANKS:
                    pe.wait_ge(free[TL.consumer[n - BANKS]], TL.rank[n - BANKS])
                return banks[n % BANKS]

            def slab_in(name):
                n = SL[name]
                pe.wait_ge(slab_full[n % SLOTS], 16 * (n // SLOTS + 1))
                return ring[:, n % SLOTS, :]

            def close(m):
                m.then_inc(tile_full, 1)

            def project(name, slab, rhs, cols, w=P, at=0, rows=None):
                bank = open_tile(name)
                s = slab_in(slab)
                for k in range(KD):
                    m = pe.matmul(bank[at:at + w, 0:cols], s[:, k * w:(k + 1) * w], rhs(k),
                                  start=(k == 0), stop=(k == KD - 1))
                close(m)

            def norm_sum(name, chunks, rhs, cols, sem_, base, stat):
                bank = open_tile(name)
                for k in range(chunks):
                    if sem_ is not None:
                        pe.wait_ge(sem_, base + k + 1)
                    m = pe.matmul(bank[:, 0:cols], stat[:, :], rhs(k), start=(k == 0), stop=(k == chunks - 1))
                close(m)

            n_kd = n_lev = 0
            pe.wait_ge(const_in, 16 * N_CONST)
            pe.wait_ge(cond_ready, 1)
            for L in range(DEPTH):
                q0 = 0 if L == 0 else SEG
                nq = T - q0
                acc = [open_tile(("ada", L, b)) for b in range(3)]
                for k in range(KD):
                    for n in range(6):
                        s = slab_in(("ada", L, k, n))
                        for j in range(2):
                            r = 2 * n + j
                            c0 = 32 * (r % 4)
                            m = pe.matmul(acc[r // 4][c0:c0 + 32, :], cond[:, k, :],
                                          s[:, j * 512:(j + 1) * 512], start=(k == 0), stop=(k == KD - 1),
                                          tile_position=(0, c0))
                        if slab_tile(("ada", L, k, n)) is None:
                            m.then_inc(slab_used, 1)
                        else:
                            close(m)
                for b in range(3):
                    bank = open_tile(("adaT", L, b))
                    emptied(pe, ("ada", L, b))
                    for c in range(4):
                        m = pe.transpose(bank[:, c * P:(c + 1) * P], ada_sb[:, b, c * P:(c + 1) * P], ident[:, :])
                    close(m)

                norm_sum(("ss1", L), KD, lambda k: h[:, k, :], T, sq_ready, 16 * L, ones)
                pe.wait_ge(h_ready, KD * (2 * L + 1))
                for i in range(8):
                    project(("ff", L, i), ("win", L, i), lambda k: h[:, k, :], T)
                s0, s1 = slab_in(("win", L, 8)), slab_in(("win", L, 9))
                for b in range(NBLK):
                    bank = open_tile(("hi", L, b))
                    for k in range(KD):
                        s = (s0, s1)[k // 4]
                        m = pe.matmul(bank[:, 0:SEG], h[:, k, b * P:(b + 1) * P],
                                      s[:, (k % 4) * SEG:(k % 4 + 1) * SEG], start=(k == 0), stop=(k == KD - 1))
                    close(m)
                for i in range(4):
                    project(("hq", L, i), ("win", L, 10 + i), lambda k: h[:, k, q0:T], nq)
                for i in range(2):
                    project(("hg", L, i), ("win", L, 14 + i), lambda k: h[:, k, q0:T], nq)

                pe.wait_ge(kk_ready, 2 * L + 2)
                for i, (d, b) in enumerate(state_steps(L)):
                    bank = open_tile(("kT", L, d, b))
                    kk = (kkf, kkb)[d]
                    for hh in range(RH):
                        m = pe.transpose(bank[:, hh * P:(hh + 1) * P], kk[:, hh, b * P:(b + 1) * P], ident[:, :])
                    close(m)
                    bank = open_tile(("st", L, d, b))
                    emptied(pe, ("kT", L, d, b))
                    for hh in range(RH):
                        m = pe.matmul(bank[:, hh * RV:(hh + 1) * RV], kt[i % 2][:, hh * P:(hh + 1) * P],
                                      hi[:, b, hh * RV:(hh + 1) * RV], start=True, stop=True)
                    close(m)

                for b in query_blocks(L):
                    bank = open_tile(("diag", L, b))
                    n_kd += 1
                    pe.wait_ge(kd_ready, n_kd)
                    for hh in range(RH):
                        m = pe.matmul(bank[:, hh * P:(hh + 1) * P], kd[:, hh * P:(hh + 1) * P],
                                      rq[:, hh, b * P:(b + 1) * P], start=True, stop=True)
                    close(m)
                    for d in (FWD, BWD):
                        n_lev += 1
                        pe.wait_ge(lev_ready, n_lev)
                        for l in range(NL):
                            bank = open_tile(("lv", L, b, d, l))
                            for hh in range(RH):
                                v = lev[:, l, hh * P:(hh + 1) * P]
                                m = pe.matmul(bank[:, hh * P:(hh + 1) * P], v, v, start=True, stop=True)
                            close(m)
                        if incoming(d, b) is None:
                            continue
                        i = state_steps(L).index((d, incoming(d, b)))
                        bank = open_tile(("in", L, b, d))
                        for hh in range(RH):
                            r0 = (hh % 2) * RV
                            m = pe.matmul(bank[r0:r0 + RV, (hh // 2) * P:(hh // 2 + 1) * P],
                                          st[:, i, hh * RV:(hh + 1) * RV], lev[:, NL, hh * P:(hh + 1) * P],
                                          start=True, stop=True)
                        close(m)
                    bank = open_tile(("o", L, b))
                    emptied(pe, ("lv", L, b, BWD, NL - 1))
                    for hh in range(RH):
                        r0 = (hh % 2) * RV
                        m = pe.matmul(bank[r0:r0 + RV, (hh // 2) * P:(hh // 2 + 1) * P],
                                      hi[:, b, hh * RV:(hh + 1) * RV], sc[:, hh * P:(hh + 1) * P],
                                      start=True, stop=True)
                    close(m)
                for i in range(2):
                    norm_sum(("rms", L, i), 1, lambda k: osq[:, i, q0:T], nq, rec_ready, 4 * L + i, ones_blk)

                for i in range(2):
                    project(("dq", L, i), ("win", L, 16 + i), lambda k: h[:, k, q0:T], nq)
                project(("dkv", L), ("win", L, 18), lambda k: h[:, k, :], T)
                project(("kr", L), ("win", L, 19), lambda k: h[:, k, :], T, w=64, at=64)
                for i in range(2):
                    project(("fo", L, i), ("win", L, 20 + i), lambda k: h[:, k, q0:T], nq)
                for b in query_blocks(L):
                    bank = open_tile(("f1", L, b))
                    emptied(pe, ("fo", L, 1))
                    for c in range(2):
                        m = pe.matmul(bank[:, c * SEG:(c + 1) * SEG], fo[:, c, b * P:(b + 1) * P], dftc[:, :],
                                      start=True, stop=True)
                    close(m)
                for s in query_segments(L):
                    for c in range(2):
                        bank = open_tile(("f2", L, s, c))
                        emptied(pe, ("f1", L, 2 * s + 1))
                        for t in range(2):
                            for part in range(2):
                                m = pe.matmul(bank[:, 0:SEG],
                                              f1[:, 2 * s + t, c * SEG + part * P:c * SEG + (part + 1) * P],
                                              dftt[:, part, t, :], start=(t == 0 and part == 0),
                                              stop=(t == 1 and part == 1))
                        close(m)
                pe.wait_ge(k_ready, 6 * L + 3)
                norm_sum(("ssq", L), 2, lambda k: lsq[:, k, q0:T], nq, None, 0, ones)
                norm_sum(("sskv", L), 1, lambda k: lsq[:, 2, :], T, None, 0, ones)
                pe.wait_ge(k_ready, 6 * L + 6)
                wuq = [slab_in(("win", L, 22)), slab_in(("win", L, 23))]
                for hh in range(HEADS):
                    bank = open_tile(("q", L, hh))
                    for k in range(2):
                        m = pe.matmul(bank[:, 0:nq], wuq[k][:, hh * P:(hh + 1) * P], dq[:, k, q0:T],
                                      start=(k == 0), stop=(k == 1))
                    close(m)
                wukv = slab_in(("win", L, 24))
                for j in range(HEADS // 2):
                    bank = open_tile(("kn", L, j))
                    m = pe.matmul(bank[:, :], wukv[:, j * P:(j + 1) * P], dkv[:, :], start=True, stop=True)
                    close(m)
                for b in range(NBLK):
                    bank = open_tile(("v", L, b))
                    m = pe.matmul(bank[:, :], dkv[:, b * P:(b + 1) * P], wukv[:, 512:1024], start=True, stop=True)
                    close(m)
                units = attention_units(L)
                n_prob0 = 0 if L == 0 else 2 * len(attention_units(0))
                emptied(pe, ("q", L, HEADS - 1))
                emptied(pe, ("v", L, NBLK - 1))
                for i in range(len(units) + 2):
                    if i < len(units):
                        hh, s = units[i]
                        for qb in range(2):
                            bank = open_tile(("s", L, i, qb))
                            c0 = s * SEG + qb * P
                            m = pe.matmul(bank[:, 0:P * len(key_blocks(s))], qall[0:QK, hh, c0:c0 + P],
                                          kall[0:QK, hh, 0:P * len(key_blocks(s))], start=True, stop=True)
                            close(m)
                    if 1 <= i <= len(units):
                        u = i - 1
                        pe.wait_ge(prob_ready, n_prob0 + 2 * (u + 1))
                        for k2 in range(len(key_blocks(units[u][1])) // 2):
                            bank = open_tile(("pT", L, u, k2))
                            for kk in range(2):
                                for qb in range(2):
                                    k0 = (2 * k2 + kk) * P
                                    m = pe.transpose(bank[:, kk * SEG + qb * P:kk * SEG + (qb + 1) * P],
                                                     prob[:, 2 * (u % 2) + qb, k0:k0 + P], ident[:, :])
                            close(m)
                    if i >= 2:
                        u = i - 2
                        hh, s = units[u]
                        kbs = key_blocks(s)
                        bank = open_tile(("pv", L, u))
                        emptied(pe, ("pT", L, u, len(kbs) // 2 - 1))
                        r0 = (hh % 2) * DV
                        for kb_ in kbs:
                            m = pe.matmul(bank[r0:r0 + DV, 0:SEG], vtok[:, kb_, hh * DV:(hh + 1) * DV],
                                          pt[:, u % 2, kb_ * SEG:(kb_ + 1) * SEG],
                                          start=(kb_ == 0), stop=(kb_ == kbs[-1]))
                        close(m)
                emptied(pe, ("pv", L, len(units) - 1))
                for m_ in range(KD):
                    project(("wo", L, m_), ("wo", L, m_), lambda k: mix[:, k, q0:T], nq)
                norm_sum(("ss2", L), KD, lambda k: h[:, k, q0:T], nq, sq_ready, 16 * L + 8, ones)
                pe.wait_ge(h_ready, KD * (2 * L + 2))
                if L == 0:
                    for k_ in range(KF):
                        project(("g", k_), ("ffn", 2 * k_), lambda k: h[:, k, :], T)
                        project(("u", k_), ("ffn", 2 * k_ + 1), lambda k: h[:, k, :], T)
                    for m_ in range(KD):
                        bank = open_tile(("dn", m_))
                        for k in range(KF):
                            if k % 8 == 0:
                                s = slab_in(("ffn", 2 * KF + 3 * m_ + k // 8))
                            if m_ == 0:
                                emptied(pe, ("u", k))
                            m = pe.matmul(bank[:, :], s[:, (k % 8) * P:(k % 8 + 1) * P], hid0[:, k, :],
                                          start=(k == 0), stop=(k == KF - 1))
                        close(m)

            bank = open_tile(("rt",))
            for b in range(2):
                for k in range(KD):
                    m = pe.matmul(bank[:, b * NE:(b + 1) * NE], h[:, k, SEG + b * P:SEG + (b + 1) * P],
                                  router[:, k, :], start=(k == 0), stop=(k == KD - 1))
            close(m)
            for j in range(4):
                bank = open_tile(("ht", j))
                for c in range(4):
                    b, k = divmod(4 * j + c, KD)
                    m = pe.transpose(bank[:, c * P:(c + 1) * P], h[:, k, SEG + b * P:SEG + (b + 1) * P], ident[:, :])
                close(m)
            pe.wait_ge(gates_ready, 1)
            bank = open_tile(("rank",))
            for c, parts in enumerate((((before, 0),), ((ones, 0), (before, 1)), ((ones, 0), (ones, 1)))):
                for n, (w, b) in enumerate(parts):
                    m = pe.matmul(bank[:, c * NE:(c + 1) * NE], w[:, :], one_hot[:, b, :],
                                  start=(n == 0), stop=(n == len(parts) - 1))
            close(m)

            def gather(opened, j):
                for c in range(4):
                    for b in range(2):
                        m = pe.matmul(opened[:, c * P:(c + 1) * P], ht[:, b, (4 * j + c) * P:(4 * j + c + 1) * P],
                                      sel[:, b, :], start=(b == 0), stop=(b == 1))
                close(m)

            emptied(pe, ("ht", 3))
            pe.wait_ge(sel_ready, 1)
            for j in range(2):
                gather(open_tile(("ga0", j)), j)
            pe.wait_ge(free["act"], BEFORE["act"])
            pe.wait_ge(free["dve"], BEFORE["dve"])

            def pe_pass(i):
                def pass_open(name):
                    at = EX_AT[name]
                    if at >= BANKS:
                        pass_emptied(pe, EXPERT_TILES[at - BANKS][0], i)
                    else:
                        was = max(q for q in range(N_EX) if q % BANKS == at % BANKS)
                        c = EXPERT_TILES[was][1]
                        pe.wait_ge(free[c], i * EX[c] + (BEFORE[c] - EX[c] + rank_in(c, was)))
                    return banks[at % BANKS]

                def pass_slab(slab):
                    n = MOE_SLAB0 + PASS_SLABS.index(slab)
                    pe.wait_ge(slab_full[n % SLOTS], i * (16 * N_PS // SLOTS) + 16 * (n // SLOTS + 1))
                    return ring[:, n % SLOTS, :]

                bank = pass_open(("selT",))
                for b in range(2):
                    m = pe.transpose(bank[:, b * P:(b + 1) * P], selg[:, b, :], ident[:, :])
                close(m)
                for c, n in (("act", 0), ("dve", 1)):
                    pe.wait_ge(free[c], i * EX[c] + (BEFORE[c] - EX[c] + rank_in(c, EX_AT[("ga", n)])))
                for r in range(NR + 1):
                    if r < NR:
                        w = range_width(r)
                        for mat in "gu":
                            bank = pass_open((mat, r))
                            for part in range(KD * w // SLAB):
                                s = pass_slab((mat, r, part))
                                for c in range(SLAB // w):
                                    k = part * (SLAB // w) + c
                                    m = pe.matmul(bank[:, 0:w], xe[:, k, :], s[:, c * w:(c + 1) * w],
                                                  start=(k == 0), stop=(k == KD - 1))
                                if closes((mat, r, part)) is None:
                                    m.then_inc(slab_used, 1)
                            close(m)
                    if r:
                        w = range_width(r - 1)
                        bank = pass_open(("hT", r - 1))
                        pass_emptied(pe, ("u", r - 1), i)
                        for c in range(w // P):
                            m = pe.transpose(bank[:, c * P:(c + 1) * P], hs[:, (r - 1) % 2, c * P:(c + 1) * P],
                                             ident[:, :])
                        close(m)
                acc = [pass_open(("dn", n)) for n in range(2)]
                for k in range(KF):
                    s = pass_slab(("dn", k))
                    if k % 4 == 0:
                        pass_emptied(pe, ("hT", k // 4), i)
                    for n in range(2):
                        m = pe.matmul(acc[n][:, :], hT[:, k, :], s[:, n * 512:(n + 1) * 512],
                                      start=(k == 0), stop=(k == KF - 1))
                        if k == KF - 1:
                            close(m)
                    if k < KF - 1:
                        m.then_inc(slab_used, 1)
                pe.wait_ge(sel_ready, i + 2)
                for j in range(2):
                    gather(pass_open(("ga", j)), j)
                pass_emptied(pe, ("dn", 0), i)
                pass_emptied(pe, ("dn", 1), i)
                for j in range(4):
                    bank = pass_open(("y", j))
                    for c in range(2):
                        m = pe.matmul(bank[:, c * SEG:(c + 1) * SEG], ye[:, (2 * j + c) * P:(2 * j + c + 1) * P],
                                      selt[:, :], start=True, stop=True)
                    close(m)

            passes(pe, pe_pass)
            for k in range(KD):
                pe.wait_ge(sq_ready, 32 + k + 1)
                m = pe.matmul(banks[0][:, 0:SEG], ones[:, :], h[:, k, seg(LAT)], start=(k == 0), stop=(k == KD - 1))
            m.then_inc(final_full, 1)

        @block.scalar
        def _(act):
            o = Own(act, act_own)
            n_sd = 0
            n_lev = 0

            def root(cols):
                nonlocal n_sd
                n_sd += 1
                act.wait_ge(var_ready, n_sd)
                o.sig(act.activation(msq[:, 0:cols], msq[:, 0:cols], ACT.Sqrt), sd_ready)

            def affine(base, cols, n0, segs):
                for k in range(KD):
                    act.wait_ge(xn_ready, n0 + k + 1)
                    for s in segs:
                        ins = act.activation(h[:, k, seg(s)], h[:, k, seg(s)], ACT.Identity,
                                             bias=mods[:, s, base + k:base + k + 1],
                                             scale=mods[:, s, base + KD + k:base + KD + k + 1])
                        o.sig(ins, h_ready if s == LAT else None)

            act.wait_ge(const_in, 16 * N_CONST)
            act.wait_ge(cond_zero, 1)
            o.sig(act.activation(cond[:, :, 0:2], craw[:, :, :], ACT.Silu), cond_ready)
            act.wait_ge(lb_in, 1)
            o.sig(act.activation(lbt[:, 1, :, :], lbt[:, 0, :, :], ACT.Exp), lb_exp)
            for L in range(DEPTH):
                q0 = 0 if L == 0 else SEG
                nq = T - q0
                for b in range(3):
                    bank = full(act, ("ada", L, b))
                    o.sig(act.activation(ada_sb[:, b, :], bank[:, :], ACT.Copy), free["act"])
                root(T)
                act.wait_ge(mods_ready, L + 1)
                affine(0, T, 16 * L, (CTX, LAT))
                for i in range(8):
                    bank = full(act, ("ff", L, i))
                    o.sig(act.activation(g_of[i // 4][:, i % 4, :], bank[:, :], ACT.Sigmoid), free["act"])
                for i in range(4):
                    bank = full(act, ("hq", L, i))
                    o.sig(act.activation(rq[:, i, q0:T], bank[:, 0:nq], ACT.Silu), free["act"])
                for i in range(2):
                    bank = full(act, ("hg", L, i))
                    o.sig(act.activation(hg[:, i, q0:T], bank[:, 0:nq], ACT.Silu), free["act"])
                for d in (FWD, BWD):
                    act.wait_ge(f_ready, 8 * L + 4 * (d + 1))
                    o.sig(act.activation(g_of[d], g_of[d], ACT.Ln), g_ready)
                act.wait_ge(kk_in, L + 1)
                o.sig(act.activation(kkf, kkf, ACT.Exp), kk_exp)
                o.sig(act.activation(kkb, gb, ACT.Exp), kk_exp)
                o.sig(act.activation(tot[:, 2:4, :, :], tot[:, 0:2, :, :], ACT.Exp), kk_exp)
                for i, (d, b) in enumerate(state_steps(L)):
                    bank = full(act, ("kT", L, d, b))
                    if i < 2 and i == 0:
                        o.settle()
                    o.sig(act.activation(kt[i % 2][:, :], bank[:, :], ACT.Copy), free["act"])
                for b in query_blocks(L):
                    for d in (FWD, BWD):
                        n_lev += 1
                        act.wait_ge(lev_in, n_lev)
                        o.sig(act.activation(lev[:, :, :], lev[:, :, :], ACT.Exp), lev_exp)
                for i in range(2):
                    root(nq)
                for i in range(2):
                    bank = full(act, ("fo", L, i))
                    o.sig(act.activation(fo[:, i, q0:T], bank[:, 0:nq], ACT.Copy), free["act"])
                for b in query_blocks(L):
                    bank = full(act, ("f1", L, b))
                    o.sig(act.activation(f1[:, b, :], bank[:, :], ACT.Copy), free["act"])
                root(nq)
                root(T)
                for j in range(HEADS // 2):
                    bank = full(act, ("kn", L, j))
                    o.sig(act.activation(kall[0:NOPE, 2 * j, :], bank[0:64, :], ACT.Copy))
                    o.sig(act.activation(kall[0:NOPE, 2 * j + 1, :], bank[64:128, :], ACT.Copy), free["act"])
                for b in range(NBLK):
                    bank = full(act, ("v", L, b))
                    o.sig(act.activation(vtok[:, b, :], bank[:, :], ACT.Copy), free["act"])
                n0 = 0 if L == 0 else 2 * len(attention_units(0))
                for i, (hh, s) in enumerate(attention_units(L)):
                    for qb in range(2):
                        bank = full(act, ("s", L, i, qb))
                        act.wait_ge(neg_max, n0 + 2 * i + qb + 1)
                        c = 2 * i + qb
                        nk = P * len(key_blocks(s))
                        o.sig(act.activation(prob[:, 2 * (i % 2) + qb, 0:nk], bank[:, 0:nk], ACT.Exp,
                                             bias=smax[:, 1, c:c + 1], scale=ATT_SCALE,
                                             accum_out=smax[:, 2, c:c + 1]), free["act"])
                root(nq)
                affine(3 * KD, nq, 16 * L + 8, query_segments(L))
                if L == 0:
                    for k in range(KF):
                        bank = full(act, ("g", k))
                        o.sig(act.activation(hid0[:, k, :], bank[:, :], ACT.Silu), free["act"])
            act.wait_ge(top_in, 1)
            o.sig(act.activation(gt[:, 1, :, 0:1], gt[:, 0, :, 0:1], ACT.Exp), top_exp)
            for j in range(4):
                bank = full(act, ("ht", j))
                o.sig(act.activation(ht[:, j // 2, (j % 2) * 512:(j % 2 + 1) * 512], bank[:, :], ACT.Copy),
                      free["act"])
            four = lambda v: v.rearrange("p (a b) -> p a b", a=4)
            for j in range(2):
                bank = full(act, ("ga0", j))
                o.sig(act.activation(xe[:, 4 * j:4 * j + 4, :], four(bank[:, :]), ACT.Copy), free["act"])

            def act_pass(i):
                for r in range(NR + 1):
                    if r < NR:
                        w = range_width(r)
                        bank = pass_full(act, ("g", r), i)
                        if r >= 2:
                            pass_emptied(act, ("u", r - 2), i)
                        else:
                            act.wait_ge(free["dve"], i * EX["dve"] + (BEFORE["dve"] - EX["dve"]
                                                                      + rank_in("dve", EX_AT[("u", NR - 2 + r)])))
                        act.activation(sg[:, r % 2, 0:w], bank[:, 0:w], ACT.Silu).then_inc(free["act"], 1)
                    if r:
                        w = range_width(r - 1)
                        bank = pass_full(act, ("hT", r - 1), i)
                        to = hT[:, 4 * (r - 1):4 * (r - 1) + w // P, :]
                        act.activation(to, bank[:, 0:w].rearrange("p (a b) -> p a b", b=P),
                                       ACT.Copy).then_inc(free["act"], 1)
                bank = pass_full(act, ("dn", 0), i)
                act.activation(ye[:, 0:512], bank[:, :], ACT.Copy).then_inc(free["act"], 1)
                bank = pass_full(act, ("ga", 0), i)
                act.activation(xe[:, 0:4, :], four(bank[:, :]), ACT.Copy).then_inc(free["act"], 1)

            passes(act, act_pass)
            root(SEG)

        @block.vector
        def _(dve):
            o = Own(dve, dve_own)
            n_sd = 0

            def norm(bank, cols, width, tile_sem=True):
                nonlocal n_sd
                n_sd += 1
                o.sig(dve.tensor_scalar(msq[:, 0:cols], bank[:, 0:cols], 1.0 / width, EPS, ALU.mult, ALU.add),
                      var_ready)
                dve.wait_ge(sd_ready, n_sd)
                if tile_sem:
                    o.sig(dve.reciprocal(rstd[:, 0:cols], msq[:, 0:cols]), free["dve"])
                else:
                    o.sig(dve.reciprocal(rstd[:, 0:cols], msq[:, 0:cols]))
                o.settle()

            def squares(cols):
                for k in range(KD):
                    o.sig(dve.tensor_tensor(h[:, k, cols], x[:, k, cols], x[:, k, cols], ALU.mult), sq_ready)

            def scaled(cols, n):
                for k in range(KD):
                    o.sig(dve.tensor_tensor(h[:, k, cols], x[:, k, cols], rstd[:, 0:n], ALU.mult), xn_ready)

            dve.wait_ge(const_in, 16 * N_CONST)
            o.sig(dve.tensor_tensor(lbt[:, 2, 0, :], lbl[:, 0, :], lbl[:, 1, :], ALU.max))
            o.settle()
            for i in range(DEPTH):
                last = dve.tensor_tensor(lbt[:, 0, i, :], lbl[:, i, :], lbt[:, 2, 0, :], ALU.subtract)
                o.sig(last, lb_in if i == DEPTH - 1 else None)
            dve.wait_ge(lb_exp, 1)
            o.sig(dve.tensor_tensor(lbt[:, 2, 1, :], lbt[:, 1, 0, :], lbt[:, 1, 1, :], ALU.add))
            o.settle()
            o.sig(dve.reciprocal(lbt[:, 3, 0, :], lbt[:, 2, 1, :]))
            o.settle()
            for i in range(DEPTH):
                o.sig(dve.tensor_tensor(lbt[:, 0, i, :], lbt[:, 1, i, :], lbt[:, 3, 0, :], ALU.mult))
            o.settle()
            o.sig(dve.tensor_tensor(lb[:, 0, 0, :], lbt[:, 0, 0, :], lbt[:, 0, 0, :], ALU.subtract))
            o.sig(dve.tensor_tensor(lbt[:, 3, 1, :], lbt[:, 0, 0, :], lbt[:, 0, 1, :], ALU.add))
            o.settle()
            o.sig(dve.tensor_tensor(lb[:, 0, 1, :], lbt[:, 3, 1, :], lbt[:, 0, 0, :], ALU.subtract))
            o.settle()
            o.sig(dve.tensor_scalar(lb[:, 1, :, :], lb[:, 0, :, :], -1.0, 1.0, ALU.mult, ALU.add))
            o.settle()

            for L in range(DEPTH):
                q0 = 0 if L == 0 else SEG
                nq = T - q0
                qs = slice(q0, T)
                squares(slice(0, T))
                for b in range(3):
                    bank = full(dve, ("adaT", L, b)).rearrange("p (c j s) -> p c j s", c=4, j=4)
                    for s in range(2):
                        to = mods[:, s, b * 16:(b + 1) * 16].rearrange("p (j c) -> p c j", j=4)
                        add = bada[:, L, b * 16:(b + 1) * 16].rearrange("p (j c) -> p c j", j=4)
                        o.sig(dve.tensor_tensor(to, bank[:, :, :, s], add, ALU.add), free["dve"] if s else None)
                o.settle()
                for i in (1, 4):
                    v = mods[:, :, i * KD:(i + 1) * KD]
                    o.sig(dve.tensor_scalar(v, v, 1.0, None, ALU.add), mods_ready if i == 4 else None)
                norm(full(dve, ("ss1", L)), T, D)
                scaled(slice(0, T), T)

                for i in range(8):
                    d, hh = divmod(i, 4)
                    emptied(dve, ("ff", L, i))
                    f = g_of[d][:, hh, :]
                    o.sig(dve.tensor_scalar(f, f, lb[:, 1, L, i:i + 1], lb[:, 0, L, i:i + 1], ALU.mult, ALU.add))
                    o.settle()
                    o.sig(dve.tensor_scalar(k_of[d][:, hh, :], f, -1.0, 1.0, ALU.mult, ALU.add), f_ready)
                for b in range(NBLK):
                    bank = full(dve, ("hi", L, b))
                    o.sig(dve.tensor_copy(hi[:, b, :], bank[:, 0:SEG]), free["dve"])
                dve.wait_ge(g_ready, 2 * L + 1)
                for hh in range(RH):
                    o.sig(dve.tensor_tensor_scan(gf[:, hh, :], reset[:, :], gf[:, hh, :], 0.0, ALU.mult, ALU.add))
                dve.wait_ge(g_ready, 2 * L + 2)
                for hh in range(RH):
                    o.sig(dve.tensor_tensor_scan(kkb[:, hh, :], reset[:, :], gb[:, hh, :], 0.0, ALU.mult, ALU.add))
                o.settle()
                ends = lambda v: v.rearrange("p h (b t) -> p h b t", t=P)[:, :, :, P - 1]
                o.sig(dve.tensor_copy(tot[:, 0, :, :], ends(gf)))
                o.sig(dve.tensor_copy(tot[:, 1, :, :], ends(kkb)))
                o.sig(dve.tensor_tensor(gb, kkb, gb, ALU.subtract))
                o.settle()
                blocks = lambda v: v.rearrange("p h (b t) -> p (h b) t", t=P)
                t0 = tot[:, 0, :, :].rearrange("p h b -> p (h b)").unsqueeze(2).to_broadcast([P, RH * NBLK, P])
                o.sig(dve.tensor_tensor(blocks(kkf), t0, blocks(gf), ALU.subtract), kk_in)
                dve.wait_ge(kk_exp, 3 * L + 3)
                o.sig(dve.tensor_tensor(kkf, kkf, kf, ALU.mult), kk_ready)
                o.sig(dve.tensor_tensor(kkb, kkb, kb, ALU.mult), kk_ready)
                steps = state_steps(L)
                for i, (d, b) in enumerate(steps):
                    bank = full(dve, ("st", L, d, b))
                    if incoming(d, b) is None:
                        o.sig(dve.tensor_copy(st[:, i, :], bank[:, 0:RH * RV]), free["dve"])
                        continue
                    was = steps.index((d, incoming(d, b)))
                    o.settle()
                    for hh in range(RH):
                        c = slice(hh * RV, (hh + 1) * RV)
                        o.sig(dve.scalar_tensor_tensor(st[:, i, c], st[:, was, c], tot[:, 2 + d, hh, b:b + 1],
                                                       bank[:, c], ALU.mult, ALU.add),
                              free["dve"] if hh == RH - 1 else None)
                o.settle()
                for b in query_blocks(L):
                    bs = slice(b * P, (b + 1) * P)
                    if b != query_blocks(L)[0]:
                        full(dve, ("diag", L, b - 1))
                    o.sig(dve.tensor_tensor(lowc(kd), kf[:, :, bs], kb[:, :, bs], ALU.add), kd_ready)
                    scopy = None
                    for d in (FWD, BWD):
                        for l, half in enumerate(LEVELS):
                            g = g_of[d][:, :, bs].rearrange("p h (n t) -> p h n t", t=2 * half)
                            z = lowc(lev[:, l, :]).rearrange("p h (n t) -> p h n t", t=2 * half)
                            at = half - 1 if d == FWD else half
                            shape = [P, RH, P // (2 * half), half]
                            mid = g[:, :, :, at:at + 1].to_broadcast(shape)
                            o.sig(dve.tensor_tensor(z[:, :, :, half:], g[:, :, :, half:], mid, ALU.subtract))
                            o.sig(dve.tensor_tensor(z[:, :, :, 0:half], mid, g[:, :, :, 0:half], ALU.subtract))
                        z = lowc(lev[:, NL, :])
                        if d == FWD:
                            o.sig(dve.tensor_copy(z, gf[:, :, bs]), lev_in)
                        else:
                            end = tot[:, 1, :, b:b + 1].to_broadcast([P, RH, P])
                            o.sig(dve.tensor_tensor(z, end, gb[:, :, bs], ALU.subtract), lev_in)
                        n_exp = sum(2 * len(query_blocks(q)) for q in range(L)) + \
                            2 * query_blocks(L).index(b) + d + 1
                        dve.wait_ge(lev_exp, n_exp)
                        for l, half in enumerate(LEVELS):
                            z = lowc(lev[:, l, :]).rearrange("p h (n t) -> p h n t", t=2 * half)
                            late, early = (rq, kf) if d == FWD else (kb, rq)
                            for sl, by in ((slice(half, 2 * half), late), (slice(0, half), early)):
                                w = by[:, :, bs].rearrange("p h (n t) -> p h n t", t=2 * half)
                                o.sig(dve.tensor_tensor(z[:, :, :, sl], z[:, :, :, sl], w[:, :, :, sl], ALU.mult))
                        z = lowc(lev[:, NL, :])
                        o.sig(dve.tensor_tensor(z, z, rq[:, :, bs], ALU.mult), lev_ready)
                        if d == FWD:
                            bank = full(dve, ("diag", L, b))
                            if b != query_blocks(L)[0]:
                                full(dve, ("o", L, b - 1))
                            o.sig(dve.tensor_copy(sc, bank[:, :]), free["dve"])
                        for l in range(NL):
                            bank = full(dve, ("lv", L, b, d, l))
                            m = mask[:, d, l, :].unsqueeze(1).to_broadcast([P, RH, P])
                            o.settle()
                            o.sig(dve.copy_predicated(lowc(sc), m, lowc(bank)), free["dve"])
                        if incoming(d, b) is not None:
                            bank = full(dve, ("in", L, b, d))
                            to = mix[:, 6:8, bs]
                            fr = bank[:, 0:2 * P].rearrange("p (a b) -> p a b", a=2)
                            first = d == FWD or incoming(FWD, b) is None
                            if first:
                                o.sig(dve.tensor_copy(to, fr), free["dve"])
                            else:
                                o.settle()
                                o.sig(dve.tensor_tensor(to, to, fr, ALU.add), free["dve"])
                    bank = full(dve, ("o", L, b))
                    to = mix[:, 6:8, bs]
                    o.settle()
                    o.sig(dve.tensor_tensor(to, to, bank[:, 0:2 * P].rearrange("p (a b) -> p a b", a=2), ALU.add),
                          free["dve"])
                o.settle()
                for i in range(2):
                    o.sig(dve.tensor_tensor(osq[:, i, qs], mix[:, 6 + i, qs], mix[:, 6 + i, qs], ALU.mult), rec_ready)
                for i in range(2):
                    norm(full(dve, ("rms", L, i)), nq, RV)
                    v = mix[:, 6 + i, qs]
                    o.sig(dve.scalar_tensor_tensor(v, v, gains[:, L, 3:4], rstd[:, 0:nq], ALU.mult, ALU.mult))
                    o.settle()
                    o.sig(dve.tensor_tensor(v, v, hg[:, i, qs], ALU.mult), rec_ready)

                o.settle()
                for i in range(2):
                    bank = full(dve, ("dq", L, i))
                    o.sig(dve.tensor_copy(dq[:, i, qs], bank[:, 0:nq]), free["dve"])
                bank = full(dve, ("dkv", L))
                o.sig(dve.tensor_copy(dkv, bank[:, :]), free["dve"])
                o.settle()
                for i in range(2):
                    o.sig(dve.tensor_tensor(lsq[:, i, qs], dq[:, i, qs], dq[:, i, qs], ALU.mult), k_ready)
                o.sig(dve.tensor_tensor(lsq[:, 2, :], dkv, dkv, ALU.mult), k_ready)

                def rotated(bank, n, out, tab):
                    o.settle()
                    o.sig(dve.tensor_tensor(rt1[64:96, 0:n], bank[64:96, 0:n], rope_t[64:96, tab], ALU.mult))
                    o.sig(dve.tensor_tensor(rt2[64:96, 0:n], bank[96:128, 0:n], rope_t[96:128, tab], ALU.mult),
                          free["dve"])
                    o.settle()
                    return dve.tensor_tensor(out, rt1[64:96, 0:n], rt2[64:96, 0:n], ALU.add)

                bank_kr = full(dve, ("kr", L))
                kr1 = kall[64:96, 0, :]
                o.sig(dve.tensor_tensor(kr1, bank_kr[64:96, :], rope_t[64:96, :], ALU.mult))
                o.sig(dve.tensor_tensor(kall[64:96, 1, :], bank_kr[96:128, :], rope_t[96:128, :], ALU.mult),
                      free["dve"])
                o.settle()
                o.sig(dve.tensor_tensor(kall[64:96, 2, :], kr1, kall[64:96, 1, :], ALU.add))
                o.settle()
                rest = kall[64:96, 2:3, :]
                o.sig(dve.tensor_copy(kall[64:96, 0:2, :], rest.to_broadcast([32, 2, T])))
                o.sig(dve.tensor_copy(kall[64:96, 3:8, :], rest.to_broadcast([32, 5, T])))
                for s in query_segments(L):
                    for c in range(2):
                        bank = full(dve, ("f2", L, s, c))
                        o.sig(dve.tensor_copy(mix[:, 4 + c, seg(s)], bank[:, 0:SEG]), free["dve"])
                norm(full(dve, ("ssq", L)), nq, Q_RANK)
                for i in range(2):
                    v = dq[:, i, qs]
                    o.sig(dve.scalar_tensor_tensor(v, v, gains[:, L, i:i + 1], rstd[:, 0:nq], ALU.mult, ALU.mult),
                          k_ready)
                norm(full(dve, ("sskv", L)), T, KV_RANK)
                o.sig(dve.scalar_tensor_tensor(dkv, dkv, gains[:, L, 2:3], rstd[:, :], ALU.mult, ALU.mult), k_ready)
                for hh in range(HEADS):
                    bank = full(dve, ("q", L, hh))
                    o.sig(dve.tensor_copy(qall[0:NOPE, hh, qs], bank[0:NOPE, 0:nq]))
                    ins = rotated(bank, nq, qall[64:96, hh, qs], qs)
                    o.sig(ins)

                units = attention_units(L)
                n0 = 0 if L == 0 else 2 * len(attention_units(0))
                for i in range(len(units) + 2):
                    if i < len(units):
                        for qb in range(2):
                            bank = full(dve, ("s", L, i, qb))
                            c = 2 * i + qb
                            nk = P * len(key_blocks(units[i][1]))
                            o.sig(dve.tensor_reduce(smax[:, 0, c:c + 1], bank[:, 0:nk], AX.X, ALU.max))
                            o.settle()
                            o.sig(dve.tensor_scalar(smax[:, 1, c:c + 1], smax[:, 0, c:c + 1], -ATT_SCALE, None,
                                                    ALU.mult), neg_max)
                        for qb in range(2):
                            c = 2 * i + qb
                            emptied(dve, ("s", L, i, qb))
                            o.sig(dve.reciprocal(smax[:, 3, c:c + 1], smax[:, 2, c:c + 1]))
                            o.settle()
                            nk = P * len(key_blocks(units[i][1]))
                            v = prob[:, 2 * (i % 2) + qb, 0:nk]
                            o.sig(dve.tensor_scalar(v, v, smax[:, 3, c:c + 1], None, ALU.mult), prob_ready)
                    if 1 <= i <= len(units):
                        u = i - 1
                        for k2 in range(len(key_blocks(units[u][1])) // 2):
                            bank = full(dve, ("pT", L, u, k2))
                            o.sig(dve.tensor_copy(pt[:, u % 2, k2 * 512:(k2 + 1) * 512], bank[:, :]), free["dve"])
                    if i >= 2:
                        u = i - 2
                        hh, s = units[u]
                        bank = full(dve, ("pv", L, u))
                        r0 = (hh % 2) * DV
                        o.sig(dve.tensor_copy(mix[r0:r0 + DV, hh // 2, seg(s)], bank[r0:r0 + DV, 0:SEG]),
                              free["dve"])

                def residual(bank, m, c0):
                    segs = query_segments(L)
                    for s in segs:
                        f0 = s * SEG - q0
                        o.sig(dve.scalar_tensor_tensor(x[:, m, seg(s)], bank[:, f0:f0 + SEG],
                                                       mods[:, s, c0 + m:c0 + m + 1], x[:, m, seg(s)],
                                                       ALU.mult, ALU.add),
                              free["dve"] if s == segs[-1] else None)

                for m in range(KD):
                    residual(full(dve, ("wo", L, m)), m, 2 * KD)
                o.settle()
                squares(qs)
                norm(full(dve, ("ss2", L)), nq, D)
                scaled(qs, nq)
                if L == 0:
                    for k in range(KF):
                        bank = full(dve, ("u", k))
                        emptied(dve, ("g", k))
                        o.sig(dve.tensor_tensor(hid0[:, k, :], hid0[:, k, :], bank[:, :], ALU.mult), free["dve"])
                    for m in range(KD):
                        residual(full(dve, ("dn", m)), m, 5 * KD)
                    o.settle()

            bank = full(dve, ("rt",))
            o.sig(dve.tensor_copy(lg, bank[:, 0:2 * NE].rearrange("p (a b) -> p a b", a=2)), free["dve"])
            o.settle()
            for b in range(2):
                o.sig(dve.max(mx8[:, b, :], lg[:, b, :]))
            o.settle()
            for b in range(2):
                o.sig(dve.max_index(ix8[:, b, :], mx8[:, b, :], lg[:, b, :]))
            o.sig(dve.tensor_tensor(gt[:, 0, :, 0:1], mx8[:, :, 1:2], mx8[:, :, 0:1], ALU.subtract), top_in)
            o.settle()
            o.sig(dve.tensor_copy(ixf[:, :, :], ix8[:, :, :]))
            dve.wait_ge(top_exp, 1)
            o.sig(dve.tensor_scalar(gt[:, 1, :, 1:2], gt[:, 1, :, 0:1], 1.0, None, ALU.add))
            o.settle()
            o.sig(dve.reciprocal(gt[:, 1, :, 2:3], gt[:, 1, :, 1:2]))
            o.settle()
            o.sig(dve.tensor_tensor(gt[:, 1, :, 3:4], gt[:, 1, :, 0:1], gt[:, 1, :, 2:3], ALU.mult))
            o.settle()
            for b in range(2):
                for i in range(2):
                    o.sig(dve.tensor_scalar(xsel[:, b, i, :], iota8[:, :], ixf[:, b, i:i + 1], None, ALU.is_equal))
            o.settle()
            for b in range(2):
                for i in range(2):
                    o.sig(dve.tensor_scalar(gt[:, 2 + i, b, :], xsel[:, b, i, :], gt[:, 1, b, 2 + i:3 + i], None,
                                            ALU.mult))
            o.settle()
            o.sig(dve.tensor_tensor(gates[:, :, :], gt[:, 2, :, :], gt[:, 3, :, :], ALU.add))
            o.sig(dve.tensor_tensor(one_hot[:, :, :], xsel[:, :, 0, :], xsel[:, :, 1, :], ALU.add), gates_ready)
            o.sig(dve.memset(yacc[:, :, :], 0.0))
            far = float(1 << 20)
            bank = full(dve, ("rank",))
            o.sig(dve.tensor_copy(rank, bank[:, 0:2 * NE].rearrange("p (a b) -> p a b", a=2)))
            o.sig(dve.tensor_copy(cnt, bank[:, 2 * NE:3 * NE]), free["dve"])
            o.sig(dve.tensor_scalar(lg, one_hot, -far, far, ALU.mult, ALU.add))
            o.settle()
            o.sig(dve.tensor_tensor(rank, rank, lg, ALU.add))
            o.sig(dve.tensor_scalar(over[:, 0, :], cnt, float(P), None, ALU.is_gt))
            o.settle()
            o.sig(dve.tensor_tensor_scan(over[:, 1, :], ones[:, 0:NE], over[:, 0, :], 0.0, ALU.mult, ALU.add))
            o.settle()
            for j in range(MAX_EXTRA):
                o.sig(dve.tensor_scalar(xsel[:, 0, j, :], over[:, 1, :], float(j + 1), None, ALU.is_equal))
            o.settle()
            for j in range(MAX_EXTRA):
                o.sig(dve.tensor_tensor(xsel[:, 0, j, :], xsel[:, 0, j, :], over[:, 0, :], ALU.mult))
            o.settle()
            o.sig(dve.tensor_copy(at_pass[:, :, 0:NE], rank))
            o.sig(dve.tensor_copy(gate_pass[:, :, 0:NE], gates))
            o.sig(dve.memset(at_pass[:, :, N_PASSES:N_PASSES + 1], -1.0))
            o.sig(dve.memset(gate_pass[:, :, N_PASSES:N_PASSES + 1], 0.0))
            for j in range(MAX_EXTRA):
                for n, (table, out) in enumerate(((rank, at_pass), (gates, gate_pass))):
                    o.settle()
                    pick = xsel[:, 0, j:j + 1, :].to_broadcast([P, 2, NE])
                    o.sig(dve.tensor_tensor(xsel[:, 1, 0:2, :], table, pick, ALU.mult))
                    o.settle()
                    o.sig(dve.tensor_reduce(out[:, :, NE + j:NE + j + 1], xsel[:, 1, 0:2, :], AX.X, ALU.add))
                o.settle()
                o.sig(dve.tensor_scalar(at_pass[:, :, NE + j:NE + j + 1], at_pass[:, :, NE + j:NE + j + 1],
                                        -float(P), None, ALU.add))
                o.sig(dve.tensor_tensor(over[:, 2, :], xsel[:, 0, j, :], iota8[:, :], ALU.mult))
                o.settle()
                o.sig(dve.tensor_reduce(over[:, 3, 0:1], over[:, 2, :], AX.X, ALU.add))
                o.settle()
                o.sig(dve.tensor_copy(extra[0:1, 1 + j:2 + j], over[0:1, 3, 0:1]))
            o.settle()
            o.sig(dve.tensor_copy(extra[0:1, 0:1], over[0:1, 1, NE - 1:NE]), extra_ready)

            def select(i):
                at = at_pass[:, :, bass.ds(i, 1)].to_broadcast([P, 2, P])
                slots = iota[:, :].unsqueeze(1).to_broadcast([P, 2, P])
                dve.tensor_tensor(sel[:, :, :], slots, at, ALU.is_equal).then_inc(sel_own, 1)
                dve.wait_ge(sel_own, i + 1)
                g = gate_pass[:, :, bass.ds(i, 1)].to_broadcast([P, 2, P])
                dve.tensor_tensor(selg[:, :, :], sel[:, :, :], g, ALU.mult).then_inc(sel_ready, 1)

            select(0)

            def dve_pass(i):
                bank = pass_full(dve, ("selT",), i)
                dve.tensor_copy(selt[:, :], bank[:, 0:2 * P]).then_inc(free["dve"], 1)
                dve.wait_ge(sel_ready, i + 1)
                select(i + 1)
                for r in range(NR):
                    w = range_width(r)
                    bank = pass_full(dve, ("u", r), i)
                    pass_emptied(dve, ("g", r), i)
                    if r >= 2:
                        pass_full(dve, ("hT", r - 2), i)
                    dve.tensor_tensor(hs[:, r % 2, 0:w], sg[:, r % 2, 0:w], bank[:, 0:w],
                                      ALU.mult).then_inc(free["dve"], 1)
                bank = pass_full(dve, ("dn", 1), i)
                dve.tensor_copy(ye[:, 512:1024], bank[:, :]).then_inc(free["dve"], 1)
                bank = pass_full(dve, ("ga", 1), i)
                dve.tensor_copy(xe[:, 4:8, :], bank[:, :].rearrange("p (a b) -> p a b", a=4)).then_inc(free["dve"], 1)
                for j in range(4):
                    bank = pass_full(dve, ("y", j), i)
                    v = yacc[:, 2 * j:2 * j + 2, :]
                    dve.tensor_tensor(v, v, bank[:, :].rearrange("p (a b) -> p a b", a=2),
                                      ALU.add).then_inc(free["dve"], 1)

            passes(dve, dve_pass)
            dve.wait_ge(free["dve"], n_passes(dve) * EX["dve"] + BEFORE["dve"])
            for m in range(KD):
                o.sig(dve.scalar_tensor_tensor(x[:, m, seg(LAT)], yacc[:, m, :], mods[:, LAT, 5 * KD + m:5 * KD + m + 1],
                                               x[:, m, seg(LAT)], ALU.mult, ALU.add))
            o.settle()
            squares(seg(LAT))
            dve.wait_ge(final_full, 1)
            norm(banks[0], SEG, D, tile_sem=False)
            for m in range(KD):
                o.sig(dve.scalar_tensor_tensor(h[:, m, seg(LAT)], x[:, m, seg(LAT)], fing[:, m:m + 1],
                                               rstd[:, 0:SEG], ALU.mult, ALU.mult), out_ready)


def constants():
    c = {"ident": np.eye(P), "ones": np.ones((P, P)),
         "ones_blk": np.kron(np.eye(2), np.ones((64, 64)))}
    t = np.arange(P)
    mask = np.zeros((P, 2, NL, P), np.int32)
    for l, half in enumerate(LEVELS):
        same = t[:, None] // (2 * half) == t[None, :] // (2 * half)
        late = (t // half) % 2 == 1
        mask[:, FWD, l] = same & ~late[:, None] & late[None, :]
        mask[:, BWD, l] = same & late[:, None] & ~late[None, :]
    c["mask"] = mask
    ang = 2 * np.pi * np.outer(np.arange(FOUR_CH), np.arange(FOUR_CH)) / FOUR_CH
    scale = (SEG * FOUR_CH) ** -0.5
    c["dftc"] = np.concatenate([np.kron(np.eye(2), np.cos(ang)), np.kron(np.eye(2), np.sin(ang))], 1)
    ang = 2 * np.pi * (np.outer(np.arange(SEG), np.arange(SEG)) % SEG) / SEG
    tab = np.stack([np.cos(ang), -np.sin(ang)]) * scale
    c["dftt"] = tab.reshape(2, 2, P, SEG).transpose(2, 0, 1, 3)
    rows = SEG // GRID_W
    row_ids = np.repeat(np.arange(rows), GRID_W).astype(np.float64)
    col_ids = np.tile(np.arange(GRID_W), rows).astype(np.float64)
    per_axis = ROPE // 2
    inv = 10000.0 ** (-np.arange(0, per_axis, 2) / per_axis)
    ang = np.stack([row_ids[:, None] * inv, col_ids[:, None] * inv], 1)
    cos, sin = np.cos(ang), np.sin(ang)
    rope = np.zeros((P, T))
    rope[64:96, :SEG] = 1.0
    rope[64:96, SEG:] = np.stack([cos, cos], 2).reshape(SEG, ROPE).T
    rope[96:128, SEG:] = np.stack([-sin, sin], 2).reshape(SEG, ROPE).T
    c["rope"] = rope
    c["reset"] = np.tile((np.arange(T) % P != 0).astype(float), (P, 1))
    c["iota"] = np.tile(np.arange(P, dtype=float), (P, 1))
    c["before"] = np.triu(np.ones((P, P)), 1)
    c["iota8"] = np.tile(np.arange(NE, dtype=float), (P, 1))
    return {k: np.ascontiguousarray(v if v.dtype == np.int32 else v.astype(np.float32)) for k, v in c.items()}


SWAP = np.array([16 * a + 8 * (1 - s) + i for a in range(2) for s in range(2) for i in range(8)])


def lay_out(x, c, ctx, c_ctx, w_ada, b_ada, w_in, q_norm_g, kv_norm_g, w_uq, w_ukv, hgrn_norm_g,
            lb_logits, w_out, ffn_w_gate, ffn_w_up, ffn_w_down, moe_router, moe_w_gate, moe_w_up,
            moe_w_down, final_g):
    def feat(v):
        v = v.reshape(v.shape[:-1] + (-1, P))
        return np.moveaxis(v, -1, 0)

    def slabs(w, width=P):
        n_l, k, n = w.shape
        return w.reshape(n_l, k // P, P, n // width, width).transpose(0, 3, 2, 1, 4).reshape(
            n_l, n // width, P, k // P * width)

    m = constants()
    m["x"] = np.stack([ctx[0].T.reshape(KD, P, SEG).transpose(1, 0, 2),
                       x[0].T.reshape(KD, P, SEG).transpose(1, 0, 2)])
    m["cond"] = np.stack([c_ctx.reshape(KD, P).T, c[0].reshape(KD, P).T], -1)
    m["bada"] = feat(b_ada)
    m["gains"] = np.concatenate([feat(q_norm_g), feat(kv_norm_g),
                                 np.concatenate([hgrn_norm_g, hgrn_norm_g], -1).T[:, :, None]], -1)
    m["fing"] = feat(final_g)
    m["lbl"] = feat(lb_logits).transpose(0, 2, 1, 3).reshape(P, DEPTH, 8)
    m["ada"] = w_ada
    sizes = [Q_RANK, KV_RANK, ROPE, SEG, 512, 512, 512, SEG, SEG]
    at = np.cumsum([0] + sizes)
    dq, dkv, kr, fo, hq, hff, hfb, hi, hg = [w_in[:, :, at[i]:at[i + 1]] for i in range(9)]
    win = np.zeros((DEPTH, len(WIN), P, SLAB), np.float32)
    win[:, 0:4], win[:, 4:8] = slabs(hff), slabs(hfb)
    win[:, 8:10] = slabs(hi, 2 * P)[:, 0].reshape(DEPTH, P, 2, SLAB).transpose(0, 2, 1, 3)
    win[:, 10:14], win[:, 14:16] = slabs(hq), slabs(hg)
    win[:, 16:18], win[:, 18:19] = slabs(dq), slabs(dkv)
    win[:, 19:20, :, 0:512] = slabs(np.concatenate([kr, kr[:, :, SWAP]], -1), 64)
    win[:, 20:22] = slabs(fo)
    uq = w_uq.reshape(DEPTH, 2, P, HEADS, QK)
    uq = np.concatenate([uq, uq[..., NOPE:][..., SWAP]], -1)
    win[:, 22:24] = uq.reshape(DEPTH, 2, P, HEADS * P)
    ukv = w_ukv.reshape(DEPTH, P, HEADS, NOPE + DV)
    win[:, 24] = np.concatenate([ukv[..., :NOPE].reshape(DEPTH, P, -1), ukv[..., NOPE:].reshape(DEPTH, P, -1)], -1)
    m["win"] = win
    m["wo"] = slabs(w_out)

    def ffn(g, u, d):
        n = g.shape[0]
        out = np.zeros((n, N_FFN_SLABS, P, SLAB), np.float32)
        out[:, 0:2 * KF:2], out[:, 1:2 * KF:2] = slabs(g), slabs(u)
        dn = slabs(d)
        for i in range(3):
            part = dn[:, :, :, i * SLAB:(i + 1) * SLAB]
            out[:, 2 * KF + i::3, :, :part.shape[-1]] = part
        return out

    m["ffn"] = ffn(ffn_w_gate, ffn_w_up, ffn_w_down)[0]
    moe = np.zeros((NE, N_PS, P, SLAB), np.float32)
    j = 0
    for r in range(NR):
        w = range_width(r)
        n = KD * w // SLAB
        for mat in (moe_w_gate[0], moe_w_up[0]):
            part = mat[:, :, 512 * r:512 * r + w].reshape(NE, n, SLAB // w, P, w)
            moe[:, j:j + n] = part.transpose(0, 1, 3, 2, 4).reshape(NE, n, P, SLAB)
            j += n
    moe[:, j:] = moe_w_down[0].reshape(NE, KF, P, D)
    m["moe"] = moe
    m["router"] = moe_router[0].reshape(KD, P, NE).transpose(1, 0, 2)
    return {k: np.ascontiguousarray(v) for k, v in m.items()}


def kernel(**inputs):
    import concourse.bacc as bacc
    from concourse.bass_utils import run_bass_kernel_spmd

    arrays = lay_out(**{k: np.asarray(v) for k, v in inputs.items()})
    nc = bacc.Bacc("TRN2", target_bir_lowering=False, num_devices=1)
    ops = {k: nc.dram_tensor(f"in_{k}", v.shape, mybir.dt.from_np(v.dtype), kind="ExternalInput").ap()
           for k, v in arrays.items()}
    ops["out"] = nc.dram_tensor("out_x", (P, KD, SEG), F32, kind="ExternalOutput").ap()
    build(nc, ops)
    r = run_bass_kernel_spmd(nc, [{f"in_{k}": v for k, v in arrays.items()}], core_ids=[0])
    got = np.asarray(r.results[0]["out_x"])
    return np.ascontiguousarray(got.transpose(2, 1, 0).reshape(1, SEG, D))
```

```python
from contextlib import ExitStack

import numpy as np

import concourse.bass as bass
from concourse import mybir

F32 = mybir.dt.float32
F32R = mybir.dt.float32r
I32 = mybir.dt.int32
U8 = mybir.dt.uint8
U32 = mybir.dt.uint32
ALU = mybir.AluOpType
ACT = mybir.ActivationFunctionType
AX = mybir.AxisListType

P = 128
D = 1024
KD = D // P
SEG = 256
T = 2 * SEG
NBLK = T // P
DEPTH = 2
EPS = 1e-6
GRID_W = 64

HEADS = 8
NOPE, ROPE, DV = 64, 32, 64
QK = NOPE + ROPE
Q_RANK, KV_RANK = 256, 128
ATT_SCALE = float(QK) ** -0.5

FOUR_CH = 64
RH = 4
RV = 64
LEVELS = [64, 32, 16, 8, 4, 2, 1]
NL = len(LEVELS)

D_FF = 2816
KF = D_FF // P
NE = 8
REGION = 16960
EX_F32 = 8480

SLOTS = 11
SLAB = 1024
N_FFN_SLABS = 2 * KF + 3 * KD
BANKS = 6
EX_BANKS = 8
FWD, BWD = 0, 1
CTX, LAT = 0, 1
N_ADA = 6 * D // P
N_ADA_TILES = 6

WIN = ([("ff", i) for i in range(8)] + [("hi", 0), ("hi", 1)] + [("hq", i) for i in range(4)]
       + [("hg", i) for i in range(2)] + [("dq", i) for i in range(2)] + [("dkv", 0), ("kr", 0)]
       + [("fo", i) for i in range(2)] + [("uq", 0), ("uq", 1), ("ukv", 0)])


def query_blocks(layer):
    return [0, 1, 2, 3] if layer == 0 else [2, 3]


def query_segments(layer):
    return [CTX, LAT] if layer == 0 else [LAT]


def state_steps(layer):
    fwd = [(FWD, b) for b in (0, 1, 2)]
    bwd = [(BWD, b) for b in (1, 0, 3)]
    return [s for pair in zip(fwd, bwd) for s in pair]


def incoming(direction, block):
    if direction == FWD:
        return block - 1 if block > 0 else None
    return {1: None, 0: 1, 3: 0, 2: 3}[block]


def attention_units(layer):
    return [(h, s) for s in query_segments(layer) for h in range(HEADS)]


def key_blocks(seg):
    return [0, 1] if seg == CTX else [0, 1, 2, 3]


class Tiles:

    def __init__(self):
        self.number, self.consumer, self.rank = {}, [], []
        self.count = {"act": 0, "dve": 0}

    def add(self, name, consumer):
        self.number[name] = len(self.consumer)
        self.consumer.append(consumer)
        self.count[consumer] += 1
        self.rank.append(self.count[consumer])


def plan_tiles():
    t = Tiles()
    for L in range(DEPTH):
        t.add(("ss1", L), "dve")
        for i in range(8):
            t.add(("ff", L, i), "act")
        for b in range(NBLK):
            t.add(("hi", L, b), "dve")
        for i in range(4):
            t.add(("hq", L, i), "act")
        for i in range(2):
            t.add(("hg", L, i), "act")
        for d, b in state_steps(L):
            t.add(("kT", L, d, b), "act")
            t.add(("st", L, d, b), "dve")
        for b in query_blocks(L):
            t.add(("diag", L, b), "dve")
            for d in (FWD, BWD):
                for l in range(NL):
                    t.add(("lv", L, b, d, l), "dve")
                if incoming(d, b) is not None:
                    t.add(("in", L, b, d), "dve")
            t.add(("o", L, b), "dve")
        for i in range(2):
            t.add(("rms", L, i), "dve")
        for i in range(2):
            t.add(("dq", L, i), "dve")
        t.add(("dkv", L), "dve")
        t.add(("kr", L), "dve")
        for i in range(2):
            t.add(("fo", L, i), "act")
        for b in query_blocks(L):
            t.add(("f1", L, b), "act")
        for s in query_segments(L):
            for c in range(2):
                t.add(("f2", L, s, c), "dve")
        t.add(("ssq", L), "dve")
        t.add(("sskv", L), "dve")
        for h in range(HEADS):
            t.add(("q", L, h), "dve")
        for j in range(HEADS // 2):
            t.add(("kn", L, j), "act")
        for b in range(NBLK):
            t.add(("v", L, b), "act")
        units = attention_units(L)
        for i in range(len(units) + 2):
            if i < len(units):
                for qb in range(2):
                    t.add(("s", L, i, qb), "act")
            if 1 <= i <= len(units):
                for kb2 in range(len(key_blocks(units[i - 1][1])) // 2):
                    t.add(("pT", L, i - 1, kb2), "dve")
            if i >= 2:
                t.add(("pv", L, i - 2), "dve")
        for m in range(KD):
            t.add(("wo", L, m), "dve")
        t.add(("ss2", L), "dve")
        if L == 0:
            for k in range(KF):
                t.add(("g", k), "act")
                t.add(("u", k), "dve")
            for m in range(KD):
                t.add(("dn", m), "dve")
        else:
            t.add(("rt",), "dve")
            for j in range(4):
                t.add(("ht", j), "act")
            t.add(("rank",), "dve")
            for j in range(2):
                t.add(("ga0", j), "dve")
    return t


TL = plan_tiles()
NR = 6


def range_width(r):
    return 512 if r < NR - 1 else D_FF - 512 * (NR - 1)


EXPERT_TILES = [(("selT",), "dve")]
for _r in range(NR + 1):
    if _r < NR:
        EXPERT_TILES += [(("g", _r), "act"), (("u", _r), "dve")]
    if _r:
        EXPERT_TILES += [(("hT", _r - 1), "dve")]
EXPERT_TILES += [(("dn", 0), "act"), (("dn", 1), "dve"), (("ga", 0), "dve"), (("ga", 1), "dve")]
EXPERT_TILES += [(("y", j), "dve") for j in range(4)]
N_EX = len(EXPERT_TILES)
EX_AT = {name: i for i, (name, _) in enumerate(EXPERT_TILES)}
EX = {c: sum(q == c for _, q in EXPERT_TILES) for c in ("act", "dve")}
N_BEFORE = len(TL.consumer)
BEFORE = TL.count


def rank_in(consumer, upto):
    return sum(c == consumer for _, c in EXPERT_TILES[:upto + 1])


def plan_pass_slabs():
    out = []
    for r in range(NR):
        for m in "gu":
            out += [(m, r, i) for i in range(KD * range_width(r) // SLAB)]
    return out + [("dn", k) for k in range(KF)]


PASS_SLABS = plan_pass_slabs()
N_PS = len(PASS_SLABS)
assert N_PS % SLOTS == 0


def closes(slab):
    if slab[0] == "dn":
        return ("dn", 1) if slab[1] == KF - 1 else None
    m, r, i = slab
    return (m, r) if i == KD * range_width(r) // SLAB - 1 else None


OWN_PER_PASS = sum(closes(q) is None for q in PASS_SLABS)
PARTS = 6
assert N_PS % PARTS == 0
PARTS_HI = NR + 2
MAX_EXTRA = 3
N_PASSES = NE + MAX_EXTRA


def plan_slabs():
    order = [("ada", 0, k, n) for k in range(KD) for n in range(2)]
    for L in range(DEPTH):
        order += [("win", L, j) for j in range(16)]
        if L == 0:
            order += [("ada", t, k, n) for t in range(1, N_ADA_TILES) for k in range(KD) for n in range(2)]
        order += [("win", L, j) for j in range(16, len(WIN))]
        order += [("wo", L, m) for m in range(KD)]
        if L == 0:
            order += [("ffn", j) for j in range(N_FFN_SLABS)]
    return {name: i for i, name in enumerate(order)}


SL = plan_slabs()
MOE_SLAB0 = len(SL)
OWN_BEFORE = N_ADA_TILES * (2 * KD - 1)


def slab_tile(name):
    if name[0] == "ada":
        return None
    if name[0] == "win":
        _, L, j = name
        kind, i = WIN[j]
        if kind == "hi":
            return ("hi", L, NBLK - 1)
        if kind == "uq":
            return ("q", L, HEADS - 1)
        if kind == "ukv":
            return ("v", L, NBLK - 1)
        return (kind, L) if kind in ("dkv", "kr") else (kind, L, i)
    if name[0] == "wo":
        return name
    return ffn_tile(name[1])


def ffn_tile(j):
    if j < 2 * KF:
        return ("gu"[j % 2], j // 2)
    return ("dn", (j - 2 * KF) // 3)


def build(nc, a):
    ctx = ExitStack()
    with ctx:
        def sb(name, shape, dt=F32):
            return ctx.enter_context(nc.sbuf_tensor(name, shape, dt))

        def sem(name):
            return ctx.enter_context(nc.semaphore(name))

        x = sb("x", [P, KD, T])
        h_at = nc.sbuf_base
        h = sb("h", [P, KD, T])
        mix = sb("mix", [P, KD, T])
        spare = sb("spare", [P, PARTS * 2 * SLAB - 2 * KD * T])
        ring = sb("ring", [P, SLOTS, SLAB])
        ident = sb("ident", [P, P])
        ones = sb("ones", [P, P])
        ones_blk = sb("ones_blk", [P, P])
        mask = sb("mask", [P, 2, NL, P], I32)
        dftc = sb("dftc", [P, 2 * P])
        dftt = sb("dftt", [P, 2, 2, SEG])
        rope_t = sb("rope_t", [P, T])
        reset = sb("reset", [P, T])
        cond = sb("cond", [P, KD, 32])
        craw = sb("craw", [P, KD, 2])
        bada = sb("bada", [P, DEPTH, N_ADA])
        gains = sb("gains", [P, DEPTH, 4])
        fing = sb("fing", [P, KD])
        iota8 = sb("iota8", [P, NE])
        iota = sb("iota", [P, P])
        before = sb("before", [P, P])
        extra = sb("extra", [1, 1 + MAX_EXTRA], I32)
        lbl = sb("lbl", [P, DEPTH, 8])
        lb = sb("lb", [P, 2, DEPTH, 8])
        lbt = sb("lbt", [P, 4, DEPTH, 8])
        mods = sb("mods", [P, DEPTH, 2, N_ADA])
        ada_sb = sb("ada_sb", [P, 512])
        router = sb("router", [P, KD, NE])
        rstd = sb("rstd", [P, T])
        msq = sb("msq", [P, T])
        smax = sb("smax", [P, 4, 2 * HEADS * 2])
        region_at = nc.sbuf_base
        region = sb("region", [P, REGION])

        def over(name, shape, offset):
            return nc.alloc_sbuf_tensor_at(name, shape, F32R, offset=offset)

        w_hi = over("w_hi", [P, PARTS, SLAB], h_at)
        w_lo = over("w_lo", [P, PARTS, SLAB], h_at + 4 * PARTS * SLAB)
        at = region_at + 4 * EX_F32
        xe_hi, xe_lo = over("xe_hi", [P, KD, P], at), over("xe_lo", [P, KD, P], at + 4 * D)
        hT_hi = over("hT_hi", [P, KF, P], at + 8 * D)
        hT_lo = over("hT_lo", [P, KF, P], at + 8 * D + 4 * D_FF)
        assert EX_F32 + 2 * D + 2 * D_FF <= REGION

        def carve(shapes):
            out, at = [], 0
            for s in shapes:
                n = int(np.prod(s))
                v = region[:, at:at + n]
                at += n
                if len(s) == 2:
                    v = v.rearrange("p (a b) -> p a b", a=s[0])
                elif len(s) == 3:
                    v = v.rearrange("p (a b c) -> p a b c", a=s[0], b=s[1])
                out.append(v)
            assert at <= REGION, at
            return out

        hi, hg, kf, kb, gf, gb, lev, st, kd, sc, tot = carve([
            [NBLK, RH * RV], [2, T], [RH, T], [RH, T], [RH, T], [RH, T],
            [NL + 1, RH * P], [6, RH * RV], [RH * P], [RH * P], [4, RH, NBLK]])
        rq = mix[:, 0:4, :]
        kkf, kkb = lev[:, 0:4, :], lev[:, 4:8, :]
        kt = [msq, rstd]
        osq = kf[:, 0:2, :]
        k_of, g_of = (kf, kb), (gf, gb)
        levs = [spare[:, :].rearrange("p (a b) -> p a b", a=NL + 1), lev]
        dq, dkv, kall, qall, vtok, pt, prob = carve([
            [2, T], [T], [HEADS, T], [HEADS, T], [NBLK, HEADS * DV], [2, 4 * SEG], [4, T]])
        fo = region[:, 11776:11776 + 2 * T].rearrange("p (a b) -> p a b", a=2)
        f1 = prob
        lsq = vtok[:, 0:3, :]
        rt1, rt2 = prob[:, 0, :], prob[:, 1, :]
        (hid0,) = carve([[KF, T]])
        (ht, sel, selg, selt, sg, hs, ye, yacc, gates, lg, mx8, ix8, ixf, gt, one_hot,
         rank, cnt, over, at_pass, gate_pass, xsel) = carve([
            [2, D], [2, P], [2, P], [2 * P], [2, 512], [2, 512], [D], [KD, SEG],
            [2, NE], [2, NE], [2, 8], [2, 8], [2, 8], [4, 2, NE], [2, NE],
            [2, NE], [NE], [4, NE], [2, N_PASSES + 1], [2, N_PASSES + 1], [2, 3, NE]])
        assert int(np.prod(ht.shape[1:])) and 2 * D + 4 * P + 2 * P + 2048 + D + KD * SEG + 400 <= EX_F32
        ix8 = ix8.bitcast(U32)

        banks = [ctx.enter_context(nc.psum_tensor(f"bank{i}", [P, 512], F32)) for i in range(EX_BANKS)]
        ada_bank, adaT_bank = banks[7], banks[6]

        slab_full = [sem(f"slab_full{i}") for i in range(SLOTS)]
        slab_used = sem("slab_used")
        tile_full = sem("tile_full")
        free = {"act": sem("tile_emptied_act"), "dve": sem("tile_emptied_dve")}
        const_in = sem("const_in")
        dve_own = sem("dve_own")
        act_own = sem("act_own")
        cond_zero = sem("cond_zero")
        cond_ready = sem("cond_ready")
        lb_in = sem("lb_in")
        lb_exp = sem("lb_exp")
        sq_ready = sem("sq_ready")
        xn_ready = sem("xn_ready")
        h_ready = sem("h_ready")
        mods_ready = sem("mods_ready")
        ada_full = sem("ada_full")
        ada_taken = sem("ada_taken")
        adaT_full = sem("adaT_full")
        adaT_taken = sem("adaT_taken")
        var_ready = sem("var_ready")
        sel_own = sem("sel_own")
        sd_ready = sem("sd_ready")
        f_ready = sem("f_ready")
        g_ready = sem("g_ready")
        kk_in = sem("kk_in")
        kk_exp = sem("kk_exp")
        kk_ready = sem("kk_ready")
        lev_in = sem("lev_in")
        lev_exp = sem("lev_exp")
        lev_ready = sem("lev_ready")
        kd_ready = sem("kd_ready")
        rec_ready = sem("rec_ready")
        neg_max = sem("neg_max")
        exp_ready = sem("exp_ready")
        prob_ready = sem("prob_ready")
        k_ready = sem("k_ready")
        sel_ready = sem("sel_ready")
        gather_done = sem("gather_done")
        extra_ready = sem("extra_ready")
        final_full = sem("final_full")
        hi_made = sem("hi_made")
        lo_made = sem("lo_made")
        part_hi = sem("part_hi")
        top_in = sem("top_in")
        top_exp = sem("top_exp")
        gates_ready = sem("gates_ready")
        out_ready = sem("out_ready")
        out_done = sem("out_done")
        block = ctx.enter_context(nc.Block())

        class Own:

            def __init__(self, eng, own):
                self.eng, self.own, self.counts, self.last, self.base = eng, own, {}, None, None

            def sig(self, ins, s=None):
                s = self.own if s is None else s
                ins.then_inc(s, 1)
                key = str(s)
                self.counts[key] = self.counts.get(key, 0) + 1
                self.last = (s, key)

            def settle(self):
                s, key = self.last
                n = self.counts[key]
                if self.base is not None:
                    e, per = self.base
                    n = e * per[key] + n
                self.eng.wait_ge(s, n)

        def full(eng, name):
            n = TL.number[name]
            eng.wait_ge(tile_full, n + 1)
            return banks[n % BANKS]

        def emptied(eng, name):
            n = TL.number[name]
            eng.wait_ge(free[TL.consumer[n]], TL.rank[n])

        def pass_full(eng, name, i):
            eng.wait_ge(tile_full, i * N_EX + (N_BEFORE + EX_AT[name] + 1))
            return banks[EX_AT[name] % EX_BANKS]

        def pass_emptied(eng, name, i):
            c = EXPERT_TILES[EX_AT[name]][1]
            eng.wait_ge(free[c], i * EX[c] + (BEFORE[c] + rank_in(c, EX_AT[name])))

        def pass_used(eng, j, i):
            tile = closes(PASS_SLABS[j])
            if tile is None:
                own = sum(closes(q) is None for q in PASS_SLABS[:j + 1])
                eng.wait_ge(slab_used, i * OWN_PER_PASS + (OWN_BEFORE + own))
            else:
                eng.wait_ge(tile_full, i * N_EX + (N_BEFORE + EX_AT[tile] + 1))

        def passes(eng, body):
            with eng.Fori(0, NE) as i:
                body(i)
            extra_passes(eng, body)

        def extra_passes(eng, body):
            eng.wait_ge(extra_ready, 1)
            n_extra = eng.value_load(extra[0:1, 0:1], min_val=0, max_val=MAX_EXTRA)
            with eng.Fori(0, MAX_EXTRA) as j:
                with eng.If(n_extra > j):
                    body(j + NE)

        def n_passes(eng):
            return eng.value_load(extra[0:1, 0:1], min_val=0, max_val=MAX_EXTRA) + NE

        def seg(s):
            return slice(s * SEG, (s + 1) * SEG)

        def lowc(v):
            return v.rearrange("p (a b) -> p a b", a=RH)

        N_CONST = 19

        @block.sync
        def _(sp):
            consts = [(craw, a["cond"]), (gains, a["gains"]), (bada, a["bada"]), (lbl, a["lbl"]),
                      (ident, a["ident"]), (ones, a["ones"]), (ones_blk, a["ones_blk"]),
                      (mask, a["mask"]), (dftc, a["dftc"]), (dftt, a["dftt"]), (rope_t, a["rope"]),
                      (reset, a["reset"]), (router, a["router"]), (fing, a["fing"]), (iota8, a["iota8"]),
                      (iota, a["iota"]), (before, a["before"])]
            assert len(consts) + 2 == N_CONST
            for dst, src in consts:
                sp.dma_start(dst[:], src).then_inc(const_in, 16)
            for s in range(2):
                sp.dma_start(x[:, :, seg(s)], a["x"][s]).then_inc(const_in, 16)

            names = list(SL)
            own_used = 0
            used_at = []
            for name in names:
                if slab_tile(name) is not None:
                    used_at.append((tile_full, TL.number[slab_tile(name)] + 1))
                elif name[2:] == (KD - 1, 1):
                    used_at.append((ada_full, name[1] + 1))
                else:
                    own_used += 1
                    used_at.append((slab_used, own_used))

            def load(n, src):
                sp.dma_start(ring[:, n % SLOTS, 0:src.shape[-1]], src).then_inc(slab_full[n % SLOTS], 16)

            for n, name in enumerate(names):
                if n >= SLOTS:
                    sp.wait_ge(*used_at[n - SLOTS])
                if name[0] == "ada":
                    _, t, k, j = name
                    c0 = (t % 3) * 2 * SLAB + j * SLAB
                    load(n, a["ada"][t // 3, k * P:(k + 1) * P, c0:c0 + SLAB])
                elif name[0] == "win":
                    load(n, a["win"][name[1], name[2]])
                elif name[0] == "wo":
                    load(n, a["wo"][name[1], name[2]])
                else:
                    load(n, a["ffn"][name[1]])
            def pass_load(j, expert):
                load(MOE_SLAB0 + j, a["moe"][bass.ds(expert, 1), j].rearrange("e p n -> (e p) n")
                     if not isinstance(expert, int) else a["moe"][expert, j])

            def head(i, expert, before_loop=False):
                for j in range(SLOTS):
                    if before_loop:
                        sp.wait_ge(*used_at[MOE_SLAB0 + j - SLOTS])
                    else:
                        sp.wait_ge(lo_made, i * N_PS + (j - SLOTS + 1))
                    pass_load(j, expert)

            def rest(i, expert):
                for j in range(SLOTS, N_PS):
                    sp.wait_ge(lo_made, i * N_PS + (j - SLOTS + 1))
                    pass_load(j, expert)

            head(0, 0, before_loop=True)
            with sp.Fori(0, NE - 1) as i:
                rest(i, i)
                head(i + 1, i + 1)
            rest(NE - 1, NE - 1)

            def again(i):
                expert = sp.value_load(extra[0:1, bass.ds(i - (NE - 1), 1)], min_val=0, max_val=NE - 1)
                head(i, expert)
                rest(i, expert)

            extra_passes(sp, again)
            for i in range(2):
                sp.wait_ge(out_ready, 4 * (i + 1))
                sp.dma_start(a["out"][:, i * 4:(i + 1) * 4, :], h[:, i * 4:(i + 1) * 4, seg(LAT)]).then_inc(out_done, 16)
            sp.wait_ge(out_done, 32)

        @block.gpsimd
        def _(pool):
            pool.memset(cond[:, :, :], 0.0).then_inc(cond_zero, 1)

        @block.tensor
        def _(pe):
            def open_tile(name):
                n = TL.number[name]
                if n >= BANKS:
                    pe.wait_ge(free[TL.consumer[n - BANKS]], TL.rank[n - BANKS])
                return banks[n % BANKS]

            def slab_in(name):
                n = SL[name]
                pe.wait_ge(slab_full[n % SLOTS], 16 * (n // SLOTS + 1))
                return ring[:, n % SLOTS, :]

            def close(m):
                m.then_inc(tile_full, 1)

            def project(name, slab, rhs, cols, w=P, at=0, ready=None):
                bank = open_tile(name)
                s = slab_in(slab)
                for k in range(KD):
                    if ready is not None:
                        pe.wait_ge(h_ready, ready + k + 1)
                    m = pe.matmul(bank[at:at + w, 0:cols], s[:, k * w:(k + 1) * w], rhs(k),
                                  start=(k == 0), stop=(k == KD - 1))
                close(m)

            def norm_sum(name, chunks, rhs, cols, sem_, base, stat):
                bank = open_tile(name)
                for k in range(chunks):
                    if sem_ is not None:
                        pe.wait_ge(sem_, base + k + 1)
                    m = pe.matmul(bank[:, 0:cols], stat[:, :], rhs(k), start=(k == 0), stop=(k == chunks - 1))
                close(m)

            def modulation_half(t, half):
                if half == 0 and t:
                    pe.wait_ge(ada_taken, t)
                for k in range(4 * half, 4 * half + 4):
                    for n in range(2):
                        s = slab_in(("ada", t, k, n))
                        for j in range(2):
                            c0 = 32 * (2 * n + j)
                            m = pe.matmul(ada_bank[c0:c0 + 32, :], cond[:, k, :], s[:, j * 512:(j + 1) * 512],
                                          start=(k == 0), stop=(k == KD - 1), tile_position=(0, c0))
                        m.then_inc(ada_full if (k, n) == (KD - 1, 1) else slab_used, 1)

            def modulation_turn(t):
                pe.wait_ge(ada_taken, t + 1)
                if t:
                    pe.wait_ge(adaT_taken, t)
                for c in range(4):
                    m = pe.transpose(adaT_bank[:, c * P:(c + 1) * P], ada_sb[:, c * P:(c + 1) * P], ident[:, :])
                m.then_inc(adaT_full, 1)

            def fill(f):
                if f % 2 == 0 and f >= 2:
                    modulation_turn(f // 2)
                if f < 2 * (N_ADA_TILES - 1):
                    modulation_half(1 + f // 2, f % 2)

            n_kd = n_lev = 0
            pe.wait_ge(const_in, 16 * N_CONST)
            pe.wait_ge(cond_ready, 1)
            for L in range(DEPTH):
                q0 = 0 if L == 0 else SEG
                nq = T - q0
                if L == 0:
                    modulation_half(0, 0)
                    modulation_half(0, 1)
                    modulation_turn(0)

                norm_sum(("ss1", L), KD, lambda k: h[:, k, :], T, sq_ready, 16 * L, ones)
                for i in range(8):
                    project(("ff", L, i), ("win", L, i), lambda k: h[:, k, :], T,
                            ready=2 * KD * L if i == 0 else None)
                s0, s1 = slab_in(("win", L, 8)), slab_in(("win", L, 9))
                for b in range(NBLK):
                    bank = open_tile(("hi", L, b))
                    for k in range(KD):
                        s = (s0, s1)[k // 4]
                        m = pe.matmul(bank[:, 0:SEG], h[:, k, b * P:(b + 1) * P],
                                      s[:, (k % 4) * SEG:(k % 4 + 1) * SEG], start=(k == 0), stop=(k == KD - 1))
                    close(m)
                for i in range(4):
                    project(("hq", L, i), ("win", L, 10 + i), lambda k: h[:, k, q0:T], nq)
                for i in range(2):
                    project(("hg", L, i), ("win", L, 14 + i), lambda k: h[:, k, q0:T], nq)

                pe.wait_ge(kk_ready, 2 * L + 2)
                for i, (d, b) in enumerate(state_steps(L)):
                    bank = open_tile(("kT", L, d, b))
                    kk = (kkf, kkb)[d]
                    for hh in range(RH):
                        m = pe.transpose(bank[:, hh * P:(hh + 1) * P], kk[:, hh, b * P:(b + 1) * P], ident[:, :])
                    close(m)
                    bank = open_tile(("st", L, d, b))
                    emptied(pe, ("kT", L, d, b))
                    for hh in range(RH):
                        m = pe.matmul(bank[:, hh * RV:(hh + 1) * RV], kt[i % 2][:, hh * P:(hh + 1) * P],
                                      hi[:, b, hh * RV:(hh + 1) * RV], start=True, stop=True)
                    close(m)
                    if L == 0 and i in (2, 5):
                        fill(i // 3)

                for b in query_blocks(L):
                    bank = open_tile(("diag", L, b))
                    n_kd += 1
                    pe.wait_ge(kd_ready, n_kd)
                    for hh in range(RH):
                        m = pe.matmul(bank[:, hh * P:(hh + 1) * P], kd[:, hh * P:(hh + 1) * P],
                                      rq[:, hh, b * P:(b + 1) * P], start=True, stop=True)
                    close(m)
                    for d in (FWD, BWD):
                        n_lev += 1
                        pe.wait_ge(lev_ready, n_lev)
                        unit = 2 * query_blocks(L).index(b) + d
                        buf = levs[unit % 2]
                        for l in range(NL):
                            bank = open_tile(("lv", L, b, d, l))
                            for hh in range(RH):
                                v = buf[:, l, hh * P:(hh + 1) * P]
                                m = pe.matmul(bank[:, hh * P:(hh + 1) * P], v, v, start=True, stop=True)
                            close(m)
                        if incoming(d, b) is not None:
                            i = state_steps(L).index((d, incoming(d, b)))
                            bank = open_tile(("in", L, b, d))
                            for hh in range(RH):
                                r0 = (hh % 2) * RV
                                m = pe.matmul(bank[r0:r0 + RV, (hh // 2) * P:(hh // 2 + 1) * P],
                                              st[:, i, hh * RV:(hh + 1) * RV], buf[:, NL, hh * P:(hh + 1) * P],
                                              start=True, stop=True)
                            close(m)
                        if L == 0:
                            fill(2 + unit)
                    bank = open_tile(("o", L, b))
                    emptied(pe, ("lv", L, b, BWD, NL - 1))
                    for hh in range(RH):
                        r0 = (hh % 2) * RV
                        m = pe.matmul(bank[r0:r0 + RV, (hh // 2) * P:(hh // 2 + 1) * P],
                                      hi[:, b, hh * RV:(hh + 1) * RV], sc[:, hh * P:(hh + 1) * P],
                                      start=True, stop=True)
                    close(m)
                if L == 0:
                    fill(2 * (N_ADA_TILES - 1))
                for i in range(2):
                    norm_sum(("rms", L, i), 1, lambda k: osq[:, i, q0:T], nq, rec_ready, 4 * L + i, ones_blk)

                for i in range(2):
                    project(("dq", L, i), ("win", L, 16 + i), lambda k: h[:, k, q0:T], nq)
                project(("dkv", L), ("win", L, 18), lambda k: h[:, k, :], T)
                project(("kr", L), ("win", L, 19), lambda k: h[:, k, :], T, w=64, at=64)
                for i in range(2):
                    project(("fo", L, i), ("win", L, 20 + i), lambda k: h[:, k, q0:T], nq)
                for b in query_blocks(L):
                    bank = open_tile(("f1", L, b))
                    emptied(pe, ("fo", L, 1))
                    for c in range(2):
                        m = pe.matmul(bank[:, c * SEG:(c + 1) * SEG], fo[:, c, b * P:(b + 1) * P], dftc[:, :],
                                      start=True, stop=True)
                    close(m)
                for s in query_segments(L):
                    for c in range(2):
                        bank = open_tile(("f2", L, s, c))
                        emptied(pe, ("f1", L, 2 * s + 1))
                        for t in range(2):
                            for part in range(2):
                                m = pe.matmul(bank[:, 0:SEG],
                                              f1[:, 2 * s + t, c * SEG + part * P:c * SEG + (part + 1) * P],
                                              dftt[:, part, t, :], start=(t == 0 and part == 0),
                                              stop=(t == 1 and part == 1))
                        close(m)
                pe.wait_ge(k_ready, 6 * L + 3)
                norm_sum(("ssq", L), 2, lambda k: lsq[:, k, q0:T], nq, None, 0, ones)
                norm_sum(("sskv", L), 1, lambda k: lsq[:, 2, :], T, None, 0, ones)
                pe.wait_ge(k_ready, 6 * L + 6)
                wuq = [slab_in(("win", L, 22)), slab_in(("win", L, 23))]
                for hh in range(HEADS):
                    bank = open_tile(("q", L, hh))
                    for k in range(2):
                        m = pe.matmul(bank[:, 0:nq], wuq[k][:, hh * P:(hh + 1) * P], dq[:, k, q0:T],
                                      start=(k == 0), stop=(k == 1))
                    close(m)
                wukv = slab_in(("win", L, 24))
                for j in range(HEADS // 2):
                    bank = open_tile(("kn", L, j))
                    m = pe.matmul(bank[:, :], wukv[:, j * P:(j + 1) * P], dkv[:, :], start=True, stop=True)
                    close(m)
                for b in range(NBLK):
                    bank = open_tile(("v", L, b))
                    m = pe.matmul(bank[:, :], dkv[:, b * P:(b + 1) * P], wukv[:, 512:1024], start=True, stop=True)
                    close(m)
                units = attention_units(L)
                n_prob0 = 0 if L == 0 else 2 * len(attention_units(0))
                emptied(pe, ("q", L, HEADS - 1))
                emptied(pe, ("v", L, NBLK - 1))
                for i in range(len(units) + 2):
                    if i < len(units):
                        hh, s = units[i]
                        for qb in range(2):
                            bank = open_tile(("s", L, i, qb))
                            c0 = s * SEG + qb * P
                            m = pe.matmul(bank[:, 0:P * len(key_blocks(s))], qall[0:QK, hh, c0:c0 + P],
                                          kall[0:QK, hh, 0:P * len(key_blocks(s))], start=True, stop=True)
                            close(m)
                    if 1 <= i <= len(units):
                        u = i - 1
                        pe.wait_ge(prob_ready, n_prob0 + 2 * (u + 1))
                        for k2 in range(len(key_blocks(units[u][1])) // 2):
                            bank = open_tile(("pT", L, u, k2))
                            for kk in range(2):
                                for qb in range(2):
                                    k0 = (2 * k2 + kk) * P
                                    m = pe.transpose(bank[:, kk * SEG + qb * P:kk * SEG + (qb + 1) * P],
                                                     prob[:, 2 * (u % 2) + qb, k0:k0 + P], ident[:, :])
                            close(m)
                    if i >= 2:
                        u = i - 2
                        hh, s = units[u]
                        kbs = key_blocks(s)
                        bank = open_tile(("pv", L, u))
                        emptied(pe, ("pT", L, u, len(kbs) // 2 - 1))
                        r0 = (hh % 2) * DV
                        for kb_ in kbs:
                            m = pe.matmul(bank[r0:r0 + DV, 0:SEG], vtok[:, kb_, hh * DV:(hh + 1) * DV],
                                          pt[:, u % 2, kb_ * SEG:(kb_ + 1) * SEG],
                                          start=(kb_ == 0), stop=(kb_ == kbs[-1]))
                        close(m)
                emptied(pe, ("pv", L, len(units) - 1))
                for m_ in range(KD):
                    project(("wo", L, m_), ("wo", L, m_), lambda k: mix[:, k, q0:T], nq)
                norm_sum(("ss2", L), KD, lambda k: h[:, k, q0:T], nq, sq_ready, 16 * L + 8, ones)
                if L == 0:
                    for k_ in range(KF):
                        project(("g", k_), ("ffn", 2 * k_), lambda k: h[:, k, :], T,
                                ready=KD if k_ == 0 else None)
                        project(("u", k_), ("ffn", 2 * k_ + 1), lambda k: h[:, k, :], T)
                    for m_ in range(KD):
                        bank = open_tile(("dn", m_))
                        for k in range(KF):
                            if k % 8 == 0:
                                s = slab_in(("ffn", 2 * KF + 3 * m_ + k // 8))
                            if m_ == 0:
                                emptied(pe, ("u", k))
                            m = pe.matmul(bank[:, :], s[:, (k % 8) * P:(k % 8 + 1) * P], hid0[:, k, :],
                                          start=(k == 0), stop=(k == KF - 1))
                        close(m)

            bank = open_tile(("rt",))
            pe.wait_ge(h_ready, KD * 2 * DEPTH)
            for b in range(2):
                for k in range(KD):
                    m = pe.matmul(bank[:, b * NE:(b + 1) * NE], h[:, k, SEG + b * P:SEG + (b + 1) * P],
                                  router[:, k, :], start=(k == 0), stop=(k == KD - 1))
            close(m)
            for j in range(4):
                bank = open_tile(("ht", j))
                for c in range(4):
                    b, k = divmod(4 * j + c, KD)
                    m = pe.transpose(bank[:, c * P:(c + 1) * P], h[:, k, SEG + b * P:SEG + (b + 1) * P], ident[:, :])
                close(m)
            pe.wait_ge(gates_ready, 1)
            bank = open_tile(("rank",))
            for c, parts in enumerate((((before, 0),), ((ones, 0), (before, 1)), ((ones, 0), (ones, 1)))):
                for n, (w, b) in enumerate(parts):
                    m = pe.matmul(bank[:, c * NE:(c + 1) * NE], w[:, :], one_hot[:, b, :],
                                  start=(n == 0), stop=(n == len(parts) - 1))
            close(m)

            def gather(opened, j):
                for c in range(4):
                    for b in range(2):
                        m = pe.matmul(opened[:, c * P:(c + 1) * P], ht[:, b, (4 * j + c) * P:(4 * j + c + 1) * P],
                                      sel[:, b, :], start=(b == 0), stop=(b == 1))
                close(m)

            emptied(pe, ("ht", 3))
            pe.wait_ge(sel_ready, 1)
            for j in range(2):
                gather(open_tile(("ga0", j)), j)
            pe.wait_ge(free["act"], BEFORE["act"])
            pe.wait_ge(free["dve"], BEFORE["dve"])

            def pe_pass(i):
                def pass_open(name):
                    at = EX_AT[name]
                    if at >= EX_BANKS:
                        pass_emptied(pe, EXPERT_TILES[at - EX_BANKS][0], i)
                    else:
                        was = max(q for q in range(N_EX) if q % EX_BANKS == at % EX_BANKS)
                        c = EXPERT_TILES[was][1]
                        pe.wait_ge(free[c], i * EX[c] + (BEFORE[c] - EX[c] + rank_in(c, was)))
                    return banks[at % EX_BANKS]

                def pass_slab(slab):
                    n = PASS_SLABS.index(slab)
                    pe.wait_ge(lo_made, i * N_PS + (n + 1))
                    return w_hi[:, n % PARTS, :], w_lo[:, n % PARTS, :]

                def product(out, a_hi, a_lo, w, cols, start, stop):
                    pe.matmul(out, a_hi, w[1][:, cols], start=start, stop=False)
                    pe.matmul(out, a_hi, w[0][:, cols], start=False, stop=False)
                    return pe.matmul(out, a_lo, w[0][:, cols], start=False, stop=stop)

                bank = pass_open(("selT",))
                for b in range(2):
                    m = pe.transpose(bank[:, b * P:(b + 1) * P], selg[:, b, :], ident[:, :])
                close(m)
                pe.wait_ge(free["dve"], i * EX["dve"] + (BEFORE["dve"] - EX["dve"]
                                                         + rank_in("dve", EX_AT[("ga", 1)])))
                for r in range(NR + 1):
                    if r < NR:
                        w = range_width(r)
                        for mat in "gu":
                            bank = pass_open((mat, r))
                            for part in range(KD * w // SLAB):
                                s = pass_slab((mat, r, part))
                                for c in range(SLAB // w):
                                    k = part * (SLAB // w) + c
                                    m = product(bank[:, 0:w], xe_hi[:, k, :], xe_lo[:, k, :], s,
                                                slice(c * w, (c + 1) * w), k == 0, k == KD - 1)
                                if closes((mat, r, part)) is None:
                                    m.then_inc(slab_used, 1)
                            close(m)
                    if r:
                        w = range_width(r - 1)
                        bank = pass_open(("hT", r - 1))
                        pass_emptied(pe, ("u", r - 1), i)
                        for c in range(w // P):
                            m = pe.transpose(bank[:, c * P:(c + 1) * P], hs[:, (r - 1) % 2, c * P:(c + 1) * P],
                                             ident[:, :])
                        close(m)
                acc = [pass_open(("dn", n)) for n in range(2)]
                for k in range(KF):
                    s = pass_slab(("dn", k))
                    if k % 4 == 0:
                        pass_emptied(pe, ("hT", k // 4), i)
                    for n in range(2):
                        m = product(acc[n][:, :], hT_hi[:, k, :], hT_lo[:, k, :], s,
                                    slice(n * 512, (n + 1) * 512), k == 0, k == KF - 1)
                        if k == KF - 1:
                            close(m)
                    if k < KF - 1:
                        m.then_inc(slab_used, 1)
                pe.wait_ge(sel_ready, i + 2)
                for j in range(2):
                    gather(pass_open(("ga", j)), j)
                pass_emptied(pe, ("dn", 0), i)
                pass_emptied(pe, ("dn", 1), i)
                for j in range(4):
                    bank = pass_open(("y", j))
                    for c in range(2):
                        m = pe.matmul(bank[:, c * SEG:(c + 1) * SEG], ye[:, (2 * j + c) * P:(2 * j + c + 1) * P],
                                      selt[:, :], start=True, stop=True)
                    close(m)

            passes(pe, pe_pass)
            for k in range(KD):
                pe.wait_ge(sq_ready, 32 + k + 1)
                m = pe.matmul(banks[0][:, 0:SEG], ones[:, :], h[:, k, seg(LAT)], start=(k == 0), stop=(k == KD - 1))
            m.then_inc(final_full, 1)

        @block.scalar
        def _(act):
            o = Own(act, act_own)
            n_sd = 0
            n_lev = 0

            def root(cols):
                nonlocal n_sd
                n_sd += 1
                act.wait_ge(var_ready, n_sd)
                o.sig(act.activation(msq[:, 0:cols], msq[:, 0:cols], ACT.Sqrt), sd_ready)

            def affine(layer, base, n0, segs):
                act.wait_ge(mods_ready, 2 * layer + (1 if base == 0 else 2))
                for k in range(KD):
                    act.wait_ge(xn_ready, n0 + k + 1)
                    for s in segs:
                        ins = act.activation(h[:, k, seg(s)], h[:, k, seg(s)], ACT.Identity,
                                             bias=mods[:, layer, s, base + k:base + k + 1],
                                             scale=mods[:, layer, s, base + KD + k:base + KD + k + 1])
                        o.sig(ins, h_ready if s == LAT else None)

            def take_modulation(t):
                act.wait_ge(ada_full, t + 1)
                if t:
                    act.wait_ge(adaT_full, t)
                o.sig(act.activation(ada_sb[:, :], ada_bank[:, :], ACT.Copy), ada_taken)

            act.wait_ge(const_in, 16 * N_CONST)
            act.wait_ge(cond_zero, 1)
            o.sig(act.activation(cond[:, :, 0:2], craw[:, :, :], ACT.Silu), cond_ready)
            act.wait_ge(lb_in, 1)
            o.sig(act.activation(lbt[:, 1, :, :], lbt[:, 0, :, :], ACT.Exp), lb_exp)
            for L in range(DEPTH):
                q0 = 0 if L == 0 else SEG
                nq = T - q0
                if L == 0:
                    take_modulation(0)
                root(T)
                affine(L, 0, 16 * L, (CTX, LAT))
                for i in range(8):
                    bank = full(act, ("ff", L, i))
                    o.sig(act.activation(g_of[i // 4][:, i % 4, :], bank[:, :], ACT.Sigmoid), free["act"])
                for i in range(4):
                    bank = full(act, ("hq", L, i))
                    o.sig(act.activation(rq[:, i, q0:T], bank[:, 0:nq], ACT.Silu), free["act"])
                for i in range(2):
                    bank = full(act, ("hg", L, i))
                    o.sig(act.activation(hg[:, i, q0:T], bank[:, 0:nq], ACT.Silu), free["act"])
                for d in (FWD, BWD):
                    act.wait_ge(f_ready, 8 * L + 4 * (d + 1))
                    o.sig(act.activation(g_of[d], g_of[d], ACT.Ln), g_ready)
                act.wait_ge(kk_in, L + 1)
                o.sig(act.activation(kkf, kkf, ACT.Exp), kk_exp)
                o.sig(act.activation(kkb, gb, ACT.Exp), kk_exp)
                o.sig(act.activation(tot[:, 2:4, :, :], tot[:, 0:2, :, :], ACT.Exp), kk_exp)
                for i, (d, b) in enumerate(state_steps(L)):
                    bank = full(act, ("kT", L, d, b))
                    if i < 2 and i == 0:
                        o.settle()
                    o.sig(act.activation(kt[i % 2][:, :], bank[:, :], ACT.Copy), free["act"])
                units = [(b, d) for b in query_blocks(L) for d in (FWD, BWD)]
                for u in range(len(units)):
                    n_lev += 1
                    act.wait_ge(lev_in, n_lev)
                    o.sig(act.activation(levs[u % 2][:, :, :], levs[u % 2][:, :, :], ACT.Exp), lev_exp)
                    if L == 0 and u % 2 == 0:
                        take_modulation(1 + u // 2)
                if L == 0:
                    take_modulation(N_ADA_TILES - 1)
                for i in range(2):
                    root(nq)
                for i in range(2):
                    bank = full(act, ("fo", L, i))
                    o.sig(act.activation(fo[:, i, q0:T], bank[:, 0:nq], ACT.Copy), free["act"])
                for b in query_blocks(L):
                    bank = full(act, ("f1", L, b))
                    o.sig(act.activation(f1[:, b, :], bank[:, :], ACT.Copy), free["act"])
                root(nq)
                root(T)
                for j in range(HEADS // 2):
                    bank = full(act, ("kn", L, j))
                    o.sig(act.activation(kall[0:NOPE, 2 * j, :], bank[0:64, :], ACT.Copy))
                    o.sig(act.activation(kall[0:NOPE, 2 * j + 1, :], bank[64:128, :], ACT.Copy), free["act"])
                for b in range(NBLK):
                    bank = full(act, ("v", L, b))
                    o.sig(act.activation(vtok[:, b, :], bank[:, :], ACT.Copy), free["act"])
                n0 = 0 if L == 0 else 2 * len(attention_units(0))
                for i, (hh, s) in enumerate(attention_units(L)):
                    for qb in range(2):
                        bank = full(act, ("s", L, i, qb))
                        act.wait_ge(neg_max, n0 + 2 * i + qb + 1)
                        c = 2 * i + qb
                        nk = P * len(key_blocks(s))
                        o.sig(act.activation(prob[:, 2 * (i % 2) + qb, 0:nk], bank[:, 0:nk], ACT.Exp,
                                             bias=smax[:, 1, c:c + 1], scale=ATT_SCALE,
                                             accum_out=smax[:, 2, c:c + 1]), free["act"])
                root(nq)
                affine(L, 3 * KD, 16 * L + 8, query_segments(L))
                if L == 0:
                    for k in range(KF):
                        bank = full(act, ("g", k))
                        o.sig(act.activation(hid0[:, k, :], bank[:, :], ACT.Silu), free["act"])
            act.wait_ge(top_in, 1)
            o.sig(act.activation(gt[:, 1, :, 0:1], gt[:, 0, :, 0:1], ACT.Exp), top_exp)
            for j in range(4):
                bank = full(act, ("ht", j))
                o.sig(act.activation(ht[:, j // 2, (j % 2) * 512:(j % 2 + 1) * 512], bank[:, :], ACT.Copy),
                      free["act"])
            four = lambda v: v.rearrange("p (a b) -> p a b", a=4)
            for j in range(2):
                bank = full(act, ("ga0", j))
                o.sig(act.activation(xe_hi[:, 4 * j:4 * j + 4, :], four(bank[:, :]), ACT.Copy), part_hi)

            def act_pass(i):
                def high(n):
                    raw = MOE_SLAB0 + n
                    act.wait_ge(slab_full[raw % SLOTS], i * (16 * N_PS // SLOTS) + 16 * (raw // SLOTS + 1))
                    if n >= PARTS:
                        pass_used(act, n - PARTS, i)
                    else:
                        pass_used(act, N_PS + n - PARTS, i - 1)
                    act.activation(w_hi[:, n % PARTS, :], ring[:, raw % SLOTS, :], ACT.Copy).then_inc(hi_made, 1)

                for n in range(PARTS):
                    high(n)
                for n, slab in enumerate(PASS_SLABS):
                    if n + PARTS < N_PS:
                        high(n + PARTS)
                    tile = closes(slab)
                    if tile is not None and tile[0] == "g":
                        r = tile[1]
                        w = range_width(r)
                        bank = pass_full(act, ("g", r), i)
                        if r >= 2:
                            pass_emptied(act, ("u", r - 2), i)
                        else:
                            act.wait_ge(free["dve"], i * EX["dve"] + (BEFORE["dve"] - EX["dve"]
                                                                      + rank_in("dve", EX_AT[("u", NR - 2 + r)])))
                        act.activation(sg[:, r % 2, 0:w], bank[:, 0:w], ACT.Silu).then_inc(free["act"], 1)
                    turned = None
                    if tile is not None and tile[0] == "u" and tile[1]:
                        turned = tile[1] - 1
                    if slab == ("dn", 0):
                        turned = NR - 1
                    if turned is not None:
                        w = range_width(turned)
                        bank = pass_full(act, ("hT", turned), i)
                        to = hT_hi[:, 4 * turned:4 * turned + w // P, :]
                        act.activation(to, bank[:, 0:w].rearrange("p (a b) -> p a b", b=P),
                                       ACT.Copy).then_inc(part_hi, 1)
                bank = pass_full(act, ("dn", 0), i)
                act.activation(ye[:, 0:512], bank[:, :], ACT.Copy).then_inc(free["act"], 1)
                for j in range(2):
                    bank = pass_full(act, ("ga", j), i)
                    act.activation(xe_hi[:, 4 * j:4 * j + 4, :], four(bank[:, :]), ACT.Copy).then_inc(part_hi, 1)

            passes(act, act_pass)
            root(SEG)

        @block.vector
        def _(dve):
            o = Own(dve, dve_own)
            n_sd = 0

            def norm(bank, cols, width, tile_sem=True):
                nonlocal n_sd
                n_sd += 1
                o.sig(dve.tensor_scalar(msq[:, 0:cols], bank[:, 0:cols], 1.0 / width, EPS, ALU.mult, ALU.add),
                      var_ready)
                dve.wait_ge(sd_ready, n_sd)
                if tile_sem:
                    o.sig(dve.reciprocal(rstd[:, 0:cols], msq[:, 0:cols]), free["dve"])
                else:
                    o.sig(dve.reciprocal(rstd[:, 0:cols], msq[:, 0:cols]))
                o.settle()

            def squares(cols):
                for k in range(KD):
                    o.sig(dve.tensor_tensor(h[:, k, cols], x[:, k, cols], x[:, k, cols], ALU.mult), sq_ready)

            def scaled(cols, n):
                for k in range(KD):
                    o.sig(dve.tensor_tensor(h[:, k, cols], x[:, k, cols], rstd[:, 0:n], ALU.mult), xn_ready)

            def turned_modulation(t):
                layer, b = divmod(t, 3)
                dve.wait_ge(adaT_full, t + 1)
                bank = adaT_bank[:, :].rearrange("p (c j s) -> p c j s", c=4, j=4)
                for s in range(2):
                    to = mods[:, layer, s, b * 16:(b + 1) * 16].rearrange("p (j c) -> p c j", j=4)
                    add = bada[:, layer, b * 16:(b + 1) * 16].rearrange("p (j c) -> p c j", j=4)
                    o.sig(dve.tensor_tensor(to, bank[:, :, :, s], add, ALU.add), adaT_taken if s else None)
                if b != 1:
                    o.settle()
                    c0 = KD if b == 0 else 4 * KD
                    v = mods[:, layer, :, c0:c0 + KD]
                    o.sig(dve.tensor_scalar(v, v, 1.0, None, ALU.add), mods_ready)

            dve.wait_ge(const_in, 16 * N_CONST)
            o.sig(dve.tensor_tensor(lbt[:, 2, 0, :], lbl[:, 0, :], lbl[:, 1, :], ALU.max))
            o.settle()
            for i in range(DEPTH):
                last = dve.tensor_tensor(lbt[:, 0, i, :], lbl[:, i, :], lbt[:, 2, 0, :], ALU.subtract)
                o.sig(last, lb_in if i == DEPTH - 1 else None)
            dve.wait_ge(lb_exp, 1)
            o.sig(dve.tensor_tensor(lbt[:, 2, 1, :], lbt[:, 1, 0, :], lbt[:, 1, 1, :], ALU.add))
            o.settle()
            o.sig(dve.reciprocal(lbt[:, 3, 0, :], lbt[:, 2, 1, :]))
            o.settle()
            for i in range(DEPTH):
                o.sig(dve.tensor_tensor(lbt[:, 0, i, :], lbt[:, 1, i, :], lbt[:, 3, 0, :], ALU.mult))
            o.settle()
            o.sig(dve.tensor_tensor(lb[:, 0, 0, :], lbt[:, 0, 0, :], lbt[:, 0, 0, :], ALU.subtract))
            o.sig(dve.tensor_tensor(lbt[:, 3, 1, :], lbt[:, 0, 0, :], lbt[:, 0, 1, :], ALU.add))
            o.settle()
            o.sig(dve.tensor_tensor(lb[:, 0, 1, :], lbt[:, 3, 1, :], lbt[:, 0, 0, :], ALU.subtract))
            o.settle()
            o.sig(dve.tensor_scalar(lb[:, 1, :, :], lb[:, 0, :, :], -1.0, 1.0, ALU.mult, ALU.add))
            o.settle()

            for L in range(DEPTH):
                q0 = 0 if L == 0 else SEG
                nq = T - q0
                qs = slice(q0, T)
                squares(slice(0, T))
                if L == 0:
                    turned_modulation(0)
                norm(full(dve, ("ss1", L)), T, D)
                scaled(slice(0, T), T)

                for i in range(8):
                    d, hh = divmod(i, 4)
                    emptied(dve, ("ff", L, i))
                    f = g_of[d][:, hh, :]
                    o.sig(dve.tensor_scalar(f, f, lb[:, 1, L, i:i + 1], lb[:, 0, L, i:i + 1], ALU.mult, ALU.add))
                    o.settle()
                    o.sig(dve.tensor_scalar(k_of[d][:, hh, :], f, -1.0, 1.0, ALU.mult, ALU.add), f_ready)
                for b in range(NBLK):
                    bank = full(dve, ("hi", L, b))
                    o.sig(dve.tensor_copy(hi[:, b, :], bank[:, 0:SEG]), free["dve"])
                dve.wait_ge(g_ready, 2 * L + 1)
                for hh in range(RH):
                    o.sig(dve.tensor_tensor_scan(gf[:, hh, :], reset[:, :], gf[:, hh, :], 0.0, ALU.mult, ALU.add))
                dve.wait_ge(g_ready, 2 * L + 2)
                for hh in range(RH):
                    o.sig(dve.tensor_tensor_scan(kkb[:, hh, :], reset[:, :], gb[:, hh, :], 0.0, ALU.mult, ALU.add))
                o.settle()
                ends = lambda v: v.rearrange("p h (b t) -> p h b t", t=P)[:, :, :, P - 1]
                o.sig(dve.tensor_copy(tot[:, 0, :, :], ends(gf)))
                o.sig(dve.tensor_copy(tot[:, 1, :, :], ends(kkb)))
                o.sig(dve.tensor_tensor(gb, kkb, gb, ALU.subtract))
                o.settle()
                blocks = lambda v: v.rearrange("p h (b t) -> p (h b) t", t=P)
                t0 = tot[:, 0, :, :].rearrange("p h b -> p (h b)").unsqueeze(2).to_broadcast([P, RH * NBLK, P])
                o.sig(dve.tensor_tensor(blocks(kkf), t0, blocks(gf), ALU.subtract), kk_in)
                dve.wait_ge(kk_exp, 3 * L + 3)
                o.sig(dve.tensor_tensor(kkf, kkf, kf, ALU.mult), kk_ready)
                o.sig(dve.tensor_tensor(kkb, kkb, kb, ALU.mult), kk_ready)
                steps = state_steps(L)
                for i, (d, b) in enumerate(steps):
                    bank = full(dve, ("st", L, d, b))
                    if incoming(d, b) is None:
                        o.sig(dve.tensor_copy(st[:, i, :], bank[:, 0:RH * RV]), free["dve"])
                        continue
                    was = steps.index((d, incoming(d, b)))
                    o.settle()
                    for hh in range(RH):
                        c = slice(hh * RV, (hh + 1) * RV)
                        o.sig(dve.scalar_tensor_tensor(st[:, i, c], st[:, was, c], tot[:, 2 + d, hh, b:b + 1],
                                                       bank[:, c], ALU.mult, ALU.add),
                              free["dve"] if hh == RH - 1 else None)
                o.settle()
                units = [(b, d) for b in query_blocks(L) for d in (FWD, BWD)]

                def exponents(u):
                    b, d = units[u]
                    bs = slice(b * P, (b + 1) * P)
                    if d == FWD:
                        o.settle()
                        o.sig(dve.tensor_tensor(lowc(kd), kf[:, :, bs], kb[:, :, bs], ALU.add), kd_ready)
                    buf = levs[u % 2]
                    for l, half in enumerate(LEVELS):
                        g = g_of[d][:, :, bs].rearrange("p h (n t) -> p h n t", t=2 * half)
                        z = lowc(buf[:, l, :]).rearrange("p h (n t) -> p h n t", t=2 * half)
                        at = half - 1 if d == FWD else half
                        mid = g[:, :, :, at:at + 1].to_broadcast([P, RH, P // (2 * half), half])
                        o.sig(dve.tensor_tensor(z[:, :, :, half:], g[:, :, :, half:], mid, ALU.subtract))
                        o.sig(dve.tensor_tensor(z[:, :, :, 0:half], mid, g[:, :, :, 0:half], ALU.subtract))
                    z = lowc(buf[:, NL, :])
                    if d == FWD:
                        o.sig(dve.tensor_copy(z, gf[:, :, bs]), lev_in)
                    else:
                        end = tot[:, 1, :, b:b + 1].to_broadcast([P, RH, P])
                        o.sig(dve.tensor_tensor(z, end, gb[:, :, bs], ALU.subtract), lev_in)

                def decayed(u):
                    b, d = units[u]
                    bs = slice(b * P, (b + 1) * P)
                    dve.wait_ge(lev_exp, (0 if L == 0 else 2 * len(query_blocks(0))) + u + 1)
                    late, early = (rq, kf) if d == FWD else (kb, rq)
                    buf = levs[u % 2]
                    for l, half in enumerate(LEVELS):
                        z = lowc(buf[:, l, :]).rearrange("p h (n t) -> p h n t", t=2 * half)
                        for sl, by in ((slice(half, 2 * half), late), (slice(0, half), early)):
                            w = by[:, :, bs].rearrange("p h (n t) -> p h n t", t=2 * half)
                            o.sig(dve.tensor_tensor(z[:, :, :, sl], z[:, :, :, sl], w[:, :, :, sl], ALU.mult))
                    z = lowc(buf[:, NL, :])
                    o.sig(dve.tensor_tensor(z, z, rq[:, :, bs], ALU.mult), lev_ready)

                def merged(u):
                    b, d = units[u]
                    to = mix[:, 6:8, b * P:(b + 1) * P]
                    if d == FWD:
                        bank = full(dve, ("diag", L, b))
                        o.settle()
                        o.sig(dve.tensor_copy(sc, bank[:, :]), free["dve"])
                    for l in range(NL):
                        bank = full(dve, ("lv", L, b, d, l))
                        m = mask[:, d, l, :].unsqueeze(1).to_broadcast([P, RH, P])
                        o.settle()
                        o.sig(dve.copy_predicated(lowc(sc), m, lowc(bank)), free["dve"])
                    if incoming(d, b) is not None:
                        bank = full(dve, ("in", L, b, d))
                        part = bank[:, 0:2 * P].rearrange("p (a b) -> p a b", a=2)
                        if d == FWD or incoming(FWD, b) is None:
                            o.sig(dve.tensor_copy(to, part), free["dve"])
                        else:
                            o.settle()
                            o.sig(dve.tensor_tensor(to, to, part, ALU.add), free["dve"])
                    if L == 0 and u % 2 == 0:
                        turned_modulation(1 + u // 2)

                def within(b):
                    bank = full(dve, ("o", L, b))
                    to = mix[:, 6:8, b * P:(b + 1) * P]
                    o.settle()
                    o.sig(dve.tensor_tensor(to, to, bank[:, 0:2 * P].rearrange("p (a b) -> p a b", a=2), ALU.add),
                          free["dve"])

                exponents(0)
                decayed(0)
                for u in range(1, len(units) + 1):
                    if u < len(units):
                        exponents(u)
                    merged(u - 1)
                    if u < len(units):
                        decayed(u)
                    if u % 2 == 0:
                        within(units[u - 1][0])
                if L == 0:
                    turned_modulation(N_ADA_TILES - 1)
                o.settle()
                for i in range(2):
                    o.sig(dve.tensor_tensor(osq[:, i, qs], mix[:, 6 + i, qs], mix[:, 6 + i, qs], ALU.mult), rec_ready)
                for i in range(2):
                    norm(full(dve, ("rms", L, i)), nq, RV)
                    v = mix[:, 6 + i, qs]
                    o.sig(dve.scalar_tensor_tensor(v, v, gains[:, L, 3:4], rstd[:, 0:nq], ALU.mult, ALU.mult))
                    o.settle()
                    o.sig(dve.tensor_tensor(v, v, hg[:, i, qs], ALU.mult), rec_ready)

                o.settle()
                for i in range(2):
                    bank = full(dve, ("dq", L, i))
                    o.sig(dve.tensor_copy(dq[:, i, qs], bank[:, 0:nq]), free["dve"])
                bank = full(dve, ("dkv", L))
                o.sig(dve.tensor_copy(dkv, bank[:, :]), free["dve"])
                o.settle()
                for i in range(2):
                    o.sig(dve.tensor_tensor(lsq[:, i, qs], dq[:, i, qs], dq[:, i, qs], ALU.mult), k_ready)
                o.sig(dve.tensor_tensor(lsq[:, 2, :], dkv, dkv, ALU.mult), k_ready)

                def rotated(bank, n, out, tab):
                    o.settle()
                    o.sig(dve.tensor_tensor(rt1[64:96, 0:n], bank[64:96, 0:n], rope_t[64:96, tab], ALU.mult))
                    o.sig(dve.tensor_tensor(rt2[64:96, 0:n], bank[96:128, 0:n], rope_t[96:128, tab], ALU.mult),
                          free["dve"])
                    o.settle()
                    return dve.tensor_tensor(out, rt1[64:96, 0:n], rt2[64:96, 0:n], ALU.add)

                bank_kr = full(dve, ("kr", L))
                kr1 = kall[64:96, 0, :]
                o.sig(dve.tensor_tensor(kr1, bank_kr[64:96, :], rope_t[64:96, :], ALU.mult))
                o.sig(dve.tensor_tensor(kall[64:96, 1, :], bank_kr[96:128, :], rope_t[96:128, :], ALU.mult),
                      free["dve"])
                o.settle()
                o.sig(dve.tensor_tensor(kall[64:96, 2, :], kr1, kall[64:96, 1, :], ALU.add))
                o.settle()
                rest = kall[64:96, 2:3, :]
                o.sig(dve.tensor_copy(kall[64:96, 0:2, :], rest.to_broadcast([32, 2, T])))
                o.sig(dve.tensor_copy(kall[64:96, 3:8, :], rest.to_broadcast([32, 5, T])))
                for s in query_segments(L):
                    for c in range(2):
                        bank = full(dve, ("f2", L, s, c))
                        o.sig(dve.tensor_copy(mix[:, 4 + c, seg(s)], bank[:, 0:SEG]), free["dve"])
                norm(full(dve, ("ssq", L)), nq, Q_RANK)
                for i in range(2):
                    v = dq[:, i, qs]
                    o.sig(dve.scalar_tensor_tensor(v, v, gains[:, L, i:i + 1], rstd[:, 0:nq], ALU.mult, ALU.mult),
                          k_ready)
                norm(full(dve, ("sskv", L)), T, KV_RANK)
                o.sig(dve.scalar_tensor_tensor(dkv, dkv, gains[:, L, 2:3], rstd[:, :], ALU.mult, ALU.mult), k_ready)
                for hh in range(HEADS):
                    bank = full(dve, ("q", L, hh))
                    o.sig(dve.tensor_copy(qall[0:NOPE, hh, qs], bank[0:NOPE, 0:nq]))
                    ins = rotated(bank, nq, qall[64:96, hh, qs], qs)
                    o.sig(ins)

                units = attention_units(L)
                n0 = 0 if L == 0 else 2 * len(attention_units(0))
                for i in range(len(units) + 2):
                    if i < len(units):
                        for qb in range(2):
                            bank = full(dve, ("s", L, i, qb))
                            c = 2 * i + qb
                            nk = P * len(key_blocks(units[i][1]))
                            o.sig(dve.tensor_reduce(smax[:, 0, c:c + 1], bank[:, 0:nk], AX.X, ALU.max))
                            o.settle()
                            o.sig(dve.tensor_scalar(smax[:, 1, c:c + 1], smax[:, 0, c:c + 1], -ATT_SCALE, None,
                                                    ALU.mult), neg_max)
                        for qb in range(2):
                            c = 2 * i + qb
                            emptied(dve, ("s", L, i, qb))
                            o.sig(dve.reciprocal(smax[:, 3, c:c + 1], smax[:, 2, c:c + 1]))
                            o.settle()
                            nk = P * len(key_blocks(units[i][1]))
                            v = prob[:, 2 * (i % 2) + qb, 0:nk]
                            o.sig(dve.tensor_scalar(v, v, smax[:, 3, c:c + 1], None, ALU.mult), prob_ready)
                    if 1 <= i <= len(units):
                        u = i - 1
                        for k2 in range(len(key_blocks(units[u][1])) // 2):
                            bank = full(dve, ("pT", L, u, k2))
                            o.sig(dve.tensor_copy(pt[:, u % 2, k2 * 512:(k2 + 1) * 512], bank[:, :]), free["dve"])
                    if i >= 2:
                        u = i - 2
                        hh, s = units[u]
                        bank = full(dve, ("pv", L, u))
                        r0 = (hh % 2) * DV
                        o.sig(dve.tensor_copy(mix[r0:r0 + DV, hh // 2, seg(s)], bank[r0:r0 + DV, 0:SEG]),
                              free["dve"])

                def residual(bank, m, c0):
                    segs = query_segments(L)
                    for s in segs:
                        f0 = s * SEG - q0
                        o.sig(dve.scalar_tensor_tensor(x[:, m, seg(s)], bank[:, f0:f0 + SEG],
                                                       mods[:, L, s, c0 + m:c0 + m + 1], x[:, m, seg(s)],
                                                       ALU.mult, ALU.add),
                              free["dve"] if s == segs[-1] else None)

                for m in range(KD):
                    residual(full(dve, ("wo", L, m)), m, 2 * KD)
                o.settle()
                squares(qs)
                norm(full(dve, ("ss2", L)), nq, D)
                scaled(qs, nq)
                if L == 0:
                    for k in range(KF):
                        bank = full(dve, ("u", k))
                        emptied(dve, ("g", k))
                        o.sig(dve.tensor_tensor(hid0[:, k, :], hid0[:, k, :], bank[:, :], ALU.mult), free["dve"])
                    for m in range(KD):
                        residual(full(dve, ("dn", m)), m, 5 * KD)
                    o.settle()

            bank = full(dve, ("rt",))
            o.sig(dve.tensor_copy(lg, bank[:, 0:2 * NE].rearrange("p (a b) -> p a b", a=2)), free["dve"])
            o.settle()
            for b in range(2):
                o.sig(dve.max(mx8[:, b, :], lg[:, b, :]))
            o.settle()
            for b in range(2):
                o.sig(dve.max_index(ix8[:, b, :], mx8[:, b, :], lg[:, b, :]))
            o.sig(dve.tensor_tensor(gt[:, 0, :, 0:1], mx8[:, :, 1:2], mx8[:, :, 0:1], ALU.subtract), top_in)
            o.settle()
            o.sig(dve.tensor_copy(ixf[:, :, :], ix8[:, :, :]))
            dve.wait_ge(top_exp, 1)
            o.sig(dve.tensor_scalar(gt[:, 1, :, 1:2], gt[:, 1, :, 0:1], 1.0, None, ALU.add))
            o.settle()
            o.sig(dve.reciprocal(gt[:, 1, :, 2:3], gt[:, 1, :, 1:2]))
            o.settle()
            o.sig(dve.tensor_tensor(gt[:, 1, :, 3:4], gt[:, 1, :, 0:1], gt[:, 1, :, 2:3], ALU.mult))
            o.settle()
            for b in range(2):
                for i in range(2):
                    o.sig(dve.tensor_scalar(xsel[:, b, i, :], iota8[:, :], ixf[:, b, i:i + 1], None, ALU.is_equal))
            o.settle()
            for b in range(2):
                for i in range(2):
                    o.sig(dve.tensor_scalar(gt[:, 2 + i, b, :], xsel[:, b, i, :], gt[:, 1, b, 2 + i:3 + i], None,
                                            ALU.mult))
            o.settle()
            o.sig(dve.tensor_tensor(gates[:, :, :], gt[:, 2, :, :], gt[:, 3, :, :], ALU.add))
            o.sig(dve.tensor_tensor(one_hot[:, :, :], xsel[:, :, 0, :], xsel[:, :, 1, :], ALU.add), gates_ready)
            o.sig(dve.memset(yacc[:, :, :], 0.0))
            far = float(1 << 20)
            bank = full(dve, ("rank",))
            o.sig(dve.tensor_copy(rank, bank[:, 0:2 * NE].rearrange("p (a b) -> p a b", a=2)))
            o.sig(dve.tensor_copy(cnt, bank[:, 2 * NE:3 * NE]), free["dve"])
            o.sig(dve.tensor_scalar(lg, one_hot, -far, far, ALU.mult, ALU.add))
            o.settle()
            o.sig(dve.tensor_tensor(rank, rank, lg, ALU.add))
            o.sig(dve.tensor_scalar(over[:, 0, :], cnt, float(P), None, ALU.is_gt))
            o.settle()
            o.sig(dve.tensor_tensor_scan(over[:, 1, :], ones[:, 0:NE], over[:, 0, :], 0.0, ALU.mult, ALU.add))
            o.settle()
            for j in range(MAX_EXTRA):
                o.sig(dve.tensor_scalar(xsel[:, 0, j, :], over[:, 1, :], float(j + 1), None, ALU.is_equal))
            o.settle()
            for j in range(MAX_EXTRA):
                o.sig(dve.tensor_tensor(xsel[:, 0, j, :], xsel[:, 0, j, :], over[:, 0, :], ALU.mult))
            o.settle()
            o.sig(dve.tensor_copy(at_pass[:, :, 0:NE], rank))
            o.sig(dve.tensor_copy(gate_pass[:, :, 0:NE], gates))
            o.sig(dve.memset(at_pass[:, :, N_PASSES:N_PASSES + 1], -1.0))
            o.sig(dve.memset(gate_pass[:, :, N_PASSES:N_PASSES + 1], 0.0))
            for j in range(MAX_EXTRA):
                for n, (table, out) in enumerate(((rank, at_pass), (gates, gate_pass))):
                    o.settle()
                    pick = xsel[:, 0, j:j + 1, :].to_broadcast([P, 2, NE])
                    o.sig(dve.tensor_tensor(xsel[:, 1, 0:2, :], table, pick, ALU.mult))
                    o.settle()
                    o.sig(dve.tensor_reduce(out[:, :, NE + j:NE + j + 1], xsel[:, 1, 0:2, :], AX.X, ALU.add))
                o.settle()
                o.sig(dve.tensor_scalar(at_pass[:, :, NE + j:NE + j + 1], at_pass[:, :, NE + j:NE + j + 1],
                                        -float(P), None, ALU.add))
                o.sig(dve.tensor_tensor(over[:, 2, :], xsel[:, 0, j, :], iota8[:, :], ALU.mult))
                o.settle()
                o.sig(dve.tensor_reduce(over[:, 3, 0:1], over[:, 2, :], AX.X, ALU.add))
                o.settle()
                o.sig(dve.tensor_copy(extra[0:1, 1 + j:2 + j], over[0:1, 3, 0:1]))
            o.settle()
            o.sig(dve.tensor_copy(extra[0:1, 0:1], over[0:1, 1, NE - 1:NE]), extra_ready)

            def select(i):
                at = at_pass[:, :, bass.ds(i, 1)].to_broadcast([P, 2, P])
                slots = iota[:, :].unsqueeze(1).to_broadcast([P, 2, P])
                dve.tensor_tensor(sel[:, :, :], slots, at, ALU.is_equal).then_inc(sel_own, 1)
                dve.wait_ge(sel_own, i + 1)
                g = gate_pass[:, :, bass.ds(i, 1)].to_broadcast([P, 2, P])
                dve.tensor_tensor(selg[:, :, :], sel[:, :, :], g, ALU.mult).then_inc(sel_ready, 1)

            select(0)
            four = lambda v: v.rearrange("p (a b) -> p a b", a=4)
            plain = lambda v: v.bitcast(F32)
            for j in range(2):
                bank = full(dve, ("ga0", j))
                dve.wait_ge(part_hi, j + 1)
                dve.tensor_tensor(xe_lo[:, 4 * j:4 * j + 4, :], four(bank[:, :]), plain(xe_hi[:, 4 * j:4 * j + 4, :]),
                                  ALU.subtract).then_inc(free["dve"], 1)

            def dve_pass(i):
                def low(n):
                    raw = MOE_SLAB0 + n
                    dve.wait_ge(hi_made, i * N_PS + (n + 1))
                    dve.tensor_tensor(w_lo[:, n % PARTS, :], ring[:, raw % SLOTS, :], plain(w_hi[:, n % PARTS, :]),
                                      ALU.subtract).then_inc(lo_made, 1)

                for n in range(PARTS):
                    low(n)
                bank = pass_full(dve, ("selT",), i)
                dve.tensor_copy(selt[:, :], bank[:, 0:2 * P]).then_inc(free["dve"], 1)
                dve.wait_ge(sel_ready, i + 1)
                select(i + 1)
                for n, slab in enumerate(PASS_SLABS):
                    if n + PARTS < N_PS:
                        low(n + PARTS)
                    tile = closes(slab)
                    if tile is not None and tile[0] == "u":
                        r = tile[1]
                        w = range_width(r)
                        bank = pass_full(dve, ("u", r), i)
                        pass_emptied(dve, ("g", r), i)
                        if r >= 2:
                            pass_full(dve, ("hT", r - 2), i)
                        dve.tensor_tensor(hs[:, r % 2, 0:w], sg[:, r % 2, 0:w], bank[:, 0:w],
                                          ALU.mult).then_inc(free["dve"], 1)
                    turned = None
                    if tile is not None and tile[0] == "u" and tile[1]:
                        turned = tile[1] - 1
                    if slab == ("dn", 0):
                        turned = NR - 1
                    if turned is not None:
                        w = range_width(turned)
                        bank = pass_full(dve, ("hT", turned), i)
                        dve.wait_ge(part_hi, i * PARTS_HI + (2 + turned + 1))
                        cs = slice(4 * turned, 4 * turned + w // P)
                        dve.tensor_tensor(hT_lo[:, cs, :], bank[:, 0:w].rearrange("p (a b) -> p a b", b=P),
                                          plain(hT_hi[:, cs, :]), ALU.subtract).then_inc(free["dve"], 1)
                bank = pass_full(dve, ("dn", 1), i)
                dve.tensor_copy(ye[:, 512:1024], bank[:, :]).then_inc(free["dve"], 1)
                for j in range(2):
                    bank = pass_full(dve, ("ga", j), i)
                    dve.wait_ge(part_hi, i * PARTS_HI + (2 + NR + j + 1))
                    dve.tensor_tensor(xe_lo[:, 4 * j:4 * j + 4, :], four(bank[:, :]),
                                      plain(xe_hi[:, 4 * j:4 * j + 4, :]), ALU.subtract).then_inc(free["dve"], 1)
                for j in range(4):
                    bank = pass_full(dve, ("y", j), i)
                    v = yacc[:, 2 * j:2 * j + 2, :]
                    dve.tensor_tensor(v, v, bank[:, :].rearrange("p (a b) -> p a b", a=2),
                                      ALU.add).then_inc(free["dve"], 1)

            passes(dve, dve_pass)
            dve.wait_ge(free["dve"], n_passes(dve) * EX["dve"] + BEFORE["dve"])
            for m in range(KD):
                o.sig(dve.scalar_tensor_tensor(x[:, m, seg(LAT)], yacc[:, m, :], mods[:, DEPTH - 1, LAT, 5 * KD + m:5 * KD + m + 1],
                                               x[:, m, seg(LAT)], ALU.mult, ALU.add))
            o.settle()
            squares(seg(LAT))
            dve.wait_ge(final_full, 1)
            norm(banks[0], SEG, D, tile_sem=False)
            for m in range(KD):
                o.sig(dve.scalar_tensor_tensor(h[:, m, seg(LAT)], x[:, m, seg(LAT)], fing[:, m:m + 1],
                                               rstd[:, 0:SEG], ALU.mult, ALU.mult), out_ready)


def constants():
    c = {"ident": np.eye(P), "ones": np.ones((P, P)),
         "ones_blk": np.kron(np.eye(2), np.ones((64, 64)))}
    t = np.arange(P)
    mask = np.zeros((P, 2, NL, P), np.int32)
    for l, half in enumerate(LEVELS):
        same = t[:, None] // (2 * half) == t[None, :] // (2 * half)
        late = (t // half) % 2 == 1
        mask[:, FWD, l] = same & ~late[:, None] & late[None, :]
        mask[:, BWD, l] = same & late[:, None] & ~late[None, :]
    c["mask"] = mask
    ang = 2 * np.pi * np.outer(np.arange(FOUR_CH), np.arange(FOUR_CH)) / FOUR_CH
    scale = (SEG * FOUR_CH) ** -0.5
    c["dftc"] = np.concatenate([np.kron(np.eye(2), np.cos(ang)), np.kron(np.eye(2), np.sin(ang))], 1)
    ang = 2 * np.pi * (np.outer(np.arange(SEG), np.arange(SEG)) % SEG) / SEG
    tab = np.stack([np.cos(ang), -np.sin(ang)]) * scale
    c["dftt"] = tab.reshape(2, 2, P, SEG).transpose(2, 0, 1, 3)
    rows = SEG // GRID_W
    row_ids = np.repeat(np.arange(rows), GRID_W).astype(np.float64)
    col_ids = np.tile(np.arange(GRID_W), rows).astype(np.float64)
    per_axis = ROPE // 2
    inv = 10000.0 ** (-np.arange(0, per_axis, 2) / per_axis)
    ang = np.stack([row_ids[:, None] * inv, col_ids[:, None] * inv], 1)
    cos, sin = np.cos(ang), np.sin(ang)
    rope = np.zeros((P, T))
    rope[64:96, :SEG] = 1.0
    rope[64:96, SEG:] = np.stack([cos, cos], 2).reshape(SEG, ROPE).T
    rope[96:128, SEG:] = np.stack([-sin, sin], 2).reshape(SEG, ROPE).T
    c["rope"] = rope
    c["reset"] = np.tile((np.arange(T) % P != 0).astype(float), (P, 1))
    c["iota"] = np.tile(np.arange(P, dtype=float), (P, 1))
    c["before"] = np.triu(np.ones((P, P)), 1)
    c["iota8"] = np.tile(np.arange(NE, dtype=float), (P, 1))
    return {k: np.ascontiguousarray(v if v.dtype == np.int32 else v.astype(np.float32)) for k, v in c.items()}


SWAP = np.array([16 * a + 8 * (1 - s) + i for a in range(2) for s in range(2) for i in range(8)])


def lay_out(x, c, ctx, c_ctx, w_ada, b_ada, w_in, q_norm_g, kv_norm_g, w_uq, w_ukv, hgrn_norm_g,
            lb_logits, w_out, ffn_w_gate, ffn_w_up, ffn_w_down, moe_router, moe_w_gate, moe_w_up,
            moe_w_down, final_g):
    def feat(v):
        v = v.reshape(v.shape[:-1] + (-1, P))
        return np.moveaxis(v, -1, 0)

    def slabs(w, width=P):
        n_l, k, n = w.shape
        return w.reshape(n_l, k // P, P, n // width, width).transpose(0, 3, 2, 1, 4).reshape(
            n_l, n // width, P, k // P * width)

    m = constants()
    m["x"] = np.stack([ctx[0].T.reshape(KD, P, SEG).transpose(1, 0, 2),
                       x[0].T.reshape(KD, P, SEG).transpose(1, 0, 2)])
    m["cond"] = np.stack([c_ctx.reshape(KD, P).T, c[0].reshape(KD, P).T], -1)
    m["bada"] = feat(b_ada)
    m["gains"] = np.concatenate([feat(q_norm_g), feat(kv_norm_g),
                                 np.concatenate([hgrn_norm_g, hgrn_norm_g], -1).T[:, :, None]], -1)
    m["fing"] = feat(final_g)
    m["lbl"] = feat(lb_logits).transpose(0, 2, 1, 3).reshape(P, DEPTH, 8)
    m["ada"] = w_ada
    sizes = [Q_RANK, KV_RANK, ROPE, SEG, 512, 512, 512, SEG, SEG]
    at = np.cumsum([0] + sizes)
    dq, dkv, kr, fo, hq, hff, hfb, hi, hg = [w_in[:, :, at[i]:at[i + 1]] for i in range(9)]
    win = np.zeros((DEPTH, len(WIN), P, SLAB), np.float32)
    win[:, 0:4], win[:, 4:8] = slabs(hff), slabs(hfb)
    win[:, 8:10] = slabs(hi, 2 * P)[:, 0].reshape(DEPTH, P, 2, SLAB).transpose(0, 2, 1, 3)
    win[:, 10:14], win[:, 14:16] = slabs(hq), slabs(hg)
    win[:, 16:18], win[:, 18:19] = slabs(dq), slabs(dkv)
    win[:, 19:20, :, 0:512] = slabs(np.concatenate([kr, kr[:, :, SWAP]], -1), 64)
    win[:, 20:22] = slabs(fo)
    uq = w_uq.reshape(DEPTH, 2, P, HEADS, QK)
    uq = np.concatenate([uq, uq[..., NOPE:][..., SWAP]], -1)
    win[:, 22:24] = uq.reshape(DEPTH, 2, P, HEADS * P)
    ukv = w_ukv.reshape(DEPTH, P, HEADS, NOPE + DV)
    win[:, 24] = np.concatenate([ukv[..., :NOPE].reshape(DEPTH, P, -1), ukv[..., NOPE:].reshape(DEPTH, P, -1)], -1)
    m["win"] = win
    m["wo"] = slabs(w_out)

    def ffn(g, u, d):
        n = g.shape[0]
        out = np.zeros((n, N_FFN_SLABS, P, SLAB), np.float32)
        out[:, 0:2 * KF:2], out[:, 1:2 * KF:2] = slabs(g), slabs(u)
        dn = slabs(d)
        for i in range(3):
            part = dn[:, :, :, i * SLAB:(i + 1) * SLAB]
            out[:, 2 * KF + i::3, :, :part.shape[-1]] = part
        return out

    m["ffn"] = ffn(ffn_w_gate, ffn_w_up, ffn_w_down)[0]
    moe = np.zeros((NE, N_PS, P, SLAB), np.float32)
    j = 0
    for r in range(NR):
        w = range_width(r)
        n = KD * w // SLAB
        for mat in (moe_w_gate[0], moe_w_up[0]):
            part = mat[:, :, 512 * r:512 * r + w].reshape(NE, n, SLAB // w, P, w)
            moe[:, j:j + n] = part.transpose(0, 1, 3, 2, 4).reshape(NE, n, P, SLAB)
            j += n
    moe[:, j:] = moe_w_down[0].reshape(NE, KF, P, D)
    m["moe"] = moe
    m["router"] = moe_router[0].reshape(KD, P, NE).transpose(1, 0, 2)
    return {k: np.ascontiguousarray(v) for k, v in m.items()}


def kernel(**inputs):
    import concourse.bacc as bacc
    from concourse.bass_utils import run_bass_kernel_spmd

    arrays = lay_out(**{k: np.asarray(v) for k, v in inputs.items()})
    nc = bacc.Bacc("TRN2", target_bir_lowering=False, num_devices=1)
    ops = {k: nc.dram_tensor(f"in_{k}", v.shape, mybir.dt.from_np(v.dtype), kind="ExternalInput").ap()
           for k, v in arrays.items()}
    ops["out"] = nc.dram_tensor("out_x", (P, KD, SEG), F32, kind="ExternalOutput").ap()
    build(nc, ops)
    r = run_bass_kernel_spmd(nc, [{f"in_{k}": v for k, v in arrays.items()}], core_ids=[0])
    got = np.asarray(r.results[0]["out_x"])
    return np.ascontiguousarray(got.transpose(2, 1, 0).reshape(1, SEG, D))
```

```python
from contextlib import ExitStack

import numpy as np

import concourse.bass as bass
from concourse import mybir

F32 = mybir.dt.float32
F32R = mybir.dt.float32r
I32 = mybir.dt.int32
U8 = mybir.dt.uint8
U32 = mybir.dt.uint32
ALU = mybir.AluOpType
ACT = mybir.ActivationFunctionType
AX = mybir.AxisListType

P = 128
D = 1024
KD = D // P
SEG = 256
T = 2 * SEG
NBLK = T // P
DEPTH = 2
EPS = 1e-6
GRID_W = 64

HEADS = 8
NOPE, ROPE, DV = 64, 32, 64
QK = NOPE + ROPE
Q_RANK, KV_RANK = 256, 128
ATT_SCALE = float(QK) ** -0.5

FOUR_CH = 64
RH = 4
RV = 64
LEVELS = [64, 32, 16, 8, 4, 2, 1]
NL = len(LEVELS)

D_FF = 2816
KF = D_FF // P
NE = 8
REGION = 16960
EX_F32 = 8480

SLOTS = 11
SLAB = 1024
KH = KF // 2
HALF_SLABS = 2 * KH + 2 * KD
N_FFN_SLABS = 2 * HALF_SLABS
FFN_PARTS = 4
BANKS = 6
EX_BANKS = 8
FWD, BWD = 0, 1
CTX, LAT = 0, 1
N_ADA = 6 * D // P
N_ADA_TILES = 6

WIN = ([("ff", i) for i in range(8)] + [("hi", 0), ("hi", 1)] + [("hq", i) for i in range(4)]
       + [("hg", i) for i in range(2)] + [("dq", i) for i in range(2)] + [("dkv", 0), ("kr", 0)]
       + [("fo", i) for i in range(2)] + [("uq", 0), ("uq", 1), ("ukv", 0)])


def query_blocks(layer):
    return [0, 1, 2, 3] if layer == 0 else [2, 3]


def query_segments(layer):
    return [CTX, LAT] if layer == 0 else [LAT]


def state_steps(layer):
    fwd = [(FWD, b) for b in (0, 1, 2)]
    bwd = [(BWD, b) for b in (1, 0, 3)]
    return [s for pair in zip(fwd, bwd) for s in pair]


def incoming(direction, block):
    if direction == FWD:
        return block - 1 if block > 0 else None
    return {1: None, 0: 1, 3: 0, 2: 3}[block]


def attention_units(layer):
    return [(h, s) for s in query_segments(layer) for h in range(HEADS)]


def key_blocks(seg):
    return [0, 1] if seg == CTX else [0, 1, 2, 3]


class Tiles:

    def __init__(self):
        self.number, self.consumer, self.rank = {}, [], []
        self.count = {"act": 0, "dve": 0}

    def add(self, name, consumer):
        self.number[name] = len(self.consumer)
        self.consumer.append(consumer)
        self.count[consumer] += 1
        self.rank.append(self.count[consumer])


def plan_ffn():
    out, n = [], 0
    for half in range(2):
        for k in range(half * KH, (half + 1) * KH):
            out += [(("g", k), [n]), (("u", k), [n + 1])]
            n += 2
        for m in range(KD):
            out.append((("dn", half, m), [n, n + 1]))
            n += 2
    assert n == N_FFN_SLABS
    return out


FFN_TILES = plan_ffn()


def ffn_width(j):
    at = j % HALF_SLABS - 2 * KH
    return KH * P - SLAB if at >= 0 and at % 2 else SLAB


def plan_tiles():
    t = Tiles()
    for L in range(DEPTH):
        t.add(("ss1", L), "dve")
        for i in range(8):
            t.add(("ff", L, i), "act")
        for b in range(NBLK):
            t.add(("hi", L, b), "dve")
        for i in range(4):
            t.add(("hq", L, i), "act")
        for i in range(2):
            t.add(("hg", L, i), "act")
        for i in range(2):
            t.add(("dq", L, i), "act")
        t.add(("dkv", L), "act")
        t.add(("kr", L), "dve")
        for i in range(2):
            t.add(("fo", L, i), "act")
        for d, b in state_steps(L):
            t.add(("kT", L, d, b), "act")
            t.add(("st", L, d, b), "dve")
        for b in query_blocks(L):
            t.add(("diag", L, b), "dve")
            for d in (FWD, BWD):
                for l in range(NL):
                    t.add(("lv", L, b, d, l), "dve")
                if incoming(d, b) is not None:
                    t.add(("in", L, b, d), "dve")
            t.add(("o", L, b), "dve")
        t.add(("ssq", L), "dve")
        t.add(("sskv", L), "dve")
        for b in query_blocks(L):
            t.add(("f1", L, b), "act")
        for s in query_segments(L):
            for c in range(2):
                t.add(("f2", L, s, c), "dve")
        for h in range(HEADS):
            t.add(("q", L, h), "dve")
        for j in range(HEADS // 2):
            t.add(("kn", L, j), "act")
        for b in range(NBLK):
            t.add(("v", L, b), "act")
        for i in range(2):
            t.add(("rms", L, i), "dve")
        units = attention_units(L)
        for i in range(len(units) + 2):
            if i < len(units):
                for qb in range(2):
                    t.add(("s", L, i, qb), "act")
            if 1 <= i <= len(units):
                for kb2 in range(len(key_blocks(units[i - 1][1])) // 2):
                    t.add(("pT", L, i - 1, kb2), "act")
            if i >= 2:
                t.add(("pv", L, i - 2), "dve")
        for m in range(KD):
            t.add(("wo", L, m), "dve")
        t.add(("ss2", L), "dve")
        if L == 0:
            for name, _ in FFN_TILES:
                t.add(name, "act" if name[0] == "g" else "dve")
        else:
            t.add(("rt",), "dve")
            for j in range(4):
                t.add(("ht", j), "act")
            t.add(("rank",), "dve")
            for j in range(2):
                t.add(("ga0", j), "dve")
    return t


TL = plan_tiles()
NR = 6


def range_width(r):
    return 512 if r < NR - 1 else D_FF - 512 * (NR - 1)


EXPERT_TILES = [(("selT",), "dve")]
for _r in range(NR + 1):
    if _r < NR:
        EXPERT_TILES += [(("g", _r), "act"), (("u", _r), "dve")]
    if _r:
        EXPERT_TILES += [(("hT", _r - 1), "dve")]
EXPERT_TILES += [(("dn", 0), "act"), (("dn", 1), "dve"), (("ga", 0), "dve"), (("ga", 1), "dve")]
EXPERT_TILES += [(("y", j), "dve") for j in range(4)]
N_EX = len(EXPERT_TILES)
EX_AT = {name: i for i, (name, _) in enumerate(EXPERT_TILES)}
EX = {c: sum(q == c for _, q in EXPERT_TILES) for c in ("act", "dve")}
N_BEFORE = len(TL.consumer)
BEFORE = TL.count


def rank_in(consumer, upto):
    return sum(c == consumer for _, c in EXPERT_TILES[:upto + 1])


def plan_pass_slabs():
    out = []
    for r in range(NR):
        for m in "gu":
            out += [(m, r, i) for i in range(KD * range_width(r) // SLAB)]
    return out + [("dn", k) for k in range(KF)]


PASS_SLABS = plan_pass_slabs()
N_PS = len(PASS_SLABS)
assert N_PS % SLOTS == 0


def closes(slab):
    if slab[0] == "dn":
        return ("dn", 1) if slab[1] == KF - 1 else None
    m, r, i = slab
    return (m, r) if i == KD * range_width(r) // SLAB - 1 else None


OWN_PER_PASS = sum(closes(q) is None for q in PASS_SLABS)
PARTS = 6
assert N_PS % PARTS == 0
PARTS_HI = NR + 2
MAX_EXTRA = 3
N_PASSES = NE + MAX_EXTRA


def plan_slabs():
    order = [("ada", 0, k, n) for k in range(KD) for n in range(2)]
    for L in range(DEPTH):
        order += [("win", L, j) for j in range(22)]
        if L == 0:
            order += [("ada", t, k, n) for t in range(1, N_ADA_TILES) for k in range(KD) for n in range(2)]
        order += [("win", L, j) for j in range(22, len(WIN))]
        order += [("wo", L, m) for m in range(KD)]
        if L == 0:
            order += [("ffn", j) for j in range(N_FFN_SLABS)]
    return {name: i for i, name in enumerate(order)}


SL = plan_slabs()
MOE_SLAB0 = len(SL)
OWN_BEFORE = N_ADA_TILES * (2 * KD - 1)


def slab_tile(name):
    if name[0] == "win":
        _, L, j = name
        kind, i = WIN[j]
        if kind == "hi":
            return ("hi", L, NBLK - 1)
        if kind == "uq":
            return ("q", L, HEADS - 1)
        if kind == "ukv":
            return ("v", L, NBLK - 1)
        return (kind, L) if kind in ("dkv", "kr") else (kind, L, i)
    if name[0] == "wo":
        return name
    return None


def build(nc, a):
    ctx = ExitStack()
    with ctx:
        def sb(name, shape, dt=F32):
            return ctx.enter_context(nc.sbuf_tensor(name, shape, dt))

        def sem(name):
            return ctx.enter_context(nc.semaphore(name))

        x = sb("x", [P, KD, T])
        h_at = nc.sbuf_base
        h = sb("h", [P, KD, T])
        mix = sb("mix", [P, KD, T])
        spare = sb("spare", [P, PARTS * 2 * SLAB - 2 * KD * T])
        ring = sb("ring", [P, SLOTS, SLAB])
        ident = sb("ident", [P, P])
        ones = sb("ones", [P, P])
        ones_blk = sb("ones_blk", [P, P])
        mask = sb("mask", [P, 2, NL, P], I32)
        dftc = sb("dftc", [P, 2 * P])
        dftt = sb("dftt", [P, 2, 2, SEG])
        rope_t = sb("rope_t", [P, T])
        reset = sb("reset", [P, T])
        cond = sb("cond", [P, KD, 32])
        craw = sb("craw", [P, KD, 2])
        bada = sb("bada", [P, DEPTH, N_ADA])
        gains = sb("gains", [P, DEPTH, 4])
        fing = sb("fing", [P, KD])
        iota8 = sb("iota8", [P, NE])
        iota = sb("iota", [P, P])
        before = sb("before", [P, P])
        extra = sb("extra", [1, 1 + MAX_EXTRA], I32)
        lbl = sb("lbl", [P, DEPTH, 8])
        lb = sb("lb", [P, 2, DEPTH, 8])
        lbt = sb("lbt", [P, 4, DEPTH, 8])
        mods = sb("mods", [P, DEPTH, 2, N_ADA])
        ada_sb = sb("ada_sb", [P, 512])
        router = sb("router", [P, KD, NE])
        rstd = sb("rstd", [P, T])
        msq = sb("msq", [P, T])
        smax = sb("smax", [P, 4, 2 * HEADS * 2])
        region_at = nc.sbuf_base
        region = sb("region", [P, REGION])

        def over(name, shape, offset):
            return nc.alloc_sbuf_tensor_at(name, shape, F32R, offset=offset)

        w_hi = over("w_hi", [P, PARTS, SLAB], h_at)
        w_lo = over("w_lo", [P, PARTS, SLAB], h_at + 4 * PARTS * SLAB)
        at = region_at + 4 * EX_F32
        xe_hi, xe_lo = over("xe_hi", [P, KD, P], at), over("xe_lo", [P, KD, P], at + 4 * D)
        hT_hi = over("hT_hi", [P, KF, P], at + 8 * D)
        hT_lo = over("hT_lo", [P, KF, P], at + 8 * D + 4 * D_FF)
        assert EX_F32 + 2 * D + 2 * D_FF <= REGION
        f_hi = over("f_hi", [P, FFN_PARTS, SLAB], h_at + 4 * 2 * KD * T)
        f_lo = over("f_lo", [P, FFN_PARTS, SLAB], h_at + 4 * KD * T)
        h_lo = over("h_lo", [P, KD, T], h_at)
        h_hi = over("h_hi", [P, KD, T], region_at)
        hid_hi = over("hid_hi", [P, KH, T], region_at + 4 * KD * T)
        hid_lo = over("hid_lo", [P, KH, T], region_at + 4 * (KD + KH) * T)
        hid = region[:, (KD + 2 * KH) * T:(KD + 2 * KH + 3) * T].rearrange("p (a b) -> p a b", a=3)

        def carve(shapes):
            out, at = [], 0
            for s in shapes:
                n = int(np.prod(s))
                v = region[:, at:at + n]
                at += n
                if len(s) == 2:
                    v = v.rearrange("p (a b) -> p a b", a=s[0])
                elif len(s) == 3:
                    v = v.rearrange("p (a b c) -> p a b c", a=s[0], b=s[1])
                out.append(v)
            assert at <= REGION, at
            return out

        hg, hi, kf, kb, gf, gb, lev, st, kd, sc, tot = carve([
            [2, T], [NBLK, RH * RV], [RH, T], [RH, T], [RH, T], [RH, T],
            [NL + 1, RH * P], [6, RH * RV], [RH * P], [RH * P], [4, RH, NBLK]])
        rq = mix[:, 0:4, :]
        kkf, kkb = lev[:, 0:4, :], lev[:, 4:8, :]
        kt = [msq, rstd]
        k_of, g_of = (kf, kb), (gf, gb)
        levs = [spare[:, :].rearrange("p (a b) -> p a b", a=NL + 1), lev]
        dq, dkv, fo, kr = h[:, 0:2, :], h[:, 2, :], h[:, 3:5, :], h[:, 5, :]
        lsq = [h[:, 6, :], h[:, 7, :], mix[:, 4, :]]
        osq = h[:, 6:8, :]
        _, kall, qall, vtok, pt, prob = carve([
            [2, T], [HEADS, T], [HEADS, T], [NBLK, HEADS * DV], [2, 4 * SEG], [4, T]])
        f1 = prob
        (ht, sel, selg, selt, sg, hs, ye, yacc, gates, lg, mx8, ix8, ixf, gt, one_hot,
         rank, cnt, over, at_pass, gate_pass, xsel) = carve([
            [2, D], [2, P], [2, P], [2 * P], [2, 512], [2, 512], [D], [KD, SEG],
            [2, NE], [2, NE], [2, 8], [2, 8], [2, 8], [4, 2, NE], [2, NE],
            [2, NE], [NE], [4, NE], [2, N_PASSES + 1], [2, N_PASSES + 1], [2, 3, NE]])
        assert int(np.prod(ht.shape[1:])) and 2 * D + 4 * P + 2 * P + 2048 + D + KD * SEG + 400 <= EX_F32
        ix8 = ix8.bitcast(U32)

        banks = [ctx.enter_context(nc.psum_tensor(f"bank{i}", [P, 512], F32)) for i in range(EX_BANKS)]
        ada_bank, adaT_bank = banks[7], banks[6]

        slab_full = [sem(f"slab_full{i}") for i in range(SLOTS)]
        slab_used = sem("slab_used")
        tile_full = sem("tile_full")
        free = {"act": sem("tile_emptied_act"), "dve": sem("tile_emptied_dve")}
        const_in = sem("const_in")
        x_in = sem("x_in")
        late_in = sem("late_in")
        dve_own = sem("dve_own")
        act_own = sem("act_own")
        pool_own = sem("pool_own")
        cond_zero = sem("cond_zero")
        cond_ready = sem("cond_ready")
        lb_in = sem("lb_in")
        lb_exp = sem("lb_exp")
        sq_ready = sem("sq_ready")
        xn_ready = sem("xn_ready")
        h_ready = sem("h_ready")
        mods_ready = sem("mods_ready")
        ada_full = sem("ada_full")
        ada_taken = sem("ada_taken")
        adaT_full = sem("adaT_full")
        adaT_taken = sem("adaT_taken")
        var_ready = sem("var_ready")
        sel_own = sem("sel_own")
        sd_ready = sem("sd_ready")
        f_ready = sem("f_ready")
        g_ready = sem("g_ready")
        kk_in = sem("kk_in")
        kk_exp = sem("kk_exp")
        kk_ready = sem("kk_ready")
        lev_in = sem("lev_in")
        lev_exp = sem("lev_exp")
        lev_ready = sem("lev_ready")
        kd_ready = sem("kd_ready")
        rec_ready = sem("rec_ready")
        neg_max = sem("neg_max")
        exp_ready = sem("exp_ready")
        prob_ready = sem("prob_ready")
        k_ready = sem("k_ready")
        kr_ready = sem("kr_ready")
        kr_spread = sem("kr_spread")
        lsq_ready = sem("lsq_ready")
        q_nope = sem("q_nope")
        sel_ready = sem("sel_ready")
        gather_done = sem("gather_done")
        extra_ready = sem("extra_ready")
        final_full = sem("final_full")
        ffn_hi = sem("ffn_hi")
        ffn_lo = sem("ffn_lo")
        h_hi_made = sem("h_hi_made")
        h_lo_made = sem("h_lo_made")
        hid_hi_made = sem("hid_hi_made")
        hid_lo_made = sem("hid_lo_made")
        hi_made = sem("hi_made")
        lo_made = sem("lo_made")
        part_hi = sem("part_hi")
        top_in = sem("top_in")
        top_exp = sem("top_exp")
        gates_ready = sem("gates_ready")
        out_ready = sem("out_ready")
        out_done = sem("out_done")
        block = ctx.enter_context(nc.Block())

        class Own:

            def __init__(self, eng, own):
                self.eng, self.own, self.counts, self.last, self.base = eng, own, {}, None, None

            def sig(self, ins, s=None):
                s = self.own if s is None else s
                ins.then_inc(s, 1)
                key = str(s)
                self.counts[key] = self.counts.get(key, 0) + 1
                self.last = (s, key)

            def settle(self):
                s, key = self.last
                n = self.counts[key]
                if self.base is not None:
                    e, per = self.base
                    n = e * per[key] + n
                self.eng.wait_ge(s, n)

        def full(eng, name):
            n = TL.number[name]
            eng.wait_ge(tile_full, n + 1)
            return banks[n % BANKS]

        def emptied(eng, name):
            n = TL.number[name]
            eng.wait_ge(free[TL.consumer[n]], TL.rank[n])

        def pass_full(eng, name, i):
            eng.wait_ge(tile_full, i * N_EX + (N_BEFORE + EX_AT[name] + 1))
            return banks[EX_AT[name] % EX_BANKS]

        def pass_emptied(eng, name, i):
            c = EXPERT_TILES[EX_AT[name]][1]
            eng.wait_ge(free[c], i * EX[c] + (BEFORE[c] + rank_in(c, EX_AT[name])))

        def pass_used(eng, j, i):
            tile = closes(PASS_SLABS[j])
            if tile is None:
                own = sum(closes(q) is None for q in PASS_SLABS[:j + 1])
                eng.wait_ge(slab_used, i * OWN_PER_PASS + (OWN_BEFORE + own))
            else:
                eng.wait_ge(tile_full, i * N_EX + (N_BEFORE + EX_AT[tile] + 1))

        def passes(eng, body):
            with eng.Fori(0, NE) as i:
                body(i)
            extra_passes(eng, body)

        def extra_passes(eng, body):
            eng.wait_ge(extra_ready, 1)
            n_extra = eng.value_load(extra[0:1, 0:1], min_val=0, max_val=MAX_EXTRA)
            with eng.Fori(0, MAX_EXTRA) as j:
                with eng.If(n_extra > j):
                    body(j + NE)

        def n_passes(eng):
            return eng.value_load(extra[0:1, 0:1], min_val=0, max_val=MAX_EXTRA) + NE

        def seg(s):
            return slice(s * SEG, (s + 1) * SEG)

        def lowc(v):
            return v.rearrange("p (a b) -> p a b", a=RH)

        N_EARLY = 6
        N_X = 2
        N_LATE = 11

        @block.sync
        def _(sp):
            early = [(craw, a["cond"]), (lbl, a["lbl"]), (ident, a["ident"]), (ones, a["ones"]),
                     (gains, a["gains"]), (bada, a["bada"])]
            late = [(reset, a["reset"]), (ones_blk, a["ones_blk"]), (mask, a["mask"]),
                    (dftc, a["dftc"]), (dftt, a["dftt"]), (rope_t, a["rope"]), (router, a["router"]),
                    (fing, a["fing"]), (iota8, a["iota8"]), (iota, a["iota"]), (before, a["before"])]
            assert len(early) == N_EARLY and len(late) == N_LATE
            for dst, src in early:
                sp.dma_start(dst[:], src).then_inc(const_in, 16)

            names = list(SL)
            own_used = 0
            used_at = []
            for name in names:
                if name[0] == "ffn":
                    used_at.append((ffn_lo, name[1] + 1))
                elif slab_tile(name) is not None:
                    used_at.append((tile_full, TL.number[slab_tile(name)] + 1))
                elif name[2:] == (KD - 1, 1):
                    used_at.append((ada_full, name[1] + 1))
                else:
                    own_used += 1
                    used_at.append((slab_used, own_used))

            def load(n, src):
                sp.dma_start(ring[:, n % SLOTS, 0:src.shape[-1]], src).then_inc(slab_full[n % SLOTS], 16)

            for n, name in enumerate(names):
                if name == ("ada", 0, 2, 0):
                    for st_ in range(N_X):
                        sp.dma_start(x[:, :, seg(st_)], a["x"][st_]).then_inc(x_in, 16)
                if name == ("win", 0, 3):
                    for dst, src in late:
                        sp.dma_start(dst[:], src).then_inc(late_in, 16)
                if n >= SLOTS:
                    sp.wait_ge(*used_at[n - SLOTS])
                if name[0] == "ada":
                    _, t, k, j = name
                    c0 = (t % 3) * 2 * SLAB + j * SLAB
                    load(n, a["ada"][t // 3, k * P:(k + 1) * P, c0:c0 + SLAB])
                elif name[0] == "win":
                    load(n, a["win"][name[1], name[2]])
                elif name[0] == "wo":
                    load(n, a["wo"][name[1], name[2]])
                else:
                    load(n, a["ffn"][name[1], :, 0:ffn_width(name[1])])

            def pass_load(j, expert):
                load(MOE_SLAB0 + j, a["moe"][bass.ds(expert, 1), j].rearrange("e p n -> (e p) n")
                     if not isinstance(expert, int) else a["moe"][expert, j])

            def head(i, expert, before_loop=False):
                for j in range(SLOTS):
                    if before_loop:
                        sp.wait_ge(*used_at[MOE_SLAB0 + j - SLOTS])
                    else:
                        sp.wait_ge(lo_made, i * N_PS + (j - SLOTS + 1))
                    pass_load(j, expert)

            def rest(i, expert):
                for j in range(SLOTS, N_PS):
                    sp.wait_ge(lo_made, i * N_PS + (j - SLOTS + 1))
                    pass_load(j, expert)

            head(0, 0, before_loop=True)
            with sp.Fori(0, NE - 1) as i:
                rest(i, i)
                head(i + 1, i + 1)
            rest(NE - 1, NE - 1)

            def again(i):
                expert = sp.value_load(extra[0:1, bass.ds(i - (NE - 1), 1)], min_val=0, max_val=NE - 1)
                head(i, expert)
                rest(i, expert)

            extra_passes(sp, again)
            for i in range(2):
                sp.wait_ge(out_ready, 4 * (i + 1))
                sp.dma_start(a["out"][:, i * 4:(i + 1) * 4, :], h[:, i * 4:(i + 1) * 4, seg(LAT)]).then_inc(out_done, 16)
            sp.wait_ge(out_done, 32)

        @block.gpsimd
        def _(pool):
            o = Own(pool, pool_own)
            pool.memset(cond[:, :, :], 0.0).then_inc(cond_zero, 1)
            for L in range(DEPTH):
                pool.wait_ge(kk_in, L + 1)
                units = [(b, d) for b in query_blocks(L) for d in (FWD, BWD)]
                for u, (b, d) in enumerate(units):
                    bs = slice(b * P, (b + 1) * P)
                    if u == 1:
                        full(pool, ("kT", L) + state_steps(L)[-1])
                    if u >= 2:
                        was_b, was_d = units[u - 2]
                        full(pool, ("in", L, was_b, was_d) if incoming(was_d, was_b) is not None
                             else ("lv", L, was_b, was_d, NL - 1))
                    if d == FWD:
                        if u:
                            o.settle()
                        o.sig(pool.tensor_tensor(lowc(kd), kf[:, :, bs], kb[:, :, bs], ALU.add), kd_ready)
                    buf = levs[u % 2]
                    for l, half in enumerate(LEVELS):
                        g = g_of[d][:, :, bs].rearrange("p h (n t) -> p h n t", t=2 * half)
                        z = lowc(buf[:, l, :]).rearrange("p h (n t) -> p h n t", t=2 * half)
                        at = half - 1 if d == FWD else half
                        mid = g[:, :, :, at:at + 1].to_broadcast([P, RH, P // (2 * half), half])
                        o.sig(pool.tensor_tensor(z[:, :, :, half:], g[:, :, :, half:], mid, ALU.subtract))
                        o.sig(pool.tensor_tensor(z[:, :, :, 0:half], mid, g[:, :, :, 0:half], ALU.subtract))
                    z = lowc(buf[:, NL, :])
                    if d == FWD:
                        o.sig(pool.tensor_copy(z, gf[:, :, bs]), lev_in)
                    else:
                        end = tot[:, 1, :, b:b + 1].to_broadcast([P, RH, P])
                        o.sig(pool.tensor_tensor(z, end, gb[:, :, bs], ALU.subtract), lev_in)

        @block.tensor
        def _(pe):
            def open_tile(name):
                n = TL.number[name]
                if n >= BANKS:
                    pe.wait_ge(free[TL.consumer[n - BANKS]], TL.rank[n - BANKS])
                return banks[n % BANKS]

            def slab_in(name):
                n = SL[name]
                pe.wait_ge(slab_full[n % SLOTS], 16 * (n // SLOTS + 1))
                return ring[:, n % SLOTS, :]

            def close(m):
                m.then_inc(tile_full, 1)

            def project(name, slab, rhs, cols, w=P, at=0, ready=None):
                bank = open_tile(name)
                s = slab_in(slab)
                for k in range(KD):
                    if ready is not None:
                        pe.wait_ge(h_ready, ready + k + 1)
                    m = pe.matmul(bank[at:at + w, 0:cols], s[:, k * w:(k + 1) * w], rhs(k),
                                  start=(k == 0), stop=(k == KD - 1))
                close(m)

            def norm_sum(name, chunks, rhs, cols, sem_, base, stat):
                bank = open_tile(name)
                for k in range(chunks):
                    if sem_ is not None:
                        pe.wait_ge(sem_, base + k + 1)
                    m = pe.matmul(bank[:, 0:cols], stat[:, :], rhs(k), start=(k == 0), stop=(k == chunks - 1))
                close(m)

            def norm_beside(name, m_, cols, rhs, base):
                if m_ < KD // 2:
                    return
                bank = open_tile(name)
                for k in (2 * m_ - KD, 2 * m_ - KD + 1):
                    pe.wait_ge(sq_ready, base + k + 1)
                    m = pe.matmul(bank[:, 0:cols], ones[:, :], rhs(k), start=(k == 0), stop=(k == KD - 1))
                if m_ == KD - 1:
                    close(m)

            def modulation_half(t, half):
                if half == 0 and t:
                    pe.wait_ge(ada_taken, t)
                for k in range(4 * half, 4 * half + 4):
                    for n in range(2):
                        s = slab_in(("ada", t, k, n))
                        for j in range(2):
                            c0 = 32 * (2 * n + j)
                            m = pe.matmul(ada_bank[c0:c0 + 32, :], cond[:, k, :], s[:, j * 512:(j + 1) * 512],
                                          start=(k == 0), stop=(k == KD - 1), tile_position=(0, c0))
                        m.then_inc(ada_full if (k, n) == (KD - 1, 1) else slab_used, 1)

            def modulation_turn(t):
                pe.wait_ge(ada_taken, t + 1)
                if t:
                    pe.wait_ge(adaT_taken, t)
                for c in range(4):
                    m = pe.transpose(adaT_bank[:, c * P:(c + 1) * P], ada_sb[:, c * P:(c + 1) * P], ident[:, :])
                m.then_inc(adaT_full, 1)

            def fill(f):
                if f % 2 == 0 and f >= 2:
                    modulation_turn(f // 2)
                if f < 2 * (N_ADA_TILES - 1):
                    modulation_half(1 + f // 2, f % 2)

            n_kd = n_lev = 0
            pe.wait_ge(const_in, 16 * N_EARLY)
            pe.wait_ge(cond_ready, 1)
            for L in range(DEPTH):
                q0 = 0 if L == 0 else SEG
                nq = T - q0

                if L == 0:
                    modulation_half(0, 0)
                    norm_sum(("ss1", L), KD, lambda k: h[:, k, :], T, sq_ready, 16 * L, ones)
                    modulation_half(0, 1)
                    modulation_turn(0)
                for i in range(8):
                    project(("ff", L, i), ("win", L, i), lambda k: h[:, k, :], T,
                            ready=2 * KD * L if i == 0 else None)
                s0, s1 = slab_in(("win", L, 8)), slab_in(("win", L, 9))
                for b in range(NBLK):
                    bank = open_tile(("hi", L, b))
                    for k in range(KD):
                        s = (s0, s1)[k // 4]
                        m = pe.matmul(bank[:, 0:SEG], h[:, k, b * P:(b + 1) * P],
                                      s[:, (k % 4) * SEG:(k % 4 + 1) * SEG], start=(k == 0), stop=(k == KD - 1))
                    close(m)
                for i in range(4):
                    project(("hq", L, i), ("win", L, 10 + i), lambda k: h[:, k, q0:T], nq)
                for i in range(2):
                    project(("hg", L, i), ("win", L, 14 + i), lambda k: h[:, k, q0:T], nq)

                if L == 0:
                    pe.wait_ge(late_in, 16 * N_LATE)
                for i in range(2):
                    project(("dq", L, i), ("win", L, 16 + i), lambda k: h[:, k, q0:T], nq)
                project(("dkv", L), ("win", L, 18), lambda k: h[:, k, :], T)
                project(("kr", L), ("win", L, 19), lambda k: h[:, k, :], T, w=64, at=64)
                for i in range(2):
                    project(("fo", L, i), ("win", L, 20 + i), lambda k: h[:, k, q0:T], nq)

                pe.wait_ge(kk_ready, 2 * L + 2)
                for i, (d, b) in enumerate(state_steps(L)):
                    bank = open_tile(("kT", L, d, b))
                    kk = (kkf, kkb)[d]
                    for hh in range(RH):
                        m = pe.transpose(bank[:, hh * P:(hh + 1) * P], kk[:, hh, b * P:(b + 1) * P], ident[:, :])
                    close(m)
                    bank = open_tile(("st", L, d, b))
                    emptied(pe, ("kT", L, d, b))
                    for hh in range(RH):
                        m = pe.matmul(bank[:, hh * RV:(hh + 1) * RV], kt[i % 2][:, hh * P:(hh + 1) * P],
                                      hi[:, b, hh * RV:(hh + 1) * RV], start=True, stop=True)
                    close(m)
                    if L == 0 and i in (2, 5):
                        fill(i // 3)

                for b in query_blocks(L):
                    bank = open_tile(("diag", L, b))
                    n_kd += 1
                    pe.wait_ge(kd_ready, n_kd)
                    for hh in range(RH):
                        m = pe.matmul(bank[:, hh * P:(hh + 1) * P], kd[:, hh * P:(hh + 1) * P],
                                      rq[:, hh, b * P:(b + 1) * P], start=True, stop=True)
                    close(m)
                    for d in (FWD, BWD):
                        n_lev += 1
                        pe.wait_ge(lev_ready, n_lev)
                        unit = 2 * query_blocks(L).index(b) + d
                        buf = levs[unit % 2]
                        for l in range(NL):
                            bank = open_tile(("lv", L, b, d, l))
                            for hh in range(RH):
                                v = buf[:, l, hh * P:(hh + 1) * P]
                                m = pe.matmul(bank[:, hh * P:(hh + 1) * P], v, v, start=True, stop=True)
                            close(m)
                        if incoming(d, b) is not None:
                            i = state_steps(L).index((d, incoming(d, b)))
                            bank = open_tile(("in", L, b, d))
                            for hh in range(RH):
                                r0 = (hh % 2) * RV
                                m = pe.matmul(bank[r0:r0 + RV, (hh // 2) * P:(hh // 2 + 1) * P],
                                              st[:, i, hh * RV:(hh + 1) * RV], buf[:, NL, hh * P:(hh + 1) * P],
                                              start=True, stop=True)
                            close(m)
                        if L == 0:
                            fill(2 + unit)
                    bank = open_tile(("o", L, b))
                    emptied(pe, ("lv", L, b, BWD, NL - 1))
                    for hh in range(RH):
                        r0 = (hh % 2) * RV
                        m = pe.matmul(bank[r0:r0 + RV, (hh // 2) * P:(hh // 2 + 1) * P],
                                      hi[:, b, hh * RV:(hh + 1) * RV], sc[:, hh * P:(hh + 1) * P],
                                      start=True, stop=True)
                    close(m)
                if L == 0:
                    fill(2 * (N_ADA_TILES - 1))
                pe.wait_ge(lsq_ready, 3 * L + 3)
                norm_sum(("ssq", L), 2, lambda k: lsq[k][:, q0:T], nq, None, 0, ones)
                norm_sum(("sskv", L), 1, lambda k: lsq[2], T, None, 0, ones)
                for b in query_blocks(L):
                    bank = open_tile(("f1", L, b))
                    emptied(pe, ("fo", L, 1))
                    for c in range(2):
                        m = pe.matmul(bank[:, c * SEG:(c + 1) * SEG], fo[:, c, b * P:(b + 1) * P], dftc[:, :],
                                      start=True, stop=True)
                    close(m)
                for s in query_segments(L):
                    for c in range(2):
                        bank = open_tile(("f2", L, s, c))
                        emptied(pe, ("f1", L, 2 * s + 1))
                        for t in range(2):
                            for part in range(2):
                                m = pe.matmul(bank[:, 0:SEG],
                                              f1[:, 2 * s + t, c * SEG + part * P:c * SEG + (part + 1) * P],
                                              dftt[:, part, t, :], start=(t == 0 and part == 0),
                                              stop=(t == 1 and part == 1))
                        close(m)
                pe.wait_ge(k_ready, 3 * L + 3)
                wuq = [slab_in(("win", L, 22)), slab_in(("win", L, 23))]
                for hh in range(HEADS):
                    bank = open_tile(("q", L, hh))
                    for k in range(2):
                        m = pe.matmul(bank[:, 0:nq], wuq[k][:, hh * P:(hh + 1) * P], dq[:, k, q0:T],
                                      start=(k == 0), stop=(k == 1))
                    close(m)
                wukv = slab_in(("win", L, 24))
                for j in range(HEADS // 2):
                    bank = open_tile(("kn", L, j))
                    m = pe.matmul(bank[:, :], wukv[:, j * P:(j + 1) * P], dkv[:, :], start=True, stop=True)
                    close(m)
                for b in range(NBLK):
                    bank = open_tile(("v", L, b))
                    m = pe.matmul(bank[:, :], dkv[:, b * P:(b + 1) * P], wukv[:, 512:1024], start=True, stop=True)
                    close(m)
                for i in range(2):
                    norm_sum(("rms", L, i), 1, lambda k: osq[:, i, q0:T], nq, rec_ready, 4 * L + i, ones_blk)
                units = attention_units(L)
                n_prob0 = 0 if L == 0 else 2 * len(attention_units(0))
                pe.wait_ge(kr_spread, L + 1)
                emptied(pe, ("q", L, HEADS - 1))
                emptied(pe, ("v", L, NBLK - 1))
                for i in range(len(units) + 2):
                    if i < len(units):
                        hh, s = units[i]
                        for qb in range(2):
                            bank = open_tile(("s", L, i, qb))
                            c0 = s * SEG + qb * P
                            m = pe.matmul(bank[:, 0:P * len(key_blocks(s))], qall[:, hh, c0:c0 + P],
                                          kall[:, hh, 0:P * len(key_blocks(s))], start=True, stop=True)
                            close(m)
                    if 1 <= i <= len(units):
                        u = i - 1
                        pe.wait_ge(prob_ready, n_prob0 + 2 * (u + 1))
                        for k2 in range(len(key_blocks(units[u][1])) // 2):
                            bank = open_tile(("pT", L, u, k2))
                            for kk in range(2):
                                for qb in range(2):
                                    k0 = (2 * k2 + kk) * P
                                    m = pe.transpose(bank[:, kk * SEG + qb * P:kk * SEG + (qb + 1) * P],
                                                     prob[:, 2 * (u % 2) + qb, k0:k0 + P], ident[:, :])
                            close(m)
                    if i >= 2:
                        u = i - 2
                        hh, s = units[u]
                        kbs = key_blocks(s)
                        bank = open_tile(("pv", L, u))
                        emptied(pe, ("pT", L, u, len(kbs) // 2 - 1))
                        r0 = (hh % 2) * DV
                        for kb_ in kbs:
                            m = pe.matmul(bank[r0:r0 + DV, 0:SEG], vtok[:, kb_, hh * DV:(hh + 1) * DV],
                                          pt[:, u % 2, kb_ * SEG:(kb_ + 1) * SEG],
                                          start=(kb_ == 0), stop=(kb_ == kbs[-1]))
                        close(m)
                emptied(pe, ("pv", L, len(units) - 1))
                for m_ in range(KD):
                    project(("wo", L, m_), ("wo", L, m_), lambda k: mix[:, k, q0:T], nq)
                    norm_beside(("ss2", L), m_, nq, lambda k: h[:, k, q0:T], 16 * L + 8)
                if L == 0:
                    for name, slabs in FFN_TILES:
                        bank = open_tile(name)
                        down = name[0] == "dn"
                        act_hi, act_lo = (hid_hi, hid_lo) if down else (h_hi, h_lo)
                        chunks = KH if down else KD
                        for k in range(chunks):
                            n = slabs[k // 8]
                            if k % 8 == 0:
                                pe.wait_ge(ffn_lo, n + 1)
                            if name == ("g", 0):
                                pe.wait_ge(h_lo_made, k + 1)
                            if down and name[2] == 0:
                                pe.wait_ge(hid_lo_made, name[1] * KH + k + 1)
                            c = slice((k % 8) * P, (k % 8 + 1) * P)
                            w_h, w_l = f_hi[:, n % FFN_PARTS, c], f_lo[:, n % FFN_PARTS, c]
                            pe.matmul(bank[:, :], w_l, act_hi[:, k, :], start=(k == 0), stop=False)
                            pe.matmul(bank[:, :], w_h, act_hi[:, k, :], start=False, stop=False)
                            m = pe.matmul(bank[:, :], w_h, act_lo[:, k, :], start=False, stop=(k == chunks - 1))
                        close(m)
                        if name[:2] == ("dn", 1):
                            norm_beside(("ss1", 1), name[2], T, lambda k: h[:, k, :], 16)

            bank = open_tile(("rt",))
            pe.wait_ge(h_ready, KD * 2 * DEPTH)
            for b in range(2):
                for k in range(KD):
                    m = pe.matmul(bank[:, b * NE:(b + 1) * NE], h[:, k, SEG + b * P:SEG + (b + 1) * P],
                                  router[:, k, :], start=(k == 0), stop=(k == KD - 1))
            close(m)
            for j in range(4):
                bank = open_tile(("ht", j))
                for c in range(4):
                    b, k = divmod(4 * j + c, KD)
                    m = pe.transpose(bank[:, c * P:(c + 1) * P], h[:, k, SEG + b * P:SEG + (b + 1) * P], ident[:, :])
                close(m)
            pe.wait_ge(gates_ready, 1)
            bank = open_tile(("rank",))
            for c, parts in enumerate((((before, 0),), ((ones, 0), (before, 1)), ((ones, 0), (ones, 1)))):
                for n, (w, b) in enumerate(parts):
                    m = pe.matmul(bank[:, c * NE:(c + 1) * NE], w[:, :], one_hot[:, b, :],
                                  start=(n == 0), stop=(n == len(parts) - 1))
            close(m)

            def gather(opened, j):
                for c in range(4):
                    for b in range(2):
                        m = pe.matmul(opened[:, c * P:(c + 1) * P], ht[:, b, (4 * j + c) * P:(4 * j + c + 1) * P],
                                      sel[:, b, :], start=(b == 0), stop=(b == 1))
                close(m)

            emptied(pe, ("ht", 3))
            pe.wait_ge(sel_ready, 1)
            for j in range(2):
                gather(open_tile(("ga0", j)), j)
            pe.wait_ge(free["act"], BEFORE["act"])
            pe.wait_ge(free["dve"], BEFORE["dve"])

            def pe_pass(i):
                def pass_open(name):
                    at = EX_AT[name]
                    if at >= EX_BANKS:
                        pass_emptied(pe, EXPERT_TILES[at - EX_BANKS][0], i)
                    else:
                        was = max(q for q in range(N_EX) if q % EX_BANKS == at % EX_BANKS)
                        c = EXPERT_TILES[was][1]
                        pe.wait_ge(free[c], i * EX[c] + (BEFORE[c] - EX[c] + rank_in(c, was)))
                    return banks[at % EX_BANKS]

                def pass_slab(slab):
                    n = PASS_SLABS.index(slab)
                    pe.wait_ge(lo_made, i * N_PS + (n + 1))
                    return w_hi[:, n % PARTS, :], w_lo[:, n % PARTS, :]

                def product(out, a_hi, a_lo, w, cols, start, stop):
                    pe.matmul(out, a_hi, w[1][:, cols], start=start, stop=False)
                    pe.matmul(out, a_hi, w[0][:, cols], start=False, stop=False)
                    return pe.matmul(out, a_lo, w[0][:, cols], start=False, stop=stop)

                bank = pass_open(("selT",))
                for b in range(2):
                    m = pe.transpose(bank[:, b * P:(b + 1) * P], selg[:, b, :], ident[:, :])
                close(m)
                pe.wait_ge(free["dve"], i * EX["dve"] + (BEFORE["dve"] - EX["dve"]
                                                         + rank_in("dve", EX_AT[("ga", 1)])))
                for r in range(NR + 1):
                    if r < NR:
                        w = range_width(r)
                        for mat in "gu":
                            bank = pass_open((mat, r))
                            for part in range(KD * w // SLAB):
                                s = pass_slab((mat, r, part))
                                for c in range(SLAB // w):
                                    k = part * (SLAB // w) + c
                                    m = product(bank[:, 0:w], xe_hi[:, k, :], xe_lo[:, k, :], s,
                                                slice(c * w, (c + 1) * w), k == 0, k == KD - 1)
                                if closes((mat, r, part)) is None:
                                    m.then_inc(slab_used, 1)
                            close(m)
                    if r:
                        w = range_width(r - 1)
                        bank = pass_open(("hT", r - 1))
                        pass_emptied(pe, ("u", r - 1), i)
                        for c in range(w // P):
                            m = pe.transpose(bank[:, c * P:(c + 1) * P], hs[:, (r - 1) % 2, c * P:(c + 1) * P],
                                             ident[:, :])
                        close(m)
                acc = [pass_open(("dn", n)) for n in range(2)]
                for k in range(KF):
                    s = pass_slab(("dn", k))
                    if k % 4 == 0:
                        pass_emptied(pe, ("hT", k // 4), i)
                    for n in range(2):
                        m = product(acc[n][:, :], hT_hi[:, k, :], hT_lo[:, k, :], s,
                                    slice(n * 512, (n + 1) * 512), k == 0, k == KF - 1)
                        if k == KF - 1:
                            close(m)
                    if k < KF - 1:
                        m.then_inc(slab_used, 1)
                pe.wait_ge(sel_ready, i + 2)
                for j in range(2):
                    gather(pass_open(("ga", j)), j)
                pass_emptied(pe, ("dn", 0), i)
                pass_emptied(pe, ("dn", 1), i)
                for j in range(4):
                    bank = pass_open(("y", j))
                    for c in range(2):
                        m = pe.matmul(bank[:, c * SEG:(c + 1) * SEG], ye[:, (2 * j + c) * P:(2 * j + c + 1) * P],
                                      selt[:, :], start=True, stop=True)
                    close(m)

            passes(pe, pe_pass)
            for k in range(KD):
                pe.wait_ge(sq_ready, 32 + k + 1)
                m = pe.matmul(banks[0][:, 0:SEG], ones[:, :], h[:, k, seg(LAT)], start=(k == 0), stop=(k == KD - 1))
            m.then_inc(final_full, 1)

        @block.scalar
        def _(act):
            o = Own(act, act_own)
            n_sd = 0
            n_lev = 0

            def root(cols):
                nonlocal n_sd
                n_sd += 1
                act.wait_ge(var_ready, n_sd)
                o.sig(act.activation(msq[:, 0:cols], msq[:, 0:cols], ACT.Sqrt), sd_ready)

            def ffn_high(n):
                raw = SL[("ffn", n)]
                act.wait_ge(slab_full[raw % SLOTS], 16 * (raw // SLOTS + 1))
                w = ffn_width(n)
                o.sig(act.activation(f_hi[:, n % FFN_PARTS, 0:w], ring[:, raw % SLOTS, 0:w], ACT.Copy), ffn_hi)

            def affine(layer, base, n0, segs, halve=False):
                act.wait_ge(mods_ready, 2 * layer + (1 if base == 0 else 2))
                for k in range(KD):
                    act.wait_ge(xn_ready, n0 + k + 1)
                    for s in segs:
                        ins = act.activation(h[:, k, seg(s)], h[:, k, seg(s)], ACT.Identity,
                                             bias=mods[:, layer, s, base + k:base + k + 1],
                                             scale=mods[:, layer, s, base + KD + k:base + KD + k + 1])
                        o.sig(ins, h_ready if s == LAT else None)
                    if halve:
                        o.settle()
                        o.sig(act.activation(h_hi[:, k, :], h[:, k, :], ACT.Copy), h_hi_made)

            def take_modulation(t):
                act.wait_ge(ada_full, t + 1)
                if t:
                    act.wait_ge(adaT_full, t)
                o.sig(act.activation(ada_sb[:, :], ada_bank[:, :], ACT.Copy), ada_taken)

            act.wait_ge(const_in, 16 * N_EARLY)
            act.wait_ge(cond_zero, 1)
            o.sig(act.activation(cond[:, :, 0:2], craw[:, :, :], ACT.Silu), cond_ready)
            act.wait_ge(lb_in, 1)
            o.sig(act.activation(lbt[:, 1, :, :], lbt[:, 0, :, :], ACT.Exp), lb_exp)
            for L in range(DEPTH):
                q0 = 0 if L == 0 else SEG
                nq = T - q0
                root(T)
                if L == 0:
                    take_modulation(0)
                affine(L, 0, 16 * L, (CTX, LAT))
                for i in range(8):
                    bank = full(act, ("ff", L, i))
                    o.sig(act.activation(g_of[i // 4][:, i % 4, :], bank[:, :], ACT.Sigmoid), free["act"])
                for i in range(4):
                    bank = full(act, ("hq", L, i))
                    o.sig(act.activation(rq[:, i, q0:T], bank[:, 0:nq], ACT.Silu), free["act"])
                for i in range(2):
                    bank = full(act, ("hg", L, i))
                    o.sig(act.activation(hg[:, i, q0:T], bank[:, 0:nq], ACT.Silu), free["act"])
                for d in (FWD, BWD):
                    act.wait_ge(f_ready, 8 * L + 4 * (d + 1))
                    o.sig(act.activation(g_of[d], g_of[d], ACT.Ln), g_ready)
                act.wait_ge(kk_in, L + 1)
                o.sig(act.activation(kkf, kkf, ACT.Exp), kk_exp)
                o.sig(act.activation(kkb, gb, ACT.Exp), kk_exp)
                o.sig(act.activation(tot[:, 2:4, :, :], tot[:, 0:2, :, :], ACT.Exp), kk_exp)
                full(act, ("fo", L, 1))
                for i in range(2):
                    bank = full(act, ("dq", L, i))
                    o.sig(act.activation(dq[:, i, q0:T], bank[:, 0:nq], ACT.Copy), free["act"])
                bank = full(act, ("dkv", L))
                o.sig(act.activation(dkv, bank[:, :], ACT.Copy), free["act"])
                for i in range(2):
                    bank = full(act, ("fo", L, i))
                    o.sig(act.activation(fo[:, i, q0:T], bank[:, 0:nq], ACT.Copy), free["act"])
                for i, (d, b) in enumerate(state_steps(L)):
                    bank = full(act, ("kT", L, d, b))
                    if i < 2 and i == 0:
                        o.settle()
                    o.sig(act.activation(kt[i % 2][:, :], bank[:, :], ACT.Copy), free["act"])
                act.wait_ge(kr_ready, L + 1)
                for i in range(2):
                    o.sig(act.activation(lsq[i][:, q0:T], dq[:, i, q0:T], ACT.Square), lsq_ready)
                o.sig(act.activation(lsq[2], dkv, ACT.Square), lsq_ready)
                units = [(b, d) for b in query_blocks(L) for d in (FWD, BWD)]
                for u in range(len(units)):
                    n_lev += 1
                    act.wait_ge(lev_in, n_lev)
                    o.sig(act.activation(levs[u % 2][:, :, :], levs[u % 2][:, :, :], ACT.Exp), lev_exp)
                    if L == 0 and u % 2 == 0:
                        take_modulation(1 + u // 2)
                if L == 0:
                    take_modulation(N_ADA_TILES - 1)
                root(nq)
                for b in query_blocks(L):
                    bank = full(act, ("f1", L, b))
                    o.sig(act.activation(f1[:, b, :], bank[:, :], ACT.Copy), free["act"])
                root(T)
                o.sig(act.activation(kall[64:128, :, :], kr[64:128, :].unsqueeze(1).to_broadcast([64, HEADS, T]),
                                     ACT.Copy), kr_spread)
                for hh in range(HEADS):
                    bank = full(act, ("q", L, hh))
                    o.sig(act.activation(qall[0:NOPE, hh, q0:T], bank[0:NOPE, 0:nq], ACT.Copy), q_nope)
                for j in range(HEADS // 2):
                    bank = full(act, ("kn", L, j))
                    o.sig(act.activation(kall[0:NOPE, 2 * j, :], bank[0:64, :], ACT.Copy))
                    o.sig(act.activation(kall[0:NOPE, 2 * j + 1, :], bank[64:128, :], ACT.Copy), free["act"])
                for b in range(NBLK):
                    bank = full(act, ("v", L, b))
                    o.sig(act.activation(vtok[:, b, :], bank[:, :], ACT.Copy), free["act"])
                for i in range(2):
                    root(nq)
                n0 = 0 if L == 0 else 2 * len(attention_units(0))
                units = attention_units(L)
                for i in range(len(units) + 1):
                    for qb in range(2 if i < len(units) else 0):
                        bank = full(act, ("s", L, i, qb))
                        act.wait_ge(neg_max, n0 + 2 * i + qb + 1)
                        c = 2 * i + qb
                        nk = P * len(key_blocks(units[i][1]))
                        o.sig(act.activation(prob[:, 2 * (i % 2) + qb, 0:nk], bank[:, 0:nk], ACT.Exp,
                                             bias=smax[:, 1, c:c + 1], scale=ATT_SCALE,
                                             accum_out=smax[:, 2, c:c + 1]), free["act"])
                    if i >= 1:
                        u = i - 1
                        for k2 in range(len(key_blocks(units[u][1])) // 2):
                            bank = full(act, ("pT", L, u, k2))
                            o.sig(act.activation(pt[:, u % 2, k2 * 512:(k2 + 1) * 512], bank[:, :], ACT.Copy),
                                  free["act"])
                if L == 0:
                    for n in range(FFN_PARTS):
                        ffn_high(n)
                root(nq)
                affine(L, 3 * KD, 16 * L + 8, query_segments(L), halve=(L == 0))
                if L == 0:
                    for name, slabs in FFN_TILES:
                        bank = full(act, name)
                        for n in slabs:
                            if n + FFN_PARTS < N_FFN_SLABS:
                                ffn_high(n + FFN_PARTS)
                        if name[0] == "g":
                            k = name[1]
                            if k >= 3:
                                act.wait_ge(hid_lo_made, k - 2)
                            o.sig(act.activation(hid[:, k % 3, :], bank[:, :], ACT.Silu), free["act"])
                        if name[0] == "u":
                            k = name[1]
                            emptied(act, name)
                            o.sig(act.activation(hid_hi[:, k % KH, :], hid[:, k % 3, :], ACT.Copy), hid_hi_made)
            act.wait_ge(top_in, 1)
            o.sig(act.activation(gt[:, 1, :, 0:1], gt[:, 0, :, 0:1], ACT.Exp), top_exp)
            for j in range(4):
                bank = full(act, ("ht", j))
                o.sig(act.activation(ht[:, j // 2, (j % 2) * 512:(j % 2 + 1) * 512], bank[:, :], ACT.Copy),
                      free["act"])
            four = lambda v: v.rearrange("p (a b) -> p a b", a=4)
            for j in range(2):
                bank = full(act, ("ga0", j))
                o.sig(act.activation(xe_hi[:, 4 * j:4 * j + 4, :], four(bank[:, :]), ACT.Copy), part_hi)

            def act_pass(i):
                def high(n):
                    raw = MOE_SLAB0 + n
                    act.wait_ge(slab_full[raw % SLOTS], i * (16 * N_PS // SLOTS) + 16 * (raw // SLOTS + 1))
                    if n >= PARTS:
                        pass_used(act, n - PARTS, i)
                    else:
                        pass_used(act, N_PS + n - PARTS, i - 1)
                    act.activation(w_hi[:, n % PARTS, :], ring[:, raw % SLOTS, :], ACT.Copy).then_inc(hi_made, 1)

                for n in range(PARTS):
                    high(n)
                for n, slab in enumerate(PASS_SLABS):
                    if n + PARTS < N_PS:
                        high(n + PARTS)
                    tile = closes(slab)
                    if tile is not None and tile[0] == "g":
                        r = tile[1]
                        w = range_width(r)
                        bank = pass_full(act, ("g", r), i)
                        if r >= 2:
                            pass_emptied(act, ("u", r - 2), i)
                        else:
                            act.wait_ge(free["dve"], i * EX["dve"] + (BEFORE["dve"] - EX["dve"]
                                                                      + rank_in("dve", EX_AT[("u", NR - 2 + r)])))
                        act.activation(sg[:, r % 2, 0:w], bank[:, 0:w], ACT.Silu).then_inc(free["act"], 1)
                    turned = None
                    if tile is not None and tile[0] == "u" and tile[1]:
                        turned = tile[1] - 1
                    if slab == ("dn", 0):
                        turned = NR - 1
                    if turned is not None:
                        w = range_width(turned)
                        bank = pass_full(act, ("hT", turned), i)
                        to = hT_hi[:, 4 * turned:4 * turned + w // P, :]
                        act.activation(to, bank[:, 0:w].rearrange("p (a b) -> p a b", b=P),
                                       ACT.Copy).then_inc(part_hi, 1)
                bank = pass_full(act, ("dn", 0), i)
                act.activation(ye[:, 0:512], bank[:, :], ACT.Copy).then_inc(free["act"], 1)
                for j in range(2):
                    bank = pass_full(act, ("ga", j), i)
                    act.activation(xe_hi[:, 4 * j:4 * j + 4, :], four(bank[:, :]), ACT.Copy).then_inc(part_hi, 1)

            passes(act, act_pass)
            root(SEG)

        @block.vector
        def _(dve):
            o = Own(dve, dve_own)
            n_sd = 0

            def norm(bank, cols, width, tile_sem=True):
                nonlocal n_sd
                n_sd += 1
                o.sig(dve.tensor_scalar(msq[:, 0:cols], bank[:, 0:cols], 1.0 / width, EPS, ALU.mult, ALU.add),
                      var_ready)
                dve.wait_ge(sd_ready, n_sd)
                if tile_sem:
                    o.sig(dve.reciprocal(rstd[:, 0:cols], msq[:, 0:cols]), free["dve"])
                else:
                    o.sig(dve.reciprocal(rstd[:, 0:cols], msq[:, 0:cols]))
                o.settle()

            def square(k, cols):
                o.sig(dve.tensor_tensor(h[:, k, cols], x[:, k, cols], x[:, k, cols], ALU.mult), sq_ready)

            def squares(cols):
                for k in range(KD):
                    square(k, cols)

            def ffn_low(n):
                raw = SL[("ffn", n)]
                w = ffn_width(n)
                dve.wait_ge(ffn_hi, n + 1)
                o.sig(dve.tensor_tensor(f_lo[:, n % FFN_PARTS, 0:w], ring[:, raw % SLOTS, 0:w],
                                        plain(f_hi[:, n % FFN_PARTS, 0:w]), ALU.subtract), ffn_lo)

            plain = lambda v: v.bitcast(F32)

            def scaled(cols, n):
                for k in range(KD):
                    o.sig(dve.tensor_tensor(h[:, k, cols], x[:, k, cols], rstd[:, 0:n], ALU.mult), xn_ready)

            def turned_modulation(t):
                layer, b = divmod(t, 3)
                dve.wait_ge(adaT_full, t + 1)
                bank = adaT_bank[:, :].rearrange("p (c j s) -> p c j s", c=4, j=4)
                for s in range(2):
                    to = mods[:, layer, s, b * 16:(b + 1) * 16].rearrange("p (j c) -> p c j", j=4)
                    add = bada[:, layer, b * 16:(b + 1) * 16].rearrange("p (j c) -> p c j", j=4)
                    o.sig(dve.tensor_tensor(to, bank[:, :, :, s], add, ALU.add), adaT_taken if s else None)
                if b != 1:
                    o.settle()
                    c0 = KD if b == 0 else 4 * KD
                    v = mods[:, layer, :, c0:c0 + KD]
                    o.sig(dve.tensor_scalar(v, v, 1.0, None, ALU.add), mods_ready)

            dve.wait_ge(const_in, 16 * N_EARLY)
            o.sig(dve.tensor_tensor(lbt[:, 2, 0, :], lbl[:, 0, :], lbl[:, 1, :], ALU.max))
            o.settle()
            for i in range(DEPTH):
                last = dve.tensor_tensor(lbt[:, 0, i, :], lbl[:, i, :], lbt[:, 2, 0, :], ALU.subtract)
                o.sig(last, lb_in if i == DEPTH - 1 else None)
            dve.wait_ge(lb_exp, 1)
            o.sig(dve.tensor_tensor(lbt[:, 2, 1, :], lbt[:, 1, 0, :], lbt[:, 1, 1, :], ALU.add))
            o.settle()
            o.sig(dve.reciprocal(lbt[:, 3, 0, :], lbt[:, 2, 1, :]))
            o.settle()
            for i in range(DEPTH):
                o.sig(dve.tensor_tensor(lbt[:, 0, i, :], lbt[:, 1, i, :], lbt[:, 3, 0, :], ALU.mult))
            o.settle()
            o.sig(dve.tensor_tensor(lb[:, 0, 0, :], lbt[:, 0, 0, :], lbt[:, 0, 0, :], ALU.subtract))
            o.sig(dve.tensor_tensor(lbt[:, 3, 1, :], lbt[:, 0, 0, :], lbt[:, 0, 1, :], ALU.add))
            o.settle()
            o.sig(dve.tensor_tensor(lb[:, 0, 1, :], lbt[:, 3, 1, :], lbt[:, 0, 0, :], ALU.subtract))
            o.settle()
            o.sig(dve.tensor_scalar(lb[:, 1, :, :], lb[:, 0, :, :], -1.0, 1.0, ALU.mult, ALU.add))
            o.settle()

            for L in range(DEPTH):
                q0 = 0 if L == 0 else SEG
                nq = T - q0
                qs = slice(q0, T)
                if L == 0:
                    dve.wait_ge(x_in, 16 * N_X)
                    squares(slice(0, T))
                norm(full(dve, ("ss1", L)), T, D)
                scaled(slice(0, T), T)
                if L == 0:
                    turned_modulation(0)

                for i in range(8):
                    d, hh = divmod(i, 4)
                    emptied(dve, ("ff", L, i))
                    f = g_of[d][:, hh, :]
                    o.sig(dve.tensor_scalar(f, f, lb[:, 1, L, i:i + 1], lb[:, 0, L, i:i + 1], ALU.mult, ALU.add))
                    o.settle()
                    o.sig(dve.tensor_scalar(k_of[d][:, hh, :], f, -1.0, 1.0, ALU.mult, ALU.add), f_ready)
                for b in range(NBLK):
                    bank = full(dve, ("hi", L, b))
                    o.sig(dve.tensor_copy(hi[:, b, :], bank[:, 0:SEG]), free["dve"])
                if L == 0:
                    dve.wait_ge(late_in, 16 * N_LATE)
                dve.wait_ge(g_ready, 2 * L + 1)
                for hh in range(RH):
                    o.sig(dve.tensor_tensor_scan(gf[:, hh, :], reset[:, :], gf[:, hh, :], 0.0, ALU.mult, ALU.add))
                dve.wait_ge(g_ready, 2 * L + 2)
                for hh in range(RH):
                    o.sig(dve.tensor_tensor_scan(kkb[:, hh, :], reset[:, :], gb[:, hh, :], 0.0, ALU.mult, ALU.add))
                o.settle()
                ends = lambda v: v.rearrange("p h (b t) -> p h b t", t=P)[:, :, :, P - 1]
                o.sig(dve.tensor_copy(tot[:, 0, :, :], ends(gf)))
                o.sig(dve.tensor_copy(tot[:, 1, :, :], ends(kkb)))
                o.sig(dve.tensor_tensor(gb, kkb, gb, ALU.subtract))
                o.settle()
                blocks = lambda v: v.rearrange("p h (b t) -> p (h b) t", t=P)
                t0 = tot[:, 0, :, :].rearrange("p h b -> p (h b)").unsqueeze(2).to_broadcast([P, RH * NBLK, P])
                o.sig(dve.tensor_tensor(blocks(kkf), t0, blocks(gf), ALU.subtract), kk_in)
                dve.wait_ge(kk_exp, 3 * L + 3)
                o.sig(dve.tensor_tensor(kkf, kkf, kf, ALU.mult), kk_ready)
                o.sig(dve.tensor_tensor(kkb, kkb, kb, ALU.mult), kk_ready)
                full(dve, ("fo", L, 1))
                bank = full(dve, ("kr", L))
                v, part = kr[64:96, :], lsq[0][64:96, :]
                o.sig(dve.tensor_tensor(v, bank[64:96, :], rope_t[64:96, :], ALU.mult))
                o.sig(dve.tensor_tensor(part, bank[96:128, :], rope_t[96:128, :], ALU.mult), free["dve"])
                o.settle()
                o.sig(dve.tensor_tensor(v, v, part, ALU.add))
                o.settle()
                o.sig(dve.tensor_copy(kr[96:128, :], v), kr_ready)
                steps = state_steps(L)
                for i, (d, b) in enumerate(steps):
                    bank = full(dve, ("st", L, d, b))
                    if incoming(d, b) is None:
                        o.sig(dve.tensor_copy(st[:, i, :], bank[:, 0:RH * RV]), free["dve"])
                        continue
                    was = steps.index((d, incoming(d, b)))
                    o.settle()
                    for hh in range(RH):
                        c = slice(hh * RV, (hh + 1) * RV)
                        o.sig(dve.scalar_tensor_tensor(st[:, i, c], st[:, was, c], tot[:, 2 + d, hh, b:b + 1],
                                                       bank[:, c], ALU.mult, ALU.add),
                              free["dve"] if hh == RH - 1 else None)
                o.settle()
                units = [(b, d) for b in query_blocks(L) for d in (FWD, BWD)]

                def decayed(u):
                    b, d = units[u]
                    bs = slice(b * P, (b + 1) * P)
                    dve.wait_ge(lev_exp, (0 if L == 0 else 2 * len(query_blocks(0))) + u + 1)
                    late, early = (rq, kf) if d == FWD else (kb, rq)
                    buf = levs[u % 2]
                    for l, half in enumerate(LEVELS):
                        z = lowc(buf[:, l, :]).rearrange("p h (n t) -> p h n t", t=2 * half)
                        for sl, by in ((slice(half, 2 * half), late), (slice(0, half), early)):
                            w = by[:, :, bs].rearrange("p h (n t) -> p h n t", t=2 * half)
                            o.sig(dve.tensor_tensor(z[:, :, :, sl], z[:, :, :, sl], w[:, :, :, sl], ALU.mult))
                    z = lowc(buf[:, NL, :])
                    o.sig(dve.tensor_tensor(z, z, rq[:, :, bs], ALU.mult), lev_ready)

                def merged(u):
                    b, d = units[u]
                    to = mix[:, 6:8, b * P:(b + 1) * P]
                    if d == FWD:
                        bank = full(dve, ("diag", L, b))
                        o.settle()
                        o.sig(dve.tensor_copy(sc, bank[:, :]), free["dve"])
                    for l in range(NL):
                        bank = full(dve, ("lv", L, b, d, l))
                        m = mask[:, d, l, :].unsqueeze(1).to_broadcast([P, RH, P])
                        o.settle()
                        o.sig(dve.copy_predicated(lowc(sc), m, lowc(bank)), free["dve"])
                    if incoming(d, b) is not None:
                        bank = full(dve, ("in", L, b, d))
                        part = bank[:, 0:2 * P].rearrange("p (a b) -> p a b", a=2)
                        if d == FWD or incoming(FWD, b) is None:
                            o.sig(dve.tensor_copy(to, part), free["dve"])
                        else:
                            o.settle()
                            o.sig(dve.tensor_tensor(to, to, part, ALU.add), free["dve"])
                    if L == 0 and u % 2 == 1:
                        turned_modulation(1 + u // 2)

                def within(b):
                    bank = full(dve, ("o", L, b))
                    to = mix[:, 6:8, b * P:(b + 1) * P]
                    o.settle()
                    o.sig(dve.tensor_tensor(to, to, bank[:, 0:2 * P].rearrange("p (a b) -> p a b", a=2), ALU.add),
                          free["dve"])

                decayed(0)
                for u in range(1, len(units) + 1):
                    merged(u - 1)
                    if u < len(units):
                        decayed(u)
                    if u % 2 == 0:
                        within(units[u - 1][0])
                if L == 0:
                    turned_modulation(N_ADA_TILES - 1)

                norm(full(dve, ("ssq", L)), nq, Q_RANK)
                for i in range(2):
                    emptied(dve, ("dq", L, i))
                    v = dq[:, i, qs]
                    o.sig(dve.scalar_tensor_tensor(v, v, gains[:, L, i:i + 1], rstd[:, 0:nq], ALU.mult, ALU.mult),
                          k_ready)
                norm(full(dve, ("sskv", L)), T, KV_RANK)
                emptied(dve, ("dkv", L))
                o.sig(dve.scalar_tensor_tensor(dkv, dkv, gains[:, L, 2:3], rstd[:, :], ALU.mult, ALU.mult), k_ready)
                for i in range(2):
                    o.sig(dve.tensor_tensor(osq[:, i, qs], mix[:, 6 + i, qs], mix[:, 6 + i, qs], ALU.mult), rec_ready)
                for s in query_segments(L):
                    for c in range(2):
                        bank = full(dve, ("f2", L, s, c))
                        o.sig(dve.tensor_copy(mix[:, 4 + c, seg(s)], bank[:, 0:SEG]), free["dve"])
                for hh in range(HEADS):
                    bank = full(dve, ("q", L, hh))
                    dve.wait_ge(q_nope, HEADS * L + hh + 1)
                    o.sig(dve.tensor_tensor(qall[64:128, hh, qs], bank[64:128, 0:nq], rope_t[64:128, qs], ALU.mult),
                          free["dve"])
                for i in range(2):
                    norm(full(dve, ("rms", L, i)), nq, RV)
                    v = mix[:, 6 + i, qs]
                    o.sig(dve.scalar_tensor_tensor(v, v, gains[:, L, 3:4], rstd[:, 0:nq], ALU.mult, ALU.mult))
                    o.settle()
                    o.sig(dve.tensor_tensor(v, v, hg[:, i, qs], ALU.mult), rec_ready)

                units = attention_units(L)
                n0 = 0 if L == 0 else 2 * len(attention_units(0))
                for i in range(len(units) + 2):
                    if i < len(units):
                        for qb in range(2):
                            bank = full(dve, ("s", L, i, qb))
                            c = 2 * i + qb
                            nk = P * len(key_blocks(units[i][1]))
                            o.sig(dve.tensor_reduce(smax[:, 0, c:c + 1], bank[:, 0:nk], AX.X, ALU.max))
                            o.settle()
                            o.sig(dve.tensor_scalar(smax[:, 1, c:c + 1], smax[:, 0, c:c + 1], -ATT_SCALE, None,
                                                    ALU.mult), neg_max)
                        for qb in range(2):
                            c = 2 * i + qb
                            emptied(dve, ("s", L, i, qb))
                            o.sig(dve.reciprocal(smax[:, 3, c:c + 1], smax[:, 2, c:c + 1]))
                            o.settle()
                            nk = P * len(key_blocks(units[i][1]))
                            v = prob[:, 2 * (i % 2) + qb, 0:nk]
                            o.sig(dve.tensor_scalar(v, v, smax[:, 3, c:c + 1], None, ALU.mult), prob_ready)
                    if i >= 2:
                        u = i - 2
                        hh, s = units[u]
                        bank = full(dve, ("pv", L, u))
                        r0 = (hh % 2) * DV
                        o.sig(dve.tensor_copy(mix[r0:r0 + DV, hh // 2, seg(s)], bank[r0:r0 + DV, 0:SEG]),
                              free["dve"])

                def residual(bank, m, c0):
                    segs = query_segments(L)
                    for s in segs:
                        f0 = s * SEG - q0
                        o.sig(dve.scalar_tensor_tensor(x[:, m, seg(s)], bank[:, f0:f0 + SEG],
                                                       mods[:, L, s, c0 + m:c0 + m + 1], x[:, m, seg(s)],
                                                       ALU.mult, ALU.add),
                              free["dve"] if s == segs[-1] else None)

                for m in range(KD):
                    residual(full(dve, ("wo", L, m)), m, 2 * KD)
                    o.settle()
                    square(m, qs)
                if L == 0:
                    ffn_low(0)
                norm(full(dve, ("ss2", L)), nq, D)
                scaled(qs, nq)
                if L == 0:
                    ffn_low(1)
                    for k in range(KD):
                        dve.wait_ge(h_hi_made, k + 1)
                        o.sig(dve.tensor_tensor(h_lo[:, k, :], h[:, k, :], plain(h_hi[:, k, :]), ALU.subtract),
                              h_lo_made)
                    ffn_low(2)
                    ffn_low(3)
                    for name, slabs in FFN_TILES:
                        bank = full(dve, name)
                        if name[0] == "u":
                            k = name[1]
                            emptied(dve, ("g", k))
                            v = hid[:, k % 3, :]
                            o.sig(dve.tensor_tensor(v, v, bank[:, :], ALU.mult), free["dve"])
                        if name[0] == "dn":
                            residual(bank, name[2], 5 * KD)
                            if name[1] == 1:
                                o.settle()
                                square(name[2], slice(0, T))
                        for n in slabs:
                            if n + FFN_PARTS < N_FFN_SLABS:
                                ffn_low(n + FFN_PARTS)
                        if name[0] == "u":
                            dve.wait_ge(hid_hi_made, k + 1)
                            o.sig(dve.tensor_tensor(hid_lo[:, k % KH, :], v, plain(hid_hi[:, k % KH, :]),
                                                    ALU.subtract), hid_lo_made)

            bank = full(dve, ("rt",))
            o.sig(dve.tensor_copy(lg, bank[:, 0:2 * NE].rearrange("p (a b) -> p a b", a=2)), free["dve"])
            o.settle()
            for b in range(2):
                o.sig(dve.max(mx8[:, b, :], lg[:, b, :]))
            o.settle()
            for b in range(2):
                o.sig(dve.max_index(ix8[:, b, :], mx8[:, b, :], lg[:, b, :]))
            o.sig(dve.tensor_tensor(gt[:, 0, :, 0:1], mx8[:, :, 1:2], mx8[:, :, 0:1], ALU.subtract), top_in)
            o.settle()
            o.sig(dve.tensor_copy(ixf[:, :, :], ix8[:, :, :]))
            dve.wait_ge(top_exp, 1)
            o.sig(dve.tensor_scalar(gt[:, 1, :, 1:2], gt[:, 1, :, 0:1], 1.0, None, ALU.add))
            o.settle()
            o.sig(dve.reciprocal(gt[:, 1, :, 2:3], gt[:, 1, :, 1:2]))
            o.settle()
            o.sig(dve.tensor_tensor(gt[:, 1, :, 3:4], gt[:, 1, :, 0:1], gt[:, 1, :, 2:3], ALU.mult))
            o.settle()
            for b in range(2):
                for i in range(2):
                    o.sig(dve.tensor_scalar(xsel[:, b, i, :], iota8[:, :], ixf[:, b, i:i + 1], None, ALU.is_equal))
            o.settle()
            for b in range(2):
                for i in range(2):
                    o.sig(dve.tensor_scalar(gt[:, 2 + i, b, :], xsel[:, b, i, :], gt[:, 1, b, 2 + i:3 + i], None,
                                            ALU.mult))
            o.settle()
            o.sig(dve.tensor_tensor(gates[:, :, :], gt[:, 2, :, :], gt[:, 3, :, :], ALU.add))
            o.sig(dve.tensor_tensor(one_hot[:, :, :], xsel[:, :, 0, :], xsel[:, :, 1, :], ALU.add), gates_ready)
            o.sig(dve.memset(yacc[:, :, :], 0.0))
            far = float(1 << 20)
            bank = full(dve, ("rank",))
            o.sig(dve.tensor_copy(rank, bank[:, 0:2 * NE].rearrange("p (a b) -> p a b", a=2)))
            o.sig(dve.tensor_copy(cnt, bank[:, 2 * NE:3 * NE]), free["dve"])
            o.sig(dve.tensor_scalar(lg, one_hot, -far, far, ALU.mult, ALU.add))
            o.settle()
            o.sig(dve.tensor_tensor(rank, rank, lg, ALU.add))
            o.settle()
            o.sig(dve.tensor_copy(at_pass[:, :, 0:NE], rank))
            o.sig(dve.tensor_copy(gate_pass[:, :, 0:NE], gates))
            o.settle()

            def select(i):
                at = at_pass[:, :, bass.ds(i, 1)].to_broadcast([P, 2, P])
                slots = iota[:, :].unsqueeze(1).to_broadcast([P, 2, P])
                dve.tensor_tensor(sel[:, :, :], slots, at, ALU.is_equal).then_inc(sel_own, 1)
                dve.wait_ge(sel_own, i + 1)
                g = gate_pass[:, :, bass.ds(i, 1)].to_broadcast([P, 2, P])
                dve.tensor_tensor(selg[:, :, :], sel[:, :, :], g, ALU.mult).then_inc(sel_ready, 1)

            select(0)
            o.sig(dve.tensor_scalar(over[:, 0, :], cnt, float(P), None, ALU.is_gt))
            o.settle()
            o.sig(dve.tensor_tensor_scan(over[:, 1, :], ones[:, 0:NE], over[:, 0, :], 0.0, ALU.mult, ALU.add))
            o.settle()
            for j in range(MAX_EXTRA):
                o.sig(dve.tensor_scalar(xsel[:, 0, j, :], over[:, 1, :], float(j + 1), None, ALU.is_equal))
            o.settle()
            for j in range(MAX_EXTRA):
                o.sig(dve.tensor_tensor(xsel[:, 0, j, :], xsel[:, 0, j, :], over[:, 0, :], ALU.mult))
            o.settle()
            o.sig(dve.memset(at_pass[:, :, N_PASSES:N_PASSES + 1], -1.0))
            o.sig(dve.memset(gate_pass[:, :, N_PASSES:N_PASSES + 1], 0.0))
            for j in range(MAX_EXTRA):
                for n, (table, out) in enumerate(((rank, at_pass), (gates, gate_pass))):
                    o.settle()
                    pick = xsel[:, 0, j:j + 1, :].to_broadcast([P, 2, NE])
                    o.sig(dve.tensor_tensor(xsel[:, 1, 0:2, :], table, pick, ALU.mult))
                    o.settle()
                    o.sig(dve.tensor_reduce(out[:, :, NE + j:NE + j + 1], xsel[:, 1, 0:2, :], AX.X, ALU.add))
                o.settle()
                o.sig(dve.tensor_scalar(at_pass[:, :, NE + j:NE + j + 1], at_pass[:, :, NE + j:NE + j + 1],
                                        -float(P), None, ALU.add))
                o.sig(dve.tensor_tensor(over[:, 2, :], xsel[:, 0, j, :], iota8[:, :], ALU.mult))
                o.settle()
                o.sig(dve.tensor_reduce(over[:, 3, 0:1], over[:, 2, :], AX.X, ALU.add))
                o.settle()
                o.sig(dve.tensor_copy(extra[0:1, 1 + j:2 + j], over[0:1, 3, 0:1]))
            o.settle()
            o.sig(dve.tensor_copy(extra[0:1, 0:1], over[0:1, 1, NE - 1:NE]), extra_ready)

            four = lambda v: v.rearrange("p (a b) -> p a b", a=4)
            for j in range(2):
                bank = full(dve, ("ga0", j))
                dve.wait_ge(part_hi, j + 1)
                dve.tensor_tensor(xe_lo[:, 4 * j:4 * j + 4, :], four(bank[:, :]), plain(xe_hi[:, 4 * j:4 * j + 4, :]),
                                  ALU.subtract).then_inc(free["dve"], 1)

            def dve_pass(i):
                def low(n):
                    raw = MOE_SLAB0 + n
                    dve.wait_ge(hi_made, i * N_PS + (n + 1))
                    dve.tensor_tensor(w_lo[:, n % PARTS, :], ring[:, raw % SLOTS, :], plain(w_hi[:, n % PARTS, :]),
                                      ALU.subtract).then_inc(lo_made, 1)

                for n in range(PARTS):
                    low(n)
                bank = pass_full(dve, ("selT",), i)
                dve.tensor_copy(selt[:, :], bank[:, 0:2 * P]).then_inc(free["dve"], 1)
                dve.wait_ge(sel_ready, i + 1)
                select(i + 1)
                for n, slab in enumerate(PASS_SLABS):
                    if n + PARTS < N_PS:
                        low(n + PARTS)
                    tile = closes(slab)
                    if tile is not None and tile[0] == "u":
                        r = tile[1]
                        w = range_width(r)
                        bank = pass_full(dve, ("u", r), i)
                        pass_emptied(dve, ("g", r), i)
                        if r >= 2:
                            pass_full(dve, ("hT", r - 2), i)
                        dve.tensor_tensor(hs[:, r % 2, 0:w], sg[:, r % 2, 0:w], bank[:, 0:w],
                                          ALU.mult).then_inc(free["dve"], 1)
                    turned = None
                    if tile is not None and tile[0] == "u" and tile[1]:
                        turned = tile[1] - 1
                    if slab == ("dn", 0):
                        turned = NR - 1
                    if turned is not None:
                        w = range_width(turned)
                        bank = pass_full(dve, ("hT", turned), i)
                        dve.wait_ge(part_hi, i * PARTS_HI + (2 + turned + 1))
                        cs = slice(4 * turned, 4 * turned + w // P)
                        dve.tensor_tensor(hT_lo[:, cs, :], bank[:, 0:w].rearrange("p (a b) -> p a b", b=P),
                                          plain(hT_hi[:, cs, :]), ALU.subtract).then_inc(free["dve"], 1)
                bank = pass_full(dve, ("dn", 1), i)
                dve.tensor_copy(ye[:, 512:1024], bank[:, :]).then_inc(free["dve"], 1)
                for j in range(2):
                    bank = pass_full(dve, ("ga", j), i)
                    dve.wait_ge(part_hi, i * PARTS_HI + (2 + NR + j + 1))
                    dve.tensor_tensor(xe_lo[:, 4 * j:4 * j + 4, :], four(bank[:, :]),
                                      plain(xe_hi[:, 4 * j:4 * j + 4, :]), ALU.subtract).then_inc(free["dve"], 1)
                for j in range(4):
                    bank = pass_full(dve, ("y", j), i)
                    v = yacc[:, 2 * j:2 * j + 2, :]
                    dve.tensor_tensor(v, v, bank[:, :].rearrange("p (a b) -> p a b", a=2),
                                      ALU.add).then_inc(free["dve"], 1)

            passes(dve, dve_pass)
            dve.wait_ge(free["dve"], n_passes(dve) * EX["dve"] + BEFORE["dve"])
            for m in range(KD):
                o.sig(dve.scalar_tensor_tensor(x[:, m, seg(LAT)], yacc[:, m, :], mods[:, DEPTH - 1, LAT, 5 * KD + m:5 * KD + m + 1],
                                               x[:, m, seg(LAT)], ALU.mult, ALU.add))
            o.settle()
            squares(seg(LAT))
            dve.wait_ge(final_full, 1)
            norm(banks[0], SEG, D, tile_sem=False)
            for m in range(KD):
                o.sig(dve.scalar_tensor_tensor(h[:, m, seg(LAT)], x[:, m, seg(LAT)], fing[:, m:m + 1],
                                               rstd[:, 0:SEG], ALU.mult, ALU.mult), out_ready)


def constants():
    c = {"ident": np.eye(P), "ones": np.ones((P, P)),
         "ones_blk": np.kron(np.eye(2), np.ones((64, 64)))}
    t = np.arange(P)
    mask = np.zeros((P, 2, NL, P), np.int32)
    for l, half in enumerate(LEVELS):
        same = t[:, None] // (2 * half) == t[None, :] // (2 * half)
        late = (t // half) % 2 == 1
        mask[:, FWD, l] = same & ~late[:, None] & late[None, :]
        mask[:, BWD, l] = same & late[:, None] & ~late[None, :]
    c["mask"] = mask
    ang = 2 * np.pi * np.outer(np.arange(FOUR_CH), np.arange(FOUR_CH)) / FOUR_CH
    scale = (SEG * FOUR_CH) ** -0.5
    c["dftc"] = np.concatenate([np.kron(np.eye(2), np.cos(ang)), np.kron(np.eye(2), np.sin(ang))], 1)
    ang = 2 * np.pi * (np.outer(np.arange(SEG), np.arange(SEG)) % SEG) / SEG
    tab = np.stack([np.cos(ang), -np.sin(ang)]) * scale
    c["dftt"] = tab.reshape(2, 2, P, SEG).transpose(2, 0, 1, 3)
    rows = SEG // GRID_W
    row_ids = np.repeat(np.arange(rows), GRID_W).astype(np.float64)
    col_ids = np.tile(np.arange(GRID_W), rows).astype(np.float64)
    per_axis = ROPE // 2
    inv = 10000.0 ** (-np.arange(0, per_axis, 2) / per_axis)
    ang = np.stack([row_ids[:, None] * inv, col_ids[:, None] * inv], 1)
    cos, sin = np.cos(ang), np.sin(ang)
    rope = np.zeros((P, T))
    rope[64:96, :SEG] = 1.0
    rope[64:96, SEG:] = np.stack([cos, cos], 2).reshape(SEG, ROPE).T
    rope[96:128, SEG:] = np.stack([-sin, sin], 2).reshape(SEG, ROPE).T
    c["rope"] = rope
    c["reset"] = np.tile((np.arange(T) % P != 0).astype(float), (P, 1))
    c["iota"] = np.tile(np.arange(P, dtype=float), (P, 1))
    c["before"] = np.triu(np.ones((P, P)), 1)
    c["iota8"] = np.tile(np.arange(NE, dtype=float), (P, 1))
    return {k: np.ascontiguousarray(v if v.dtype == np.int32 else v.astype(np.float32)) for k, v in c.items()}


SWAP = np.array([16 * a + 8 * (1 - s) + i for a in range(2) for s in range(2) for i in range(8)])


def lay_out(x, c, ctx, c_ctx, w_ada, b_ada, w_in, q_norm_g, kv_norm_g, w_uq, w_ukv, hgrn_norm_g,
            lb_logits, w_out, ffn_w_gate, ffn_w_up, ffn_w_down, moe_router, moe_w_gate, moe_w_up,
            moe_w_down, final_g):
    def feat(v):
        v = v.reshape(v.shape[:-1] + (-1, P))
        return np.moveaxis(v, -1, 0)

    def slabs(w, width=P):
        n_l, k, n = w.shape
        return w.reshape(n_l, k // P, P, n // width, width).transpose(0, 3, 2, 1, 4).reshape(
            n_l, n // width, P, k // P * width)

    m = constants()
    m["x"] = np.stack([ctx[0].T.reshape(KD, P, SEG).transpose(1, 0, 2),
                       x[0].T.reshape(KD, P, SEG).transpose(1, 0, 2)])
    m["cond"] = np.stack([c_ctx.reshape(KD, P).T, c[0].reshape(KD, P).T], -1)
    m["bada"] = feat(b_ada)
    m["gains"] = np.concatenate([feat(q_norm_g), feat(kv_norm_g),
                                 np.concatenate([hgrn_norm_g, hgrn_norm_g], -1).T[:, :, None]], -1)
    m["fing"] = feat(final_g)
    m["lbl"] = feat(lb_logits).transpose(0, 2, 1, 3).reshape(P, DEPTH, 8)
    m["ada"] = w_ada
    sizes = [Q_RANK, KV_RANK, ROPE, SEG, 512, 512, 512, SEG, SEG]
    at = np.cumsum([0] + sizes)
    dq, dkv, kr, fo, hq, hff, hfb, hi, hg = [w_in[:, :, at[i]:at[i + 1]] for i in range(9)]
    win = np.zeros((DEPTH, len(WIN), P, SLAB), np.float32)
    win[:, 0:4], win[:, 4:8] = slabs(hff), slabs(hfb)
    win[:, 8:10] = slabs(hi, 2 * P)[:, 0].reshape(DEPTH, P, 2, SLAB).transpose(0, 2, 1, 3)
    win[:, 10:14], win[:, 14:16] = slabs(hq), slabs(hg)
    win[:, 16:18], win[:, 18:19] = slabs(dq), slabs(dkv)
    win[:, 19:20, :, 0:512] = slabs(np.concatenate([kr, kr[:, :, SWAP]], -1), 64)
    win[:, 20:22] = slabs(fo)
    uq = w_uq.reshape(DEPTH, 2, P, HEADS, QK)
    uq = np.concatenate([uq, uq[..., NOPE:][..., SWAP]], -1)
    win[:, 22:24] = uq.reshape(DEPTH, 2, P, HEADS * P)
    ukv = w_ukv.reshape(DEPTH, P, HEADS, NOPE + DV)
    win[:, 24] = np.concatenate([ukv[..., :NOPE].reshape(DEPTH, P, -1), ukv[..., NOPE:].reshape(DEPTH, P, -1)], -1)
    m["win"] = win
    m["wo"] = slabs(w_out)

    def ffn(g, u, d):
        n = g.shape[0]
        out = np.zeros((n, N_FFN_SLABS, P, SLAB), np.float32)
        gate, up, dn = slabs(g), slabs(u), slabs(d)
        for half in range(2):
            at = half * HALF_SLABS
            ks = slice(half * KH, (half + 1) * KH)
            out[:, at:at + 2 * KH:2], out[:, at + 1:at + 2 * KH:2] = gate[:, ks], up[:, ks]
            part = dn[:, :, :, half * KH * P:(half + 1) * KH * P]
            down = out[:, at + 2 * KH:at + HALF_SLABS]
            down[:, 0::2] = part[..., :SLAB]
            down[:, 1::2, :, :KH * P - SLAB] = part[..., SLAB:]
        return out

    m["ffn"] = ffn(ffn_w_gate, ffn_w_up, ffn_w_down)[0]
    moe = np.zeros((NE, N_PS, P, SLAB), np.float32)
    j = 0
    for r in range(NR):
        w = range_width(r)
        n = KD * w // SLAB
        for mat in (moe_w_gate[0], moe_w_up[0]):
            part = mat[:, :, 512 * r:512 * r + w].reshape(NE, n, SLAB // w, P, w)
            moe[:, j:j + n] = part.transpose(0, 1, 3, 2, 4).reshape(NE, n, P, SLAB)
            j += n
    moe[:, j:] = moe_w_down[0].reshape(NE, KF, P, D)
    m["moe"] = moe
    m["router"] = moe_router[0].reshape(KD, P, NE).transpose(1, 0, 2)
    return {k: np.ascontiguousarray(v) for k, v in m.items()}


def kernel(**inputs):
    import concourse.bacc as bacc
    from concourse.bass_utils import run_bass_kernel_spmd

    arrays = lay_out(**{k: np.asarray(v) for k, v in inputs.items()})
    nc = bacc.Bacc("TRN2", target_bir_lowering=False, num_devices=1)
    ops = {k: nc.dram_tensor(f"in_{k}", v.shape, mybir.dt.from_np(v.dtype), kind="ExternalInput").ap()
           for k, v in arrays.items()}
    ops["out"] = nc.dram_tensor("out_x", (P, KD, SEG), F32, kind="ExternalOutput").ap()
    build(nc, ops)
    r = run_bass_kernel_spmd(nc, [{f"in_{k}": v for k, v in arrays.items()}], core_ids=[0])
    got = np.asarray(r.results[0]["out_x"])
    return np.ascontiguousarray(got.transpose(2, 1, 0).reshape(1, SEG, D))
```
